# Optimizing a Trainium2 kernel written in Bass

```python
import math
import jax, jax.numpy as jnp
from jax import lax
import numpy as np

D_MODEL = 1024
BATCH = 1
SEQ = 256
DEPTH = 2
DEC_BATCH = 8
DEC_SEQ = 4
PAST_LEN = 1024
PAGE_SIZE = 128

N_A_LAYERS = DEPTH // 2
N_B_LAYERS = DEPTH - N_A_LAYERS
N_DENSE = (DEPTH + 1) // 2
N_MOE = DEPTH // 2

A_HEADS = 8
A_DQK = D_MODEL // (2 * A_HEADS)
A_DV = D_MODEL // A_HEADS
A_CHUNK = 64
GATE_CAP = 15.0
A_PROJ = A_HEADS * (2 * A_DQK + 2 * A_DV + 2)

B_HEADS = 8
Q_LORA = 384
KV_LORA = 256
NOPE_DIM = 128
ROPE_DIM = 64
B_DV = 128
ROPE_THETA = 10000.0
Q_BLOCK = 128
SOFTMAX_SCALE = (NOPE_DIM + ROPE_DIM) ** -0.5

D_FF = 2752
N_EXPERTS = 8
TOP_K = 2
D_FF_EXPERT = 3584
EPS = 1e-6

kernel_name = "yoco_mlstm_mla_moe_step"

def rms_norm(x, g):
    xf = x.astype(jnp.float32)
    y = xf * lax.rsqrt(jnp.mean(xf * xf, axis=-1, keepdims=True) + EPS)
    return (y * g.astype(jnp.float32)).astype(x.dtype)

def rope(x, pos):
    half = ROPE_DIM // 2
    inv = ROPE_THETA ** (-jnp.arange(half, dtype=jnp.float32) / half)
    ang = pos.astype(jnp.float32)[:, None] * inv[None, :]
    shape = (ang.shape[0],) + (1,) * (x.ndim - 3) + (half,)
    cos, sin = jnp.cos(ang).reshape(shape), jnp.sin(ang).reshape(shape)
    x1 = x[..., :half].astype(jnp.float32)
    x2 = x[..., half:].astype(jnp.float32)
    return jnp.concatenate([x1 * cos - x2 * sin, x2 * cos + x1 * sin], axis=-1).astype(x.dtype)

def _mlstm_chunk(carry, inp):
    C, n, m = carry
    q, k, v, li, lf = inp
    L = q.shape[1]
    a = jnp.swapaxes(jnp.cumsum(lf, axis=1), 1, 2)
    li = jnp.swapaxes(li, 1, 2)
    causal = jnp.tril(jnp.ones((L, L), dtype=bool))
    d = jnp.where(causal, a[..., :, None] - a[..., None, :] + li[..., None, :], -jnp.inf)
    inter = a + m[..., None]
    m_t = jnp.maximum(inter, jnp.max(d, axis=-1))
    w = jnp.exp(d - m_t[..., None]) * jnp.einsum('bthk,bshk->bhts', q, k)
    e_inter = jnp.exp(inter - m_t)
    num = jnp.einsum('bhts,bshv->bthv', w, v) + jnp.einsum('bht,bthk,bhkv->bthv', e_inter, q, C)
    den = jnp.sum(w, axis=-1) + e_inter * jnp.einsum('bthk,bhk->bht', q, n)
    h = num / jnp.swapaxes(jnp.maximum(jnp.abs(den), jnp.exp(-m_t)), 1, 2)[..., None]
    m_new = m_t[..., -1]
    e_end = jnp.exp(a[..., -1:] - a + li - m_new[..., None])
    e_carry = jnp.exp(inter[..., -1] - m_new)
    C_new = e_carry[..., None, None] * C + jnp.einsum('bhs,bshk,bshv->bhkv', e_end, k, v)
    n_new = e_carry[..., None] * n + jnp.einsum('bhs,bshk->bhk', e_end, k)
    return (C_new, n_new, m_new), h

def mlstm_recurrence(q, k, v, logi, logf, C0, n0, m0):
    B, T = q.shape[:2]
    L = math.gcd(T, A_CHUNK)
    nc = T // L

    def chunks(x):
        return jnp.moveaxis(x.astype(jnp.float32).reshape((B, nc, L) + x.shape[2:]), 1, 0)

    q = q.astype(jnp.float32) * (A_DQK ** -0.5)
    carry0 = (C0.astype(jnp.float32), n0.astype(jnp.float32), m0.astype(jnp.float32))
    (C, n, m), h = lax.scan(_mlstm_chunk, carry0, (chunks(q), chunks(k), chunks(v), chunks(logi), chunks(logf)))
    h = jnp.moveaxis(h, 0, 1).reshape(B, T, A_HEADS, A_DV)
    return h, C, n, m

def mlstm_layer(x, C0, n0, m0, g_norm, w_in, b_gate, g_head, w_out):
    B, T, _ = x.shape
    xn = rms_norm(x, g_norm)
    proj = xn @ w_in
    hq, hv = A_HEADS * A_DQK, A_HEADS * A_DV
    q, k, v, o, gates = jnp.split(proj, [hq, 2 * hq, 2 * hq + hv, 2 * hq + 2 * hv], axis=-1)
    q = q.reshape(B, T, A_HEADS, A_DQK)
    k = k.reshape(B, T, A_HEADS, A_DQK)
    v = v.reshape(B, T, A_HEADS, A_DV)
    gates = gates.astype(jnp.float32) + b_gate.astype(jnp.float32)
    gates = GATE_CAP * jnp.tanh(gates / GATE_CAP)
    logi = gates[..., :A_HEADS]
    logf = jax.nn.log_sigmoid(gates[..., A_HEADS:])
    h, C, n, m = mlstm_recurrence(q, k, v, logi, logf, C0, n0, m0)
    h = rms_norm(h.astype(x.dtype), g_head).reshape(B, T, hv)
    y = (jax.nn.sigmoid(o) * h) @ w_out
    return y, C, n, m

def shared_latent_kv(h, pos, g_kv, w_dkv, g_ckv):
    hn = rms_norm(h, g_kv)
    ckv, kr = jnp.split(hn @ w_dkv, [KV_LORA], axis=-1)
    return rms_norm(ckv, g_ckv), rope(kr, pos)

def mla_attend(q_lat, q_rope, ckv, krope, q_pos, k_pos):
    B, T = q_lat.shape[:2]
    qb = math.gcd(T, Q_BLOCK)
    nb = T // qb

    def blocks(a):
        return jnp.moveaxis(a.reshape((B, nb, qb) + a.shape[2:]), 1, 0)

    def one_block(args):
        ql, qr, qp = args
        s = (jnp.einsum('bthc,bsc->bhts', ql, ckv) + jnp.einsum('bthr,bsr->bhts', qr, krope)).astype(jnp.float32) * SOFTMAX_SCALE
        s = jnp.where(k_pos[None, :] <= qp[:, None], s, -jnp.inf)
        p = jax.nn.softmax(s, axis=-1).astype(ckv.dtype)
        return jnp.einsum('bhts,bsc->bthc', p, ckv)

    out = lax.map(one_block, (blocks(q_lat), blocks(q_rope), q_pos.reshape(nb, qb)))
    return jnp.moveaxis(out, 0, 1).reshape(B, T, B_HEADS, KV_LORA)

def mla_layer(x, pos, keys_ckv, keys_krope, k_pos, g_norm, w_dq, g_q, w_uq, w_uk, w_uv, w_o):
    B, T, _ = x.shape
    xn = rms_norm(x, g_norm)
    cq = rms_norm(xn @ w_dq, g_q)
    q = (cq @ w_uq).reshape(B, T, B_HEADS, NOPE_DIM + ROPE_DIM)
    q_nope, q_rope = q[..., :NOPE_DIM], rope(q[..., NOPE_DIM:], pos)
    q_lat = jnp.einsum('bthn,chn->bthc', q_nope, w_uk)
    o_lat = mla_attend(q_lat, q_rope, keys_ckv, keys_krope, pos, k_pos)
    o = jnp.einsum('bthc,chv->bthv', o_lat, w_uv).reshape(B, T, B_HEADS * B_DV)
    return o @ w_o

def dense_swiglu(x, g_norm, w_gate, w_up, w_down):
    xn = rms_norm(x, g_norm)
    return (jax.nn.silu(xn @ w_gate) * (xn @ w_up)) @ w_down

def moe_swiglu(x, g_norm, w_router, w_gate, w_up, w_down):
    xn = rms_norm(x, g_norm)
    logits = (xn @ w_router).astype(jnp.float32)
    top_v, top_i = lax.top_k(logits, TOP_K)
    top_w = jax.nn.softmax(top_v, axis=-1)
    gate = jnp.sum(jax.nn.one_hot(top_i, N_EXPERTS, dtype=jnp.float32) * top_w[..., None], axis=-2).astype(x.dtype)
    y = jnp.zeros_like(x)
    for e in range(N_EXPERTS):
        he = jax.nn.silu(xn @ w_gate[e]) * (xn @ w_up[e])
        y = y + gate[..., e:e + 1] * (he @ w_down[e])
    return y

def run_trunk(x, pos, C_in, n_in, m_in, past_ckv, past_krope, p):
    new_C, new_n, new_m = [], [], []
    ckv_new = krope_new = keys_ckv = keys_krope = k_pos = None
    i_dense = i_moe = 0
    for layer in range(DEPTH):
        if layer < N_A_LAYERS:
            a = layer
            y, C, n, m = mlstm_layer(x, C_in[a], n_in[a], m_in[a], p['g_norm_a'][a], p['w_in_a'][a],
                                     p['b_gate_a'][a], p['g_head_a'][a], p['w_out_a'][a])
            new_C.append(C); new_n.append(n); new_m.append(m)
        else:
            if layer == N_A_LAYERS:
                ckv_new, krope_new = shared_latent_kv(x, pos, p['g_kv'], p['w_dkv'], p['g_ckv'])
                if past_ckv is None:
                    keys_ckv, keys_krope, k_pos = ckv_new, krope_new, pos
                else:
                    keys_ckv = jnp.concatenate([past_ckv, ckv_new], axis=1)
                    keys_krope = jnp.concatenate([past_krope, krope_new], axis=1)
                    k_pos = jnp.concatenate([jnp.arange(past_ckv.shape[1], dtype=jnp.int32), pos])
            b = layer - N_A_LAYERS
            y = mla_layer(x, pos, keys_ckv, keys_krope, k_pos, p['g_norm_b'][b], p['w_dq'][b], p['g_q'][b],
                          p['w_uq'][b], p['w_uk'], p['w_uv'], p['w_o_b'][b])
        x = x + y
        if layer % 2 == 0:
            x = x + dense_swiglu(x, p['g_ffn_d'][i_dense], p['w_gate_d'][i_dense], p['w_up_d'][i_dense], p['w_down_d'][i_dense])
            i_dense += 1
        else:
            x = x + moe_swiglu(x, p['g_ffn_m'][i_moe], p['w_router'][i_moe], p['w_gate_m'][i_moe],
                               p['w_up_m'][i_moe], p['w_down_m'][i_moe])
            i_moe += 1
    return rms_norm(x, p['g_final']), jnp.stack(new_C), jnp.stack(new_n), jnp.stack(new_m), ckv_new, krope_new

def setup_inputs(seed: int = 0) -> dict:
    key = jax.random.key(seed)
    ks = iter(jax.random.split(key, 48))

    def nrm(shape, scale):
        return scale * jax.random.normal(next(ks), shape, jnp.float32)

    def gain(shape):
        return 1.0 + nrm(shape, 0.02)

    n_pages = PAST_LEN // PAGE_SIZE
    n_used = DEC_BATCH * n_pages
    n_phys = n_used + n_used // 4
    perm = jax.random.permutation(next(ks), n_phys)
    page_table = perm[:n_used].reshape(DEC_BATCH, n_pages).astype(jnp.int32)
    forget_bias = jnp.broadcast_to(jnp.linspace(3.0, 6.0, A_HEADS, dtype=jnp.float32), (N_A_LAYERS, A_HEADS))
    b_gate_a = jnp.concatenate([nrm((N_A_LAYERS, A_HEADS), 0.1), forget_bias + nrm((N_A_LAYERS, A_HEADS), 0.1)], axis=-1)
    return {
        "x_prompt": nrm((BATCH, SEQ, D_MODEL), 1.0),
        "x_sample": nrm((DEC_BATCH, DEC_SEQ, D_MODEL), 1.0),
        "state_C": nrm((N_A_LAYERS, DEC_BATCH, A_HEADS, A_DQK, A_DV), 0.5),
        "state_n": nrm((N_A_LAYERS, DEC_BATCH, A_HEADS, A_DQK), 0.5),
        "state_m": nrm((N_A_LAYERS, DEC_BATCH, A_HEADS), 1.0),
        "cache_ckv": nrm((n_phys, PAGE_SIZE, KV_LORA), 1.0),
        "cache_krope": nrm((n_phys, PAGE_SIZE, ROPE_DIM), 1.0),
        "page_table": page_table,
        "g_norm_a": gain((N_A_LAYERS, D_MODEL)),
        "w_in_a": nrm((N_A_LAYERS, D_MODEL, A_PROJ), D_MODEL ** -0.5),
        "b_gate_a": b_gate_a,
        "g_head_a": gain((N_A_LAYERS, A_HEADS, A_DV)),
        "w_out_a": nrm((N_A_LAYERS, A_HEADS * A_DV, D_MODEL), (A_HEADS * A_DV) ** -0.5),
        "g_kv": gain((D_MODEL,)),
        "w_dkv": nrm((D_MODEL, KV_LORA + ROPE_DIM), D_MODEL ** -0.5),
        "g_ckv": gain((KV_LORA,)),
        "w_uk": nrm((KV_LORA, B_HEADS, NOPE_DIM), KV_LORA ** -0.5),
        "w_uv": nrm((KV_LORA, B_HEADS, B_DV), KV_LORA ** -0.5),
        "g_norm_b": gain((N_B_LAYERS, D_MODEL)),
        "w_dq": nrm((N_B_LAYERS, D_MODEL, Q_LORA), D_MODEL ** -0.5),
        "g_q": gain((N_B_LAYERS, Q_LORA)),
        "w_uq": nrm((N_B_LAYERS, Q_LORA, B_HEADS * (NOPE_DIM + ROPE_DIM)), Q_LORA ** -0.5),
        "w_o_b": nrm((N_B_LAYERS, B_HEADS * B_DV, D_MODEL), (B_HEADS * B_DV) ** -0.5),
        "g_ffn_d": gain((N_DENSE, D_MODEL)),
        "w_gate_d": nrm((N_DENSE, D_MODEL, D_FF), D_MODEL ** -0.5),
        "w_up_d": nrm((N_DENSE, D_MODEL, D_FF), D_MODEL ** -0.5),
        "w_down_d": nrm((N_DENSE, D_FF, D_MODEL), D_FF ** -0.5),
        "g_ffn_m": gain((N_MOE, D_MODEL)),
        "w_router": nrm((N_MOE, D_MODEL, N_EXPERTS), D_MODEL ** -0.5),
        "w_gate_m": nrm((N_MOE, N_EXPERTS, D_MODEL, D_FF_EXPERT), D_MODEL ** -0.5),
        "w_up_m": nrm((N_MOE, N_EXPERTS, D_MODEL, D_FF_EXPERT), D_MODEL ** -0.5),
        "w_down_m": nrm((N_MOE, N_EXPERTS, D_FF_EXPERT, D_MODEL), D_FF_EXPERT ** -0.5),
        "g_final": gain((D_MODEL,)),
    }

def reference(x_prompt, x_sample, state_C, state_n, state_m, cache_ckv, cache_krope, page_table,
              g_norm_a, w_in_a, b_gate_a, g_head_a, w_out_a,
              g_kv, w_dkv, g_ckv, w_uk, w_uv,
              g_norm_b, w_dq, g_q, w_uq, w_o_b,
              g_ffn_d, w_gate_d, w_up_d, w_down_d,
              g_ffn_m, w_router, w_gate_m, w_up_m, w_down_m,
              g_final):
    p = dict(g_norm_a=g_norm_a, w_in_a=w_in_a, b_gate_a=b_gate_a, g_head_a=g_head_a, w_out_a=w_out_a,
             g_kv=g_kv, w_dkv=w_dkv, g_ckv=g_ckv, w_uk=w_uk, w_uv=w_uv,
             g_norm_b=g_norm_b, w_dq=w_dq, g_q=g_q, w_uq=w_uq, w_o_b=w_o_b,
             g_ffn_d=g_ffn_d, w_gate_d=w_gate_d, w_up_d=w_up_d, w_down_d=w_down_d,
             g_ffn_m=g_ffn_m, w_router=w_router, w_gate_m=w_gate_m, w_up_m=w_up_m, w_down_m=w_down_m,
             g_final=g_final)

    bp, tp = x_prompt.shape[:2]
    pos_p = jnp.arange(tp, dtype=jnp.int32)
    C0 = jnp.zeros((N_A_LAYERS, bp, A_HEADS, A_DQK, A_DV), jnp.float32)
    n0 = jnp.zeros((N_A_LAYERS, bp, A_HEADS, A_DQK), jnp.float32)
    m0 = jnp.zeros((N_A_LAYERS, bp, A_HEADS), jnp.float32)
    y_prompt, C_prompt, n_prompt, m_prompt, ckv_prompt, krope_prompt = run_trunk(
        x_prompt, pos_p, C0, n0, m0, None, None, p)

    bs, ts = x_sample.shape[:2]
    n_pages = page_table.shape[1]
    past_ckv = cache_ckv[page_table].reshape(bs, n_pages * PAGE_SIZE, KV_LORA)
    past_krope = cache_krope[page_table].reshape(bs, n_pages * PAGE_SIZE, ROPE_DIM)
    pos_s = n_pages * PAGE_SIZE + jnp.arange(ts, dtype=jnp.int32)
    y_sample, C_sample, n_sample, m_sample, ckv_sample, krope_sample = run_trunk(
        x_sample, pos_s, state_C, state_n, state_m, past_ckv, past_krope, p)

    return (y_prompt, y_sample, C_prompt, n_prompt, m_prompt, ckv_prompt, krope_prompt,
            C_sample, n_sample, m_sample, ckv_sample, krope_sample)


_drawn_inputs = setup_inputs


def setup_inputs(seed=0):
    import zlib

    import numpy as np

    out = dict(_drawn_inputs(seed))
    spreads = {}
    factors = {'g_head_a': 2.761,
     'g_kv': 2.849,
     'g_ckv': 2.745,
     'g_norm_b': 4.16,
     'g_q': 3.408,
     'g_final': 8.06,
     'g_ffn_m': 2.766}
    for name, (base, spread) in spreads.items():
        noise = np.random.default_rng([zlib.crc32(name.encode()), seed]).standard_normal(out[name].shape)
        drawn = base * np.exp(spread * noise) if base else spread * noise
        out[name] = __import__('jax').numpy.asarray(drawn.astype(out[name].dtype))
    for name, factor in factors.items():
        out[name] = (out[name] * factor).astype(out[name].dtype)
    return out
```

```python
from contextlib import ExitStack

import concourse.bass as bass
from concourse import mybir

F32 = mybir.dt.float32
I32 = mybir.dt.int32
U32 = mybir.dt.uint32

P = 128
D = 1024
DC = D // P
TP = 256
NB, NS = 8, 4
TS = NB * NS
T = TP + TS
TOK = [(0, P, 0), (P, P, 1), (TP, TS, 2)]
H = 8
HP = H // 2
DK, DV = 64, 128
CAP = 15.0
NOPE, ROPE = 128, 64
CKV = 256
CT = CKV // P
QL = 384
QT = QL // P
SCALE = (NOPE + ROPE) ** -0.5
PAGE = 128
NPG = 8
PAST = NPG * PAGE
FF = 2752
FT = (FF + P - 1) // P
FLAST = FF - (FT - 1) * P
E = 8
FE = 3584
CW = 512
CE = FE // CW
KD = CW // P
SLOTS = 7
SLOTW = DC * CW
EPS = 1e-6
NEG = -1e30
EXTRA = 4
ITEMS = E + EXTRA

GAINS = [("g_norm_a", DC), ("g_head_a", H), ("g_ffn_d", DC), ("g_kv", DC), ("g_norm_b", DC), ("g_ffn_m", DC),
         ("g_ckv", CT), ("g_q", QT)]
G0, GROWS = {}, 0
for _name, _rows in GAINS:
    G0[_name] = GROWS
    GROWS += _rows

CONSTS = [("ident", P), ("ones", P), ("pmask", P), ("smask", (2 * NB - 1) * NS), ("cos", T), ("sin", T),
          ("rot", ROPE), ("bsel", NB), ("eps", 1), ("one", 1)]
MCONSTS = [("tri", P), ("iota", P), ("eidx", 2 * E), ("kbase", 2 * E), ("valid", 3)]
C0, CCOLS = {}, 0
for _name, _cols in CONSTS:
    C0[_name] = (CCOLS, _cols)
    CCOLS += _cols
M0, MCOLS = {}, 0
for _name, _cols in MCONSTS:
    M0[_name] = (MCOLS, _cols)
    MCOLS += _cols
WM = TP + P + TS
ACOLS = WM + HP * P


def build(nc, i, out):
    ALU = mybir.AluOpType
    ACT = mybir.ActivationFunctionType
    AX = mybir.AxisListType

    with ExitStack() as ctx:
        ctx.enter_context(nc.allow_non_contiguous_dma(reason="state vectors and gate biases: a few KiB in all"))

        def sb(name, shape, dt=F32):
            return ctx.enter_context(nc.sbuf_tensor(name, shape, dt))

        def sem(name):
            return ctx.enter_context(nc.semaphore(name))

        ring = sb("ring", [P, SLOTS, SLOTW])
        xT = sb("xT", [P, DC, T])
        xn = sb("xn", [P, DC, T])
        cs = sb("cs", [P, CCOLS])
        gT = sb("gT", [P, GROWS])
        wg = sb("wg", [P, DC, 2 * H])
        cols = sb("cols", [P, 16])
        tiny = sb("tiny", [H, 32])
        ints = sb("ints", [1, 8], I32)
        pages = sb("pages", [1, NB * NPG], I32)
        arena = sb("arena", [P, 18368])
        bank = [ctx.enter_context(nc.psum_tensor(f"bank{n}", [P, 512], F32)) for n in range(5)]
        wide = ctx.enter_context(nc.psum_tensor("wide", [P, 3 * 512], F32))
        bank += [wide[:, 512 * n:512 * (n + 1)] for n in range(3)]

        def c(name, rows=P):
            a, n = C0[name]
            return cs[0:rows, a:a + n]

        def mc(name):
            a, n = M0[name]
            return arena[:, 15000 + a:15000 + a + n]

        def gain(name, k):
            return gT[:, G0[name] + k:G0[name] + k + 1]

        def area(at, *dims, rows=P):
            n = 1
            for d in dims:
                n *= d
            v = arena[0:rows, at:at + n]
            if len(dims) == 2:
                return v.rearrange("p (a b) -> p a b", a=dims[0])
            if len(dims) == 3:
                return v.rearrange("p (a b d) -> p a b d", a=dims[0], b=dims[1])
            return v

        ident, ones = c("ident"), c("ones")
        xtok = area(0, 3, D)
        VX = area(0, 3, H, DV + 1)
        qT, kT = area(3096, HP, T), area(4248, HP, T)
        Cp = area(3096, H, DV + 1, rows=DK)
        kmb = [area(4248, H * DK, rows=TS), area(4760, H * DK, rows=TS)]
        oT = area(5400, DC, T)
        Ke = area(7704, 3, H * DK)
        Ce = area(9240, HP, NB, DV + 1)
        ac = area(13368, ACOLS)
        cmask = ac[:, 0:WM]
        selp = ac[0:H, WM:].rearrange("p (j m) -> p j m", j=HP)
        rU, rE, rA, rM, rZ = (area(14296 + T * k, T, rows=H) for k in range(5))
        Dh = [area(15736, WM), area(16152, WM)]
        Wt = area(16568, WM)
        inN, inD = area(16984, H, TS), area(17240, H, TS)
        uT = area(17496, 3, 2 * H)
        eI, eC = area(17544, HP, TS), area(17672, HP * NB)
        qe = area(17704, HP, TS)
        den = area(17832, T)
        hT = area(0, FT, T)
        sg = [area(6336, T), area(6624, T)]
        hn = area(0, DC, T)
        qlat = area(0, CT, H, TP)
        qls = area(CT * H * TP, CT, NB, H * NS)
        qrope = area(4608, H, TP, rows=ROPE)
        qrs = area(4608 + H * TP, NB, H * NS, rows=ROPE)
        ckvT, krT = area(6912, CT, T), area(7488, T, rows=ROPE)
        ctok = area(7776, 3, CKV + ROPE)
        raw = area(8736, 3, T)
        qn = [area(8736, T), area(9024, T)]
        rtmp = [area(9312, T, rows=ROPE), area(9600, T, rows=ROPE)]
        rt2 = area(9888, T, rows=ROPE)
        prob = area(8736, PAST + TS)
        prob2 = [area(8736, TP), area(8736 + TP, TP)]
        PT = area(9792, 384)
        cacheT = area(10176, CT, PAST)
        cacheR = area(12224, PAST, rows=ROPE)
        cq = area(10176, QT, T)
        ukT = area(11040, H, CKV)
        ctk = [area(13248 + 2560 * k, NPG, CKV) for k in range(2)]
        crk = [area(13248 + 2560 * k + NPG * CKV, NPG, ROPE) for k in range(2)]
        acc_sq = area(0, DC, T)

        def stdv(k):
            return den if k == 0 else area(9600 if 2 <= k <= 4 else 6912, T)

        acc = area(0, 3, D)
        xtk = area(3072, 3, D)
        xg = area(6144, DC, P)
        hh = [area(7168, CW), area(7680, CW)]
        hhT = [area(8192, CW), area(8704, CW)]
        ysb = area(9216, D)
        Pm, Pg = area(10240, 3, P), area(10624, 3, P)
        PTg = area(11008, T)
        gfin = area(11296, D)
        sl = [area(12320, CW), area(12832, CW)]
        rt = area(13344, 1600)
        lg, mk, gt, pos = (rt[:, 24 * k:24 * (k + 1)].rearrange("p (a b) -> p a b", a=3) for k in range(4))
        oh1, oh2, top = (rt[:, 96 + 24 * k:120 + 24 * k].rearrange("p (a b) -> p a b", a=3) for k in range(3))
        idf = rt[:, 168:192].rearrange("p (a b) -> p a b", a=3)
        gk = rt[:, 192:198].rearrange("p (a b) -> p a b", a=3)
        cnt = rt[:, 200:208]
        fl, cum, sel, s16 = (rt[:, 208 + 16 * k:224 + 16 * k] for k in range(4))
        posI = rt[:, 272:272 + 3 * 13].rearrange("p (a b) -> p a b", a=3)
        gateI = rt[:, 312:312 + 3 * 13].rearrange("p (a b) -> p a b", a=3)
        nf = rt[:, 352:360]
        p48 = rt[:, 360:408].rearrange("p (a b) -> p a b", a=3)
        idu = sb("idu", [P, 3, 8], U32)

        names = """ld_const ld_x ld_gain ld_tiny ld_wg ld_state ld_ac ld_pages ld_wr ld_gf
            gt_full gt_ready bg_ready x_full x_ready sq_ready ss_full std_ready xn_ready
            ga_full ga_free gd_full gd_free gates_full lf_ready rows_ready uT_full uT_ready e_ready
            qe_ready inter_full inter_ready s_full D_made exp_done W_made nd_full em_done h_made kd_made
            st_full st_free hsq_ready hss_full hstd_ready y_ready stored
            ckv_raw ckv_ready kr_ready cq_raw cq_ready ss2_full std2_ready sq2_ready
            uk_ready qn_ready rr_ready qr_ready rot_full ql_ready
            sc_full max_ready p_exp p_ready pt_full pt_ready ol_full ol_ready tp_full tpa_free tpd_free
            lg_full mask_ready rank_full tables_ready p_made
            g_full u_full d_done silu_done gu_done misc_full m_full xg_ready gk_exp acc_done fin_ss kv_stored misc_free y_full y_free
            dchain achain fin_sq fin_ready outs""".split()
        S = {n: sem(n) for n in names}
        ck_full = [sem("ck_full0"), sem("ck_full1")]
        w_full = [sem(f"w_full{k}") for k in range(SLOTS)]

        w_in, w_out = i["w_in_a"][0], i["w_out_a"][0]
        chunks = []

        def rows_of(w, c0, n):
            return w[:, c0:c0 + n].rearrange("(c p) n -> p c n", p=P)

        def chunk(name, w, c0, n):
            k = w.shape[0] // P
            chunks.append((name, [(k, n, 0, P, rows_of(w, c0, n))]))

        hq, hv = H * DK, H * DV
        chunk("k0", w_in, hq, hq)
        chunk("q0", w_in, 0, hq)
        for n in range(2):
            chunk(f"o{n}", w_in, 2 * hq + hv + n * CW, CW)
        for n in range(2):
            chunk(f"v{n}", w_in, 2 * hq + n * CW, CW)
        for n in range(2):
            chunk(f"out{n}", w_out, n * CW, CW)
        FCH = [(n * CW, min(CW, FF - n * CW)) for n in range((FF + CW - 1) // CW)]
        for n, (a, w) in enumerate(FCH):
            chunk(f"gd{n}", i["w_gate_d"][0], a, w)
            chunk(f"ud{n}", i["w_up_d"][0], a, w)
        wd = i["w_down_d"][0]
        for m in range(DC):
            chunks.append((f"dd{m}", [
                (FT - 1, P, 0, P, wd[0:(FT - 1) * P, m * P:(m + 1) * P].rearrange("(c p) n -> p c n", p=P)),
                (1, P, (FT - 1) * P, FLAST, wd[(FT - 1) * P:FF, m * P:(m + 1) * P].rearrange("(c p) n -> p c n", c=1)),
            ]))
        chunk("dkv", i["w_dkv"], 0, CKV + ROPE)
        chunk("dq", i["w_dq"][0], 0, QL)
        chunk("uk", i["w_uk"].rearrange("c h n -> c (h n)"), 0, H * NOPE)
        for n in range(2):
            chunk(f"uq{n}", i["w_uq"][0], n * HP * (NOPE + ROPE), HP * (NOPE + ROPE))
        chunk("uv", i["w_uv"].rearrange("c h n -> c (h n)"), 0, hv)
        for n in range(2):
            chunk(f"wo{n}", i["w_o_b"][0], n * CW, CW)
        NPRE = len(chunks)
        CH = {name: n for n, (name, _) in enumerate(chunks)}
        arrive, slot_sum = [], [0] * SLOTS
        for n, (_, parts) in enumerate(chunks):
            slot_sum[n % SLOTS] += 16 * len(parts)
            arrive.append(slot_sum[n % SLOTS])
        release = {}

        def wview(name, k, n):
            s = CH[name] % SLOTS
            return ring[:, s, 0:k * n].rearrange("p (c n) -> p c n", c=k)

        def moe_slot(k):
            n = NPRE + k
            s = n % SLOTS
            before = sum(1 for m in range(k) if (NPRE + m) % SLOTS == s)
            return s, slot_sum[s] + 16 * (before + 1)

        SHARED = 1 + CE + 2 + 6
        PER_ITEM = 3 * CE
        SLOT_STEP = 16 * PER_ITEM // SLOTS

        block = ctx.enter_context(nc.Block())

        @block.tensor
        def _(pe):
            n_ga, n_gd = [0], [0]

            def arrived(name):
                pe.wait_ge(w_full[CH[name] % SLOTS], arrive[CH[name]])

            def out_a():
                if n_ga[0] >= 2:
                    pe.wait_ge(S["ga_free"], n_ga[0] - 1)
                n_ga[0] += 1
                return bank[(n_ga[0] - 1) % 2]

            def out_d():
                if n_gd[0] >= 2:
                    pe.wait_ge(S["gd_free"], n_gd[0] - 1)
                n_gd[0] += 1
                return bank[2 + (n_gd[0] - 1) % 2]

            def done_a(ins, last_of=None):
                ins.then_inc(S["ga_full"], 1)
                if last_of:
                    release[CH[last_of]] = (S["ga_full"], n_ga[0])

            def done_d(ins, last_of=None):
                ins.then_inc(S["gd_full"], 1)
                if last_of:
                    release[CH[last_of]] = (S["gd_full"], n_gd[0])

            def product(o, pairs):
                for n, (w, x) in enumerate(pairs):
                    ins = pe.matmul(o, w, x, start=(n == 0), stop=(n == len(pairs) - 1))
                return ins

            def sum_squares(k, chunks_, sq, first):
                if k:
                    pe.wait_ge(S["std_ready"], k)
                for m in range(chunks_):
                    pe.wait_ge(S["sq_ready"], first + m + 1)
                    ins = pe.matmul(bank[7][:, 0:T], ones, sq[:, m, :], start=(m == 0), stop=(m == chunks_ - 1))
                ins.then_inc(S["ss_full"], 1)

            pe.wait_ge(S["ld_const"], 16)
            pe.wait_ge(S["ld_gain"], 16 * len(GAINS))
            pe.transpose(bank[4][:, 0:GROWS], Dh[0][0:GROWS, 0:P], ident[0:GROWS, 0:GROWS]).then_inc(S["gt_full"], 1)
            pe.wait_ge(S["ld_x"], 48)
            for m in range(DC):
                if m >= 2:
                    pe.wait_ge(S["x_ready"], m - 1)
                for t0, tn, tt in TOK:
                    ins = pe.transpose(bank[m % 2][:, t0:t0 + tn], xtok[0:tn, tt, m * P:(m + 1) * P],
                                       ident[0:tn, 0:tn])
                ins.then_inc(S["x_full"], 1)
            sum_squares(0, DC, xn, 0)

            pe.wait_ge(S["x_ready"], DC)
            arrived("k0")
            w = wview("k0", DC, CW)
            for m in range(HP):
                o = out_d()
                for k in range(DC):
                    if m == 0:
                        pe.wait_ge(S["xn_ready"], k + 1)
                    ins = pe.matmul(o[:, 0:T], w[:, k, m * P:(m + 1) * P], xn[:, k, :], start=(k == 0), stop=(k == DC - 1))
                done_d(ins, "k0" if m == HP - 1 else None)
            pe.wait_ge(S["ld_wg"], 16)
            pe.wait_ge(S["gt_ready"], 1)
            product(bank[4][0:H, 0:T], [(wg[:, k, 0:H], xn[:, k, :]) for k in range(DC)])
            product(bank[5][0:H, 0:T], [(wg[:, k, H:2 * H], xn[:, k, :]) for k in range(DC)]).then_inc(S["gates_full"], 1)
            arrived("q0")
            w = wview("q0", DC, CW)
            for m in range(HP):
                o = out_a()
                ins = product(o[:, 0:T], [(w[:, k, m * P:(m + 1) * P], xn[:, k, :]) for k in range(DC)])
                done_a(ins, "q0" if m == HP - 1 else None)
            for m in range(DC):
                name = f"o{m // 4}"
                arrived(name)
                w = wview(name, DC, CW)
                o = out_a()
                ins = product(o[:, 0:T], [(w[:, k, (m % 4) * P:(m % 4 + 1) * P], xn[:, k, :]) for k in range(DC)])
                done_a(ins, name if m % 4 == 3 else None)
            for n in range(2):
                name = f"v{n}"
                arrived(name)
                w = wview(name, DC, CW)
                for t0, tn, tt in TOK:
                    o = out_d()
                    ins = product(o[0:tn, :], [(xn[:, k, t0:t0 + tn], w[:, k, :]) for k in range(DC)])
                    done_d(ins, name if tt == 2 else None)

            pe.wait_ge(S["rows_ready"], 1)
            pe.wait_ge(S["ld_ac"], 16)
            for t0, tn, tt in TOK:
                pe.transpose(bank[4][0:tn, tt * 16:tt * 16 + H], rU[:, t0:t0 + tn], ident[0:H, 0:H])
                pe.transpose(bank[4][0:tn, tt * 16 + H:tt * 16 + 2 * H], rE[:, t0:t0 + tn], ident[0:H, 0:H])
            for j in range(HP):
                pe.matmul(bank[5][:, j * TS:(j + 1) * TS], selp[:, j, :], rZ[:, 0:TS], start=True, stop=True)
                ins = pe.matmul(bank[5][:, HP * TS + j * NB:HP * TS + (j + 1) * NB], selp[:, j, :],
                                rZ[:, TS:TS + NB], start=True, stop=True)
            ins.then_inc(S["uT_full"], 1)

            for t0, tn, tt in TOK:
                o = out_d()
                for j in range(HP):
                    ins = pe.transpose(o[0:tn, j * P:(j + 1) * P], kT[:, j, t0:t0 + tn], ident)
                done_d(ins)

            pe.wait_ge(S["ld_state"], 16 * 16)
            pe.wait_ge(S["qe_ready"], 1)
            pe.wait_ge(S["ga_free"], n_ga[0])
            for h in range(H):
                r = (h % 2) * DK
                for b in range(NB):
                    qq = qe[r:r + DK, h // 2, b * NS:(b + 1) * NS]
                    a = (h // 2 * NB + b) * NS
                    bn, bd = (bank[6], bank[7]) if h % 2 == 0 else (bank[0], bank[1])
                    pe.matmul(bn[:, a:a + NS], Ce[r:r + DK, h // 2, b, 0:DV], qq, start=True, stop=True)
                    ins = pe.matmul(bd[:, a:a + NS], Ce[r:r + DK, h // 2, b, DV:DV + 1].to_broadcast([DK, P]), qq,
                                    start=True, stop=True)
            ins.then_inc(S["inter_full"], 1)

            pe.wait_ge(S["gd_free"], n_gd[0])
            pe.wait_ge(S["e_ready"], 1)
            pe.wait_ge(S["inter_ready"], 1)

            def scores(h):
                if h >= 2:
                    pe.wait_ge(S["D_made"], h - 1)
                    pe.wait_ge(S["W_made"], h - 1)
                r = (h % 2) * DK
                kk, qq = kT[r:r + DK, h // 2, :], qT[r:r + DK, h // 2, :]
                s = bank[2 + h % 2]
                pe.matmul(bank[h % 2][:, 0:T], ident[0:H, h:h + 1].to_broadcast([H, P]), rM, start=True, stop=True)
                pe.matmul(s[:, 0:TP], kk[:, 0:P], qq[:, 0:TP], start=True, stop=True)
                pe.matmul(s[:, TP:TP + P], kk[:, P:TP], qq[:, P:TP], start=True, stop=True)
                pe.matmul(s[0:TS, TP + P:WM], kk[:, TP:T], qq[:, TP:T], start=True, stop=True).then_inc(S["s_full"], 1)

            def attend(h):
                if h:
                    pe.wait_ge(S["h_made"], h)
                pe.matmul(bank[4][:, 0:T], ident[0:H, h:h + 1].to_broadcast([H, P]), rA, start=True,
                          stop=True).then_inc(S["m_full"], 1)
                pe.wait_ge(S["W_made"], h + 1)
                for o, v0, v1, v2 in ((bank[5], VX[:, 0, h, 0:DV], VX[:, 1, h, 0:DV], VX[0:TS, 2, h, 0:DV]),
                                      (bank[6], ones, ones, ones[0:TS, :])):
                    pe.matmul(o[:, TP:T], v2, Wt[0:TS, TP + P:WM], start=True, stop=True)
                    pe.matmul(o[:, 0:TP], v0, Wt[:, 0:TP], start=True, stop=False)
                    ins = pe.matmul(o[:, P:TP], v1, Wt[:, TP:TP + P], start=False, stop=True)
                ins.then_inc(S["nd_full"], 1)

            scores(0)
            for h in range(H):
                if h + 1 < H:
                    scores(h + 1)
                attend(h)

            pe.wait_ge(S["h_made"], H)
            n_st = 0
            for g in range(HP):
                if n_st >= 4:
                    pe.wait_ge(S["st_free"], n_st - 3)
                o = bank[n_st % 4]
                for hh_ in range(2):
                    h = 2 * g + hh_
                    for s in range(2):
                        ins = pe.matmul(o[0:DK, hh_ * 129:hh_ * 129 + 129], Ke[:, s, h * DK:(h + 1) * DK],
                                        VX[:, s, h, :], start=(s == 0), stop=(s == 1))
                ins.then_inc(S["st_full"], 1)
                n_st += 1
            for b in range(NB):
                pe.wait_ge(S["kd_made"], b + 1)
                for g in range(2):
                    if n_st >= 4:
                        pe.wait_ge(S["st_free"], n_st - 3)
                    o = bank[n_st % 4]
                    for jj in range(2):
                        for par in range(2):
                            h = 2 * (2 * g + jj) + par
                            ins = pe.matmul(o[par * DK:(par + 1) * DK, jj * 129:jj * 129 + 129],
                                            kmb[b % 2][:, h * DK:(h + 1) * DK], VX[0:TS, 2, h, :], start=True, stop=True)
                    ins.then_inc(S["st_full"], 1)
                    n_st += 1

            for h in range(H):
                pe.wait_ge(S["hsq_ready"], h + 1)
                if h >= 2:
                    pe.wait_ge(S["y_ready"], h - 1)
                pe.matmul(bank[4 + h % 2][:, 0:T], ones, Dh[h % 2][:, 0:T], start=True, stop=True).then_inc(S["hss_full"], 1)
            pe.wait_ge(S["st_free"], n_st)
            for m in range(DC):
                name = f"out{m // 4}"
                arrived(name)
                w = wview(name, DC, CW)
                o = out_d()
                for k in range(DC):
                    if m == 0:
                        pe.wait_ge(S["y_ready"], k + 1)
                    ins = pe.matmul(o[:, 0:T], w[:, k, (m % 4) * P:(m % 4 + 1) * P], oT[:, k, :], start=(k == 0), stop=(k == DC - 1))
                done_d(ins, name if m % 4 == 3 else None)

            sum_squares(1, DC, xn, DC)
            pe.wait_ge(S["xn_ready"], 2 * DC)
            for f in range(FT):
                n, q = f // 4, f % 4
                rows = P if f < FT - 1 else FLAST
                arrived(f"gd{n}")
                arrived(f"ud{n}")
                wide_ = FCH[n][1]
                last = q == 3 or f == FT - 1
                w = wview(f"gd{n}", DC, wide_)
                o = out_a()
                ins = product(o[0:rows, 0:T], [(w[:, k, q * P:q * P + rows], xn[:, k, :]) for k in range(DC)])
                done_a(ins, f"gd{n}" if last else None)
                w = wview(f"ud{n}", DC, wide_)
                o = out_d()
                ins = product(o[0:rows, 0:T], [(w[:, k, q * P:q * P + rows], xn[:, k, :]) for k in range(DC)])
                done_d(ins, f"ud{n}" if last else None)
            up_done = n_gd[0]
            for m in range(DC):
                arrived(f"dd{m}")
                w = wview(f"dd{m}", FT, P)
                o = out_d()
                if m == 0:
                    pe.wait_ge(S["gd_free"], up_done)
                for k in range(FT):
                    rows = P if k < FT - 1 else FLAST
                    ins = pe.matmul(o[:, 0:T], w[0:rows, k, :], hT[0:rows, k, :], start=(k == 0), stop=(k == FT - 1))
                done_d(ins, f"dd{m}")

            sum_squares(2, DC, xn, 2 * DC)
            arrived("dkv")
            w = wview("dkv", DC, CKV + ROPE)
            pe.wait_ge(S["xn_ready"], 3 * DC)
            for m in range(CT + 1):
                rows = P if m < CT else ROPE
                o = out_d()
                ins = product(o[0:rows, 0:T], [(w[:, k, m * P:m * P + rows], hn[:, k, :]) for k in range(DC)])
                done_d(ins, "dkv" if m == CT else None)
            pe.wait_ge(S["xn_ready"], 4 * DC)
            arrived("dq")
            w = wview("dq", DC, QL)
            pe.wait_ge(S["gd_free"], GD_CQ)
            pe.matmul(bank[4][0:ROPE, 0:T], c("rot", ROPE), rtmp[0], start=True, stop=True).then_inc(S["rot_full"], 1)
            sum_squares(3, CT, ckvT, 3 * DC)
            pe.wait_ge(S["ckv_ready"], 1)
            for m in range(QT):
                o = out_d()
                ins = product(o[:, 0:T], [(w[:, k, m * P:(m + 1) * P], xn[:, k, :]) for k in range(DC)])
                done_d(ins, "dq" if m == QT - 1 else None)
            arrived("uk")
            w = wview("uk", CT, H * NOPE)
            for g in range(HP):
                o = out_d()
                for hh_ in range(2):
                    for k in range(CT):
                        h = 2 * g + hh_
                        ins = pe.transpose(o[:, (hh_ * CT + k) * P:(hh_ * CT + k + 1) * P],
                                           w[:, k, h * NOPE:(h + 1) * NOPE], ident)
                done_d(ins, "uk" if g == HP - 1 else None)
            sum_squares(4, QT, cq, 3 * DC + CT)
            for t0, tn, tt in TOK:
                o = out_d()
                for k in range(CT):
                    pe.transpose(o[0:tn, k * P:(k + 1) * P], ckvT[:, k, t0:t0 + tn], ident)
                ins = pe.transpose(o[0:tn, CKV:CKV + ROPE], krT[:, t0:t0 + tn], ident[0:ROPE, 0:ROPE])
                done_d(ins)
            pe.wait_ge(S["cq_ready"], 1)
            pe.wait_ge(S["kr_ready"], 1)

            def up_q(h):
                name = f"uq{h // HP}"
                arrived(name)
                w = wview(name, QT, HP * (NOPE + ROPE))
                a = (h % HP) * (NOPE + ROPE)
                o = out_a()
                done_a(product(o[:, 0:T], [(w[:, k, a:a + NOPE], cq[:, k, :]) for k in range(QT)]))
                o = out_a()
                ins = product(o[0:ROPE, 0:T], [(w[:, k, a + NOPE:a + NOPE + ROPE], cq[:, k, :]) for k in range(QT)])
                done_a(ins, name if h % HP == HP - 1 else None)

            def latent_q(h):
                pe.wait_ge(S["ga_free"], ga_q + 2 * (h + 1))
                if h:
                    pe.wait_ge(S["qr_ready"], h)
                pe.matmul(bank[4][0:ROPE, 0:T], c("rot", ROPE), rtmp[h % 2], start=True, stop=True).then_inc(S["rot_full"], 1)
                for k in range(CT):
                    o = out_d()
                    done_d(pe.matmul(o[:, 0:T], ukT[:, h, k * P:(k + 1) * P], qn[h % 2], start=True, stop=True))

            ga_q = n_ga[0]
            up_q(0)
            for h in range(H):
                if h + 1 < H:
                    up_q(h + 1)
                latent_q(h)
            pe.wait_ge(S["qr_ready"], H)
            pe.wait_ge(S["gd_free"], n_gd[0])

            units = [(h, q) for h in range(H) for q in range(2)]

            def p_scores(u):
                h, q = units[u]
                if u >= 2:
                    pe.wait_ge(S["p_exp"], u - 1)
                keys = (q + 1) * P
                o = bank[5 + u % 2][:, 0:keys]
                for k in range(CT):
                    pe.matmul(o, qlat[:, k, h, q * P:(q + 1) * P], ckvT[:, k, 0:keys], start=(k == 0), stop=False)
                pe.matmul(o, qrope[:, h, q * P:(q + 1) * P], krT[:, 0:keys], start=False, stop=True).then_inc(S["sc_full"], 1)

            def p_attend(u):
                h, q = units[u]
                pe.wait_ge(S["p_ready"], u + 1)
                if u:
                    pe.wait_ge(S["pt_ready"], u)
                for s in range(q + 1):
                    ins = pe.transpose(bank[7][:, s * P:(s + 1) * P], prob2[u % 2][:, s * P:(s + 1) * P], ident)
                ins.then_inc(S["pt_full"], 1)
                pe.wait_ge(S["pt_ready"], u + 1)
                if u:
                    pe.wait_ge(S["ol_ready"], u)
                for k in range(CT):
                    for s in range(q + 1):
                        ins = pe.matmul(bank[4][:, k * P:(k + 1) * P], ctok[:, s, k * P:(k + 1) * P],
                                        PT[:, s * P:(s + 1) * P], start=(s == 0), stop=(s == q))
                ins.then_inc(S["ol_full"], 1)

            p_scores(0)
            for u in range(len(units)):
                if u + 1 < len(units):
                    p_scores(u + 1)
                p_attend(u)

            NU = len(units)

            def cache_transposes(b):
                pe.wait_ge(ck_full[b % 2], 16 * 2 * NPG * (b // 2 + 1))
                for g in range(6):
                    n = 6 * b + g
                    if n >= 2:
                        pe.wait_ge(S["tpa_free"] if n % 2 == 0 else S["tpd_free"], n // 2)
                    part, half = g // 2, g % 2
                    for pg in range(4):
                        page = half * 4 + pg
                        src = ctk[b % 2][:, page, part * P:(part + 1) * P] if part < CT else crk[b % 2][:, page, :]
                        rows = P if part < CT else ROPE
                        ins = pe.transpose(bank[n % 2][0:rows, pg * P:(pg + 1) * P], src, ident)
                    ins.then_inc(S["tp_full"], 1)

            def s_scores(b):
                pe.wait_ge(S["tpa_free"], 3 * (b + 1))
                pe.wait_ge(S["tpd_free"], 3 * (b + 1))
                pe.wait_ge(S["p_exp"], NU + b)
                if b == 0:
                    pe.wait_ge(S["pt_ready"], NU)
                for a, n, kv, kr in ((0, 512, cacheT[:, :, 0:512], cacheR[:, 0:512]),
                                     (512, 512, cacheT[:, :, 512:PAST], cacheR[:, 512:PAST]),
                                     (PAST, TS, ckvT[:, :, TP:T], krT[:, TP:T])):
                    for k in range(CT):
                        pe.matmul(wide[0:TS, a:a + n], qls[:, k, b, :], kv[:, k, :], start=(k == 0), stop=False)
                    ins = pe.matmul(wide[0:TS, a:a + n], qrs[:, b, :], kr, start=False, stop=True)
                ins.then_inc(S["sc_full"], 1)

            def s_attend(b):
                pe.wait_ge(S["p_ready"], NU + b + 1)
                for pg in range(NPG + 1):
                    rows = P if pg < NPG else TS
                    ins = pe.transpose(bank[4][0:rows, pg * TS:(pg + 1) * TS], prob[0:TS, pg * P:pg * P + rows],
                                       ident[0:TS, 0:TS])
                ins.then_inc(S["pt_full"], 1)
                pe.wait_ge(S["pt_ready"], NU + b + 1)
                for k in range(CT):
                    for pg in range(NPG + 1):
                        v = ctk[b % 2][:, pg, k * P:(k + 1) * P] if pg < NPG else ctok[0:TS, 2, k * P:(k + 1) * P]
                        rows = P if pg < NPG else TS
                        ins = pe.matmul(bank[3][:, k * TS:(k + 1) * TS], v, PT[0:rows, pg * TS:(pg + 1) * TS],
                                        start=(pg == 0), stop=(pg == NPG))
                ins.then_inc(S["ol_full"], 1)

            pe.wait_ge(S["ol_ready"], NU)
            cache_transposes(0)
            for b in range(NB):
                s_scores(b)
                if b + 1 < NB:
                    cache_transposes(b + 1)
                if b:
                    pe.wait_ge(S["ol_ready"], NU + b)
                s_attend(b)
            pe.wait_ge(S["ol_ready"], NU + NB)
            pe.wait_ge(S["tpa_free"], 3 * NB)
            arrived("uv")
            w = wview("uv", CT, hv)
            for h in range(H):
                o = out_d()
                product(o[:, TP:T].rearrange("p (b s) -> p b s", s=NS),
                        [(w[:, k, h * DV:(h + 1) * DV], qls[:, k, :, h * NS:(h + 1) * NS]) for k in range(CT)])
                ins = product(o[:, 0:TP], [(w[:, k, h * DV:(h + 1) * DV], qlat[:, k, h, :]) for k in range(CT)])
                done_d(ins, "uv" if h == H - 1 else None)
            heads_out = n_gd[0]
            for m in range(DC):
                name = f"wo{m // 4}"
                arrived(name)
                w = wview(name, DC, CW)
                o = out_d()
                for k in range(DC):
                    if m == 0:
                        pe.wait_ge(S["gd_free"], heads_out - DC + k + 1)
                    ins = pe.matmul(o[:, 0:T], w[:, k, (m % 4) * P:(m % 4 + 1) * P], xn[:, k, :], start=(k == 0), stop=(k == DC - 1))
                done_d(ins, name if m % 4 == 3 else None)

            sum_squares(5, DC, acc_sq, 3 * DC + CT + QT)
            pe.wait_ge(S["xn_ready"], 5 * DC)
            pe.wait_ge(S["ld_wr"], 16)
            for t0, tn, tt in TOK:
                ins = product(bank[4][0:tn, tt * E:(tt + 1) * E], [(xn[:, k, t0:t0 + tn], wg[:, k, 0:E]) for k in range(DC)])
            ins.then_inc(S["lg_full"], 1)
            for src in (xn, xT):
                for t0, tn, tt in TOK:
                    for half in range(2):
                        o = out_d()
                        for q in range(4):
                            ins = pe.transpose(o[0:tn, q * P:(q + 1) * P], src[:, half * 4 + q, t0:t0 + tn], ident)
                        done_d(ins)
            pe.wait_ge(S["gd_free"], n_gd[0])
            pe.wait_ge(S["mask_ready"], 1)
            pe.wait_ge(S["ld_gf"], 32)
            tri = mc("tri")
            for t0, tn, tt in TOK:
                ins = product(bank[4][:, 32 + tt * E:32 + (tt + 1) * E],
                              [(ones, mk[:, s, :]) for s in range(tt)] + [(tri, mk[:, tt, :])])
            ins = product(bank[4][:, 64:64 + E], [(ones, mk[:, s, :]) for s in range(3)])
            ins.then_inc(S["rank_full"], 1)

            def gather(half):
                for q in range(4):
                    m = half * 4 + q
                    for t0, tn, tt in TOK:
                        ins = pe.matmul(bank[6 + half][:, q * P:(q + 1) * P], xtk[0:tn, tt, m * P:(m + 1) * P],
                                        Pm[0:tn, tt, :], start=(tt == 0), stop=(tt == 2))
                ins.then_inc(S["misc_full"], 1)

            pe.wait_ge(S["p_made"], 1)
            gather(0)
            gather(1)
            pe.wait_ge(S["tables_ready"], 1)
            n_items = pe.value_load(ints[0:1, 0:1], min_val=E, max_val=ITEMS)
            with pe.Fori(0, n_items) as it:
                def slot(k, a):
                    s, v = moe_slot(k)
                    pe.wait_ge(w_full[s], it * SLOT_STEP + v)
                    return ring[:, s, :].rearrange("p (c n) -> p c n", c=a)

                def free(use):
                    if use == 11:
                        pe.wait_ge(S["xg_ready"], it + 2)
                    else:
                        pe.wait_ge(S["misc_free"], it * (SHARED - 1) + (max(1, use) if use <= 10 else use - 1))

                def gate(j):
                    pe.wait_ge(S["gu_done"], it * CE + 1 + max(0, j - 1))
                    w = slot(3 * j, DC)
                    product(bank[j % 2][:, :], [(xg[:, q, :], w[:, q, :]) for q in range(DC)]).then_inc(S["g_full"], 1)

                def up(j):
                    w = slot(3 * j + 1, DC)
                    product(bank[2 + j % 2][:, :], [(xg[:, q, :], w[:, q, :]) for q in range(DC)]).then_inc(S["u_full"], 1)

                def turn(j):
                    pe.wait_ge(S["gu_done"], it * CE + 1 + j + 1)
                    free(1 + j)
                    for q in range(KD):
                        ins = pe.transpose(bank[6 + (1 + j) % 2][:, q * P:(q + 1) * P], hh[j % 2][:, q * P:(q + 1) * P], ident)
                    ins.then_inc(S["misc_full"], 1)

                def down(j):
                    w = slot(3 * j + 2, KD)
                    pe.wait_ge(S["misc_free"], it * (SHARED - 1) + j + 3)
                    if j == 0:
                        pe.wait_ge(S["y_free"], it + 1)
                    for q in range(KD):
                        for half in range(2):
                            ins = pe.matmul(bank[4 + half][:, :], hhT[j % 2][:, q * P:(q + 1) * P],
                                            w[:, q, half * CW:(half + 1) * CW],
                                            start=(j == 0 and q == 0), stop=(j == CE - 1 and q == KD - 1))
                    ins.then_inc(S["d_done"], 1)

                pe.wait_ge(S["xg_ready"], it + 1)
                gate(0)
                up(0)
                free(0)
                for t0, tn, tt in TOK:
                    ins = pe.transpose(bank[6][:, t0:t0 + tn], Pg[0:tn, tt, :], ident[0:tn, 0:tn])
                ins.then_inc(S["misc_full"], 1)
                for j in range(CE - 1):
                    gate(j + 1)
                    turn(j)
                    up(j + 1)
                    down(j)
                turn(CE - 1)
                pe.wait_ge(S["p_made"], it + 2)
                free(1 + CE)
                gather(0)
                down(CE - 1)
                free(2 + CE)
                gather(1)
                pe.wait_ge(S["y_free"], it + 2)
                for u, (t0, tn, tt) in enumerate(TOK):
                    for half in range(2):
                        n = 1 + CE + 2 + 2 * u + half
                        free(n)
                        pe.matmul(bank[6 + n % 2][0:tn, :], PTg[:, t0:t0 + tn], ysb[:, half * CW:(half + 1) * CW],
                                  start=True, stop=True).then_inc(S["misc_full"], 1)

        @block.vector
        def _(v):
            chain = [0]

            def link(ins):
                chain[0] += 1
                ins.then_inc(S["dchain"], 1)
                v.wait_ge(S["dchain"], chain[0])

            n_gd = [0]

            def in_d():
                n_gd[0] += 1
                v.wait_ge(S["gd_full"], n_gd[0])
                return bank[2 + (n_gd[0] - 1) % 2]

            def free_d(ins):
                ins.then_inc(S["gd_free"], 1)

            def normalise(k, chunks_, src, gname, dst, ready, first=True, every=True):
                if first:
                    v.wait_ge(S["std_ready"], k + 1)
                    link(v.reciprocal(stdv(k), stdv(k)))
                for m in range(chunks_):
                    ins = v.scalar_tensor_tensor(out=dst[:, m, :], in0=src[:, m, :], scalar=gain(gname, m),
                                                 in1=stdv(k), op0=ALU.mult, op1=ALU.mult)
                    if every or m == chunks_ - 1:
                        ins.then_inc(S[ready], 1)

            v.wait_ge(S["gt_full"], 1)
            v.tensor_copy(gT[:, :], bank[4][:, 0:GROWS]).then_inc(S["gt_ready"], 1)
            v.wait_ge(S["ld_tiny"], 32)
            v.tensor_scalar(tiny[:, 2:4], tiny[:, 0:2], 1.0 / CAP, None, ALU.mult).then_inc(S["bg_ready"], 1)
            for m in range(DC):
                v.wait_ge(S["x_full"], m + 1)
                v.tensor_copy(xT[:, m, :], bank[m % 2][:, 0:T]).then_inc(S["x_ready"], 1)
            v.wait_ge(S["gt_ready"], 1)
            normalise(0, DC, xT, "g_norm_a", xn, "xn_ready")
            link(v.memset(VX[:, :, :, DV:DV + 1], 1.0))
            link(v.memset(uT[:, :, :], 0.0))
            link(v.memset(rZ[:, :], 0.0))
            for m in range(HP):
                o = in_d()
                free_d(v.tensor_copy(kT[:, m, :], o[:, 0:T]))

            v.wait_ge(S["lf_ready"], 1)
            m0 = tiny[:, 8:16]
            link(v.tensor_scalar(rU, rU, CAP, None, ALU.mult))
            link(v.tensor_scalar(rE, rE, -1.0, None, ALU.mult))
            link(v.tensor_tensor_scan(rA[:, 0:TP], rE[:, 0:TP], rZ[:, 0:TP], 0.0, ALU.add, ALU.add))

            def step(row, t):
                return row[:, TP:T].rearrange("p (b s) -> p b s", s=NS)[:, :, t]

            link(v.tensor_copy(step(rA, 0), step(rE, 0)))
            for t in range(1, NS):
                link(v.tensor_tensor(step(rA, t), step(rA, t - 1), step(rE, t), ALU.add))
            link(v.tensor_tensor(rU, rU, rA, ALU.subtract))
            link(v.tensor_tensor_scan(rM[:, 0:TP], rU[:, 0:TP], rU[:, 0:TP], 0.0, ALU.max, ALU.max))
            link(v.tensor_tensor(step(rM, 0), m0, step(rU, 0), ALU.max))
            for t in range(1, NS):
                link(v.tensor_tensor(step(rM, t), step(rM, t - 1), step(rU, t), ALU.max))
            link(v.tensor_scalar(rE[:, 0:TP], rU[:, 0:TP], rM[:, TP - 1:TP], None, ALU.subtract))
            for t in range(NS):
                link(v.tensor_tensor(step(rE, t), step(rU, t), step(rM, NS - 1), ALU.subtract))
            zt = rZ[:, 0:TS].rearrange("p (b s) -> p b s", s=NS)
            for t in range(NS):
                link(v.tensor_tensor(zt[:, :, t], m0, step(rM, t), ALU.subtract))
            link(v.tensor_tensor(rZ[:, TS:TS + NB], m0, step(rM, NS - 1), ALU.subtract))
            link(v.tensor_tensor(rA, rA, rM, ALU.add))
            link(v.tensor_copy(tiny[:, 16:17], rA[:, TP - 1:TP]))
            link(v.tensor_copy(tiny[:, 17:17 + NB], step(rA, NS - 1)))
            link(v.tensor_scalar(rA, rA, -1.0, None, ALU.mult))
            v.tensor_scalar(rM, rM, -1.0, None, ALU.mult).then_inc(S["rows_ready"], 1)

            for n in range(2):
                for t0, tn, tt in TOK:
                    o = in_d()
                    free_d(v.tensor_copy(VX[0:tn, tt, 4 * n:4 * n + 4, 0:DV],
                                         o[0:tn, :].rearrange("p (h n) -> p h n", h=4)))
            v.wait_ge(S["uT_full"], 1)
            v.tensor_copy(uT[:, 0:2, :], bank[4][:, 0:32].rearrange("p (a b) -> p a b", a=2)).then_inc(S["uT_ready"], 1)
            v.tensor_copy(uT[0:TS, 2, :], bank[4][0:TS, 32:48]).then_inc(S["uT_ready"], 1)
            v.wait_ge(S["e_ready"], 1)
            v.wait_ge(S["ga_free"], HP)
            v.tensor_tensor(qe[:, :, :], qT[:, :, TP:T], eI[:, :, :], ALU.mult).then_inc(S["qe_ready"], 1)
            for t0, tn, tt in TOK:
                o = in_d()
                free_d(v.tensor_tensor(Ke[0:tn, tt, :].rearrange("p (h k) -> p h k", h=H),
                                       o[0:tn, :].rearrange("p (h k) -> p h k", h=H),
                                       uT[0:tn, tt, H:2 * H].unsqueeze(2).to_broadcast([tn, H, DK]), ALU.mult))
            v.wait_ge(S["inter_full"], 1)
            for dst, even, odd in ((inN, bank[6], bank[0]), (inD, bank[7], bank[1])):
                for par, o in ((0, even), (1, odd)):
                    ins = v.tensor_copy(dst.rearrange("p (j a) b -> p j a b", a=2)[:, :, par, :],
                                        o[:, 0:HP * TS].rearrange("p (j b) -> p j b", j=HP))
            link(ins)
            v.memset(den[:, 0:1], 0.0).then_inc(S["inter_ready"], 1)

            def decay(h):
                v.wait_ge(S["s_full"], h + 1)
                if h >= 2:
                    v.wait_ge(S["W_made"], h - 1)
                d, m = Dh[h % 2], bank[h % 2]
                for a, n, m_at, tt in ((0, TP, 0, 0), (TP, P, P, 1), (TP + P, TS, TP, 2)):
                    ins = v.scalar_tensor_tensor(out=d[:, a:a + n], in0=m[:, m_at:m_at + n], scalar=uT[:, tt, h:h + 1],
                                                 in1=cmask[:, a:a + n], op0=ALU.add, op1=ALU.min)
                ins.then_inc(S["D_made"], 1)

            v.wait_ge(S["ld_ac"], 16)
            v.wait_ge(S["uT_ready"], 2)
            decay(0)
            for h in range(H):
                if h + 1 < H:
                    decay(h + 1)
                v.wait_ge(S["exp_done"], h + 1)
                if h:
                    v.wait_ge(S["nd_full"], h)
                s = bank[2 + h % 2]
                v.tensor_tensor(Wt[:, 0:TP + P], Dh[h % 2][:, 0:TP + P], s[:, 0:TP + P], ALU.mult)
                v.tensor_tensor(Wt[0:TS, TP + P:WM], Dh[h % 2][0:TS, TP + P:WM], s[0:TS, TP + P:WM],
                                ALU.mult).then_inc(S["W_made"], 1)
                v.wait_ge(S["nd_full"], h + 1)
                v.tensor_copy(den[:, 0:TP], bank[6][:, 0:TP])
                link(v.tensor_tensor(den[:, TP:T], bank[6][:, TP:T], inD[:, h, :], ALU.add))
                v.wait_ge(S["em_done"], h + 1)
                link(v.scalar_tensor_tensor(out=den, in0=den, scalar=-1.0, in1=den, op0=ALU.mult, op1=ALU.max))
                link(v.tensor_tensor(den, den, bank[4][:, 0:T], ALU.max))
                link(v.reciprocal(den, den))
                v.tensor_tensor(xn[:, h, 0:TP], bank[5][:, 0:TP], den[:, 0:TP], ALU.mult)
                link(v.tensor_tensor(inN[:, h, :], bank[5][:, TP:T], inN[:, h, :], ALU.add))
                v.tensor_tensor(xn[:, h, TP:T], inN[:, h, :], den[:, TP:T], ALU.mult).then_inc(S["h_made"], 1)

            n_st = 0
            for g in range(HP):
                n_st += 1
                v.wait_ge(S["st_full"], n_st)
                v.tensor_copy(Cp[:, 2 * g:2 * g + 2, :],
                              bank[(n_st - 1) % 4][0:DK, 0:258].rearrange("p (a b) -> p a b", a=2)).then_inc(S["st_free"], 1)

            def mask_keys(b):
                v.tensor_scalar(kmb[b % 2], Ke[0:TS, 2, :], c("bsel", TS)[:, b:b + 1], None, ALU.mult).then_inc(S["kd_made"], 1)

            v.wait_ge(S["gd_free"], n_gd[0])
            mask_keys(0)
            mask_keys(1)
            for b in range(NB):
                for g in range(2):
                    n_st += 1
                    v.wait_ge(S["st_full"], n_st)
                    o = bank[(n_st - 1) % 4]
                    for jj in range(2):
                        j = 2 * g + jj
                        ins = v.scalar_tensor_tensor(out=Ce[:, j, b, :], in0=Ce[:, j, b, :],
                                                     scalar=eC[:, j * NB + b:j * NB + b + 1],
                                                     in1=o[:, jj * 129:jj * 129 + 129], op0=ALU.mult, op1=ALU.add)
                    ins.then_inc(S["st_free"], 1)
                if b + 2 < NB:
                    mask_keys(b + 2)

            for h in range(H):
                v.wait_ge(S["hstd_ready"], h + 1)
                link(v.reciprocal(den, bank[4 + h % 2][:, 0:T]))
                link(v.scalar_tensor_tensor(out=xn[:, h, :], in0=xn[:, h, :], scalar=gain("g_head_a", h), in1=den,
                                            op0=ALU.mult, op1=ALU.mult))
                v.tensor_tensor(oT[:, h, :], oT[:, h, :], xn[:, h, :], ALU.mult).then_inc(S["y_ready"], 1)

            def residual():
                for m in range(DC):
                    o = in_d()
                    free_d(v.tensor_tensor(xT[:, m, :], xT[:, m, :], o[:, 0:T], ALU.add))

            residual()
            normalise(1, DC, xT, "g_ffn_d", xn, "xn_ready")
            v.wait_ge(S["stored"], 16 * STORES_A)
            for f in range(FT):
                rows = P if f < FT - 1 else FLAST
                o = in_d()
                v.wait_ge(S["ga_free"], GA_FFN + f + 1)
                free_d(v.tensor_tensor(hT[0:rows, f, :], sg[f % 2][0:rows, :], o[0:rows, 0:T], ALU.mult))
            residual()

            normalise(2, DC, xT, "g_kv", hn, "xn_ready")
            normalise(2, DC, xT, "g_norm_b", xn, "xn_ready", first=False)
            for m in range(CT):
                o = in_d()
                free_d(v.tensor_copy(raw[:, m, :], o[:, 0:T]))
            o = in_d()
            free_d(v.tensor_copy(rtmp[0], o[0:ROPE, 0:T]))

            def rotate(n, src):
                v.wait_ge(S["rot_full"], n)
                v.tensor_tensor(rt2, bank[4][0:ROPE, 0:T], c("sin", ROPE), ALU.mult)
                link(v.tensor_tensor(src, src, c("cos", ROPE), ALU.mult))

            rotate(1, rtmp[0])
            v.tensor_tensor(krT, rtmp[0], rt2, ALU.add).then_inc(S["kr_ready"], 1)
            normalise(3, CT, raw, "g_ckv", ckvT, "ckv_ready", every=False)
            for m in range(QT):
                o = in_d()
                if m == 0:
                    v.wait_ge(S["ckv_ready"], 1)
                free_d(v.tensor_copy(raw[:, m, :], o[:, 0:T]))
            for g in range(HP):
                o = in_d()
                free_d(v.tensor_copy(ukT[:, 2 * g:2 * g + 2, :], o[:, :].rearrange("p (a b) -> p a b", a=2)))
            normalise(4, QT, raw, "g_q", cq, "cq_ready", every=False)
            for t0, tn, tt in TOK:
                o = in_d()
                free_d(v.tensor_copy(ctok[0:tn, tt, :], o[0:tn, 0:CKV + ROPE]))
            for h in range(H):
                rt_ = rtmp[h % 2]
                rotate(2 + h, rt_)
                v.tensor_tensor(qrope[:, h, :], rt_[:, 0:TP], rt2[:, 0:TP], ALU.add)
                v.tensor_tensor(qrs[:, :, h * NS:(h + 1) * NS], rt_[:, TP:T].rearrange("p (b s) -> p b s", s=NS),
                                rt2[:, TP:T].rearrange("p (b s) -> p b s", s=NS), ALU.add).then_inc(S["qr_ready"], 1)
                for k in range(CT):
                    o = in_d()
                    v.tensor_copy(qlat[:, k, h, :], o[:, 0:TP])
                    free_d(v.tensor_copy(qls[:, k, :, h * NS:(h + 1) * NS],
                                         o[:, TP:T].rearrange("p (b s) -> p b s", s=NS)))

            mx, nb, sm = cols[:, 0:1], cols[:, 1:2], cols[:, 2:3]

            def softmax_max(n, s, rows, mask_at, mask):
                v.wait_ge(S["sc_full"], n + 1)
                m = s[:, mask_at:mask_at + mask.shape[-1]]
                link(v.tensor_tensor(m, m, mask, ALU.add))
                link(v.reduce_max(mx[0:rows, :], s, AX.X))
                v.tensor_scalar(nb[0:rows, :], mx[0:rows, :], -SCALE, None, ALU.mult).then_inc(S["max_ready"], 1)

            def softmax_divide(n, p, rows):
                v.wait_ge(S["p_exp"], n + 1)
                link(v.reciprocal(sm[0:rows, :], sm[0:rows, :]))
                v.tensor_scalar(p, p, sm[0:rows, :], None, ALU.mult).then_inc(S["p_ready"], 1)

            units = [(h, q) for h in range(H) for q in range(2)]
            for u, (h, q) in enumerate(units):
                keys = (q + 1) * P
                softmax_max(u, bank[5 + u % 2][:, 0:keys], P, q * P, c("pmask"))
                softmax_divide(u, prob2[u % 2][:, 0:keys], P)
                v.wait_ge(S["pt_full"], u + 1)
                v.tensor_copy(PT[:, 0:keys], bank[7][:, 0:keys]).then_inc(S["pt_ready"], 1)
                v.wait_ge(S["ol_full"], u + 1)
                v.tensor_copy(qlat[:, :, h, q * P:(q + 1) * P],
                              bank[4][:, 0:CT * P].rearrange("p (a b) -> p a b", a=CT)).then_inc(S["ol_ready"], 1)
            NU = len(units)

            def cache_evac(b):
                for g in (1, 3, 5):
                    n = 6 * b + g
                    v.wait_ge(S["tp_full"], n + 1)
                    part, half = g // 2, g % 2
                    if part < CT:
                        ins = v.tensor_copy(cacheT[:, part, half * 512:(half + 1) * 512], bank[1][:, :])
                    else:
                        ins = v.tensor_copy(cacheR[:, half * 512:(half + 1) * 512], bank[1][0:ROPE, :])
                    ins.then_inc(S["tpd_free"], 1)

            cache_evac(0)
            for b in range(NB):
                u = NU + b
                softmax_max(u, wide[0:TS, 0:PAST + TS], TS, PAST, c("smask", TS)[:, (NB - 1 - b) * NS:(NB - 1 - b) * NS + TS])
                if b + 1 < NB:
                    cache_evac(b + 1)
                softmax_divide(u, prob[0:TS, :], TS)
                v.wait_ge(S["pt_full"], u + 1)
                v.tensor_copy(PT[:, 0:NPG * TS], bank[4][:, 0:NPG * TS])
                v.tensor_copy(PT[0:TS, NPG * TS:(NPG + 1) * TS],
                              bank[4][0:TS, NPG * TS:(NPG + 1) * TS]).then_inc(S["pt_ready"], 1)
                v.wait_ge(S["ol_full"], u + 1)
                ins = v.tensor_copy(qls[:, :, b, :], bank[3][:, 0:CT * TS].rearrange("p (a n) -> p a n", a=CT))
                ins.then_inc(S["ol_ready"], 1)
            for h in range(H):
                o = in_d()
                free_d(v.tensor_copy(xn[:, h, :], o[:, 0:T]))
            residual()
            normalise(5, DC, xT, "g_ffn_m", xn, "xn_ready")

            for dst in (xtk, acc):
                for t0, tn, tt in TOK:
                    for half in range(2):
                        o = in_d()
                        free_d(v.tensor_copy(dst[0:tn, tt, half * CW:(half + 1) * CW], o[0:tn, :]))
            v.wait_ge(S["lg_full"], 1)
            v.wait_ge(S["ld_gf"], 32)
            link(v.memset(rt[:, 0:408], 0.0))
            link(v.tensor_copy(lg[:, 0:2, :], bank[4][:, 0:2 * E].rearrange("p (a b) -> p a b", a=2)))
            link(v.tensor_copy(lg[0:TS, 2, :], bank[4][0:TS, 2 * E:3 * E]))
            for tt in range(3):
                link(v.max(top[:, tt, :], lg[:, tt, :]))
                link(v.max_index(idu[:, tt, :], top[:, tt, :], lg[:, tt, :]))
            link(v.tensor_copy(idf, idu[:, :, :]))
            iota8 = mc("iota")[:, 0:E].unsqueeze(1).to_broadcast([P, 3, E])
            link(v.tensor_tensor(oh1, iota8, idf[:, :, 0:1].to_broadcast([P, 3, E]), ALU.is_equal))
            link(v.tensor_tensor(oh2, iota8, idf[:, :, 1:2].to_broadcast([P, 3, E]), ALU.is_equal))
            link(v.tensor_tensor(mk, oh1, oh2, ALU.add))
            v.tensor_tensor(mk, mk, mc("valid").unsqueeze(2).to_broadcast([P, 3, E]), ALU.mult).then_inc(S["mask_ready"], 1)
            v.tensor_tensor(gk[:, :, 1:2], top[:, :, 1:2], top[:, :, 0:1], ALU.subtract).then_inc(S["mask_ready"], 1)
            v.wait_ge(S["gk_exp"], 1)
            link(v.tensor_scalar(gk[:, :, 0:1], gk[:, :, 1:2], 1.0, None, ALU.add))
            link(v.reciprocal(gk[:, :, 0:1], gk[:, :, 0:1]))
            link(v.tensor_tensor(gk[:, :, 1:2], gk[:, :, 1:2], gk[:, :, 0:1], ALU.mult))
            link(v.tensor_tensor(oh1, oh1, gk[:, :, 0:1].to_broadcast([P, 3, E]), ALU.mult))
            link(v.tensor_tensor(oh2, oh2, gk[:, :, 1:2].to_broadcast([P, 3, E]), ALU.mult))
            link(v.tensor_tensor(gt, oh1, oh2, ALU.add))
            v.wait_ge(S["rank_full"], 1)
            link(v.tensor_copy(pos, bank[4][:, 32:56].rearrange("p (a b) -> p a b", a=3)))
            link(v.tensor_copy(cnt, bank[4][:, 64:72]))
            link(v.tensor_tensor(pos, pos, mk, ALU.mult))
            link(v.tensor_scalar(pos, pos, -1.0, None, ALU.add))
            link(v.tensor_copy(posI[:, :, 0:E], pos))
            link(v.tensor_copy(gateI[:, :, 0:E], gt))

            def one_hots(item):
                for tt in range(3):
                    v.tensor_scalar(Pm[:, tt, :], mc("iota"), posI[:, tt, item], None, ALU.is_equal)
                    ins = v.tensor_scalar(Pg[:, tt, :], mc("iota"), posI[:, tt, item], gateI[:, tt, item],
                                          ALU.is_equal, ALU.mult)
                return ins

            one_hots(slice(0, 1)).then_inc(S["p_made"], 1)
            two = lambda a: a.unsqueeze(2).to_broadcast([P, E, 2])
            link(v.tensor_tensor(fl.rearrange("p (e k) -> p e k", k=2), two(cnt),
                                 mc("kbase").rearrange("p (e k) -> p e k", k=2), ALU.is_gt))
            link(v.tensor_tensor_scan(cum, fl, mc("kbase"), 0.0, ALU.add, ALU.min))
            link(v.tensor_scalar(nf[:, 0:1], cum[:, 2 * E - 1:2 * E], float(E), None, ALU.add))
            link(v.tensor_tensor(cum, cum, fl, ALU.subtract))
            for j in range(EXTRA):
                link(v.scalar_tensor_tensor(out=sel, in0=cum, scalar=float(j), in1=fl, op0=ALU.is_equal, op1=ALU.mult))
                link(v.tensor_tensor(s16, sel, mc("eidx"), ALU.mult))
                link(v.reduce_sum(nf[:, 1 + j:2 + j], s16, AX.X))
                link(v.tensor_tensor(s16, sel, mc("kbase"), ALU.mult))
                link(v.reduce_sum(nf[:, 6:7], s16, AX.X))
                for src, dst in ((pos, posI), (gt, gateI)):
                    link(v.tensor_tensor(p48.rearrange("p a (e k) -> p a e k", k=2),
                                         src.unsqueeze(3).to_broadcast([P, 3, E, 2]),
                                         sel.rearrange("p (e k) -> p e k", k=2).unsqueeze(1).to_broadcast([P, 3, E, 2]), ALU.mult))
                    link(v.reduce_sum(dst[:, :, E + j:E + j + 1], p48, AX.X))
                link(v.tensor_scalar(posI[:, :, E + j], posI[:, :, E + j], nf[:, 6:7], None, ALU.subtract))
            v.tensor_copy(ints[0:1, 0:5], nf[0:1, 0:5]).then_inc(S["tables_ready"], 1)

            v.wait_ge(S["tables_ready"], 1)
            n_items = v.value_load(ints[0:1, 0:1], min_val=E, max_val=ITEMS)

            def take_tokens(value):
                for half, taken in ((0, "misc_free"), (1, "xg_ready")):
                    v.wait_ge(S["misc_full"], value + half)
                    v.tensor_copy(xg[:, 4 * half:4 * half + 4, :].rearrange("p a b -> p (a b)"),
                                  bank[6 + half][:, :]).then_inc(S[taken], 1)

            v.wait_ge(S["kv_stored"], 64)
            take_tokens(1)
            v.memset(cols[0:1, 4:5], 0.0).then_inc(S["gu_done"], 1)
            v.memset(cols[0:1, 5:6], 0.0).then_inc(S["y_free"], 1)
            with v.Fori(0, n_items) as it:
                base = it * SHARED + 2
                v.wait_ge(S["misc_full"], base + 1)
                v.tensor_copy(PTg, bank[6][:, 0:T]).then_inc(S["misc_free"], 1)
                one_hots(bass.ds(it + 1, 1)).then_inc(S["p_made"], 1)
                for j in range(CE):
                    v.wait_ge(S["silu_done"], it * CE + j + 1)
                    v.wait_ge(S["u_full"], it * CE + j + 1)
                    v.tensor_tensor(hh[j % 2], sl[j % 2], bank[2 + j % 2][:, :], ALU.mult).then_inc(S["gu_done"], 1)
                    v.wait_ge(S["misc_full"], base + 1 + j + 1)
                    if j >= 2:
                        v.wait_ge(S["d_done"], it * CE + j - 1)
                    v.tensor_copy(hhT[j % 2], bank[6 + (1 + j) % 2][:, :]).then_inc(S["misc_free"], 1)
                v.wait_ge(S["misc_full"], base + 1 + CE + 1)
                v.tensor_copy(xg[:, 0:4, :].rearrange("p a b -> p (a b)"), bank[6][:, :]).then_inc(S["misc_free"], 1)
                v.wait_ge(S["d_done"], it * CE + CE)
                v.tensor_copy(ysb[:, 0:CW], bank[4][:, :])
                v.tensor_copy(ysb[:, CW:D], bank[5][:, :]).then_inc(S["y_free"], 1)
                v.wait_ge(S["misc_full"], base + 1 + CE + 2)
                v.tensor_copy(xg[:, 4:8, :].rearrange("p a b -> p (a b)"), bank[7][:, :]).then_inc(S["xg_ready"], 1)
                for u, (t0, tn, tt) in enumerate(TOK):
                    for half in range(2):
                        n = 1 + CE + 2 + 2 * u + half
                        v.wait_ge(S["misc_full"], base + n + 1)
                        a = acc[0:tn, tt, half * CW:(half + 1) * CW]
                        v.tensor_tensor(a, a, bank[6 + n % 2][0:tn, :], ALU.add).then_inc(S["misc_free"], 1)

            v.memset(cols[0:1, 6:7], 0.0).then_inc(S["acc_done"], 1)
            for t0, tn, tt in TOK:
                v.wait_ge(S["fin_ss"], tt + 1)
                s = cols[0:tn, 8 + tt:9 + tt]
                link(v.reciprocal(s, s))
                v.scalar_tensor_tensor(out=acc[0:tn, tt, :], in0=acc[0:tn, tt, :], scalar=s, in1=gfin[0:tn, :],
                                       op0=ALU.mult, op1=ALU.mult).then_inc(S["fin_ready"], 1)

        @block.scalar
        def _(a):
            b_gate = i["b_gate_a"][0].rearrange("(g h) -> h g", g=2)
            a.dma_start(tiny[:, 0:2], b_gate).then_inc(S["ld_tiny"], 16)
            a.dma_start(tiny[:, 8:16], i["state_m"][0].rearrange("b h -> h b")).then_inc(S["ld_tiny"], 16)
            a.dma_start(wg[:, :, :], rows_of(w_in, 2 * hq + 2 * hv, 2 * H)).then_inc(S["ld_wg"], 16)
            a.dma_start(ac[:, :], i["aconst"]).then_inc(S["ld_ac"], 16)
            n_ga, n_link = [0], [0]

            def link(ins):
                n_link[0] += 1
                ins.then_inc(S["achain"], 1)
                a.wait_ge(S["achain"], n_link[0])

            def in_a():
                n_ga[0] += 1
                a.wait_ge(S["ga_full"], n_ga[0])
                return bank[(n_ga[0] - 1) % 2]

            def squares(chunks_, src, dst, sem_, first):
                for m in range(chunks_):
                    a.wait_ge(S[sem_], first + m + 1)
                    a.activation(dst[:, m, :], src[:, m, :], ACT.Square).then_inc(S["sq_ready"], 1)

            def root(k, width):
                a.wait_ge(S["ss_full"], k + 1)
                a.activation(stdv(k), bank[7][:, 0:T], ACT.Sqrt, bias=c("eps"), scale=1.0 / width).then_inc(S["std_ready"], 1)

            a.wait_ge(S["ld_const"], 16)
            squares(DC, xT, xn, "x_ready", 0)
            root(0, D)
            a.wait_ge(S["gates_full"], 1)
            a.wait_ge(S["bg_ready"], 1)
            a.activation(rU, bank[4][0:H, 0:T], ACT.Tanh, bias=tiny[:, 2:3], scale=1.0 / CAP)
            link(a.activation(rE, bank[5][0:H, 0:T], ACT.Tanh, bias=tiny[:, 3:4], scale=1.0 / CAP))
            link(a.activation(rE, rE, ACT.Exp, scale=-CAP))
            a.activation(rE, rE, ACT.Ln, bias=c("one", H), scale=1.0).then_inc(S["lf_ready"], 1)
            for m in range(HP):
                o = in_a()
                a.activation(qT[:, m, :], o[:, 0:T], ACT.Copy, scale=DK ** -0.5).then_inc(S["ga_free"], 1)
            for m in range(DC):
                o = in_a()
                a.activation(oT[:, m, :], o[:, 0:T], ACT.Sigmoid).then_inc(S["ga_free"], 1)
            a.wait_ge(S["uT_full"], 1)
            a.activation(eI.rearrange("p a b -> p (a b)"), bank[5][:, 0:HP * TS], ACT.Exp)
            a.activation(eC, bank[5][:, HP * TS:HP * TS + HP * NB], ACT.Exp)
            a.wait_ge(S["uT_ready"], 2)
            a.activation(uT[:, :, H:2 * H], uT[:, :, H:2 * H], ACT.Exp).then_inc(S["e_ready"], 1)
            for h in range(H):
                a.wait_ge(S["D_made"], h + 1)
                a.activation(Dh[h % 2], Dh[h % 2], ACT.Exp).then_inc(S["exp_done"], 1)
                a.wait_ge(S["m_full"], h + 1)
                a.activation(bank[4][:, 0:T], bank[4][:, 0:T], ACT.Exp).then_inc(S["em_done"], 1)
            a.wait_ge(S["h_made"], H)

            def head_square(h):
                if h >= 2:
                    a.wait_ge(S["hss_full"], h - 1)
                a.activation(Dh[h % 2][:, 0:T], xn[:, h, :], ACT.Square).then_inc(S["hsq_ready"], 1)

            head_square(0)
            for h in range(H):
                if h + 1 < H:
                    head_square(h + 1)
                a.wait_ge(S["hss_full"], h + 1)
                b4 = bank[4 + h % 2][:, 0:T]
                a.activation(b4, b4, ACT.Sqrt, bias=c("eps"), scale=1.0 / DV).then_inc(S["hstd_ready"], 1)
            squares(DC, xT, xn, "gd_free", GD_FFN - DC)
            root(1, D)
            for f in range(FT):
                rows = P if f < FT - 1 else FLAST
                o = in_a()
                if f >= 2:
                    a.wait_ge(S["gd_free"], GD_FFN + f - 1)
                a.activation(sg[f % 2][0:rows, :], o[0:rows, 0:T], ACT.Silu).then_inc(S["ga_free"], 1)
            squares(DC, xT, xn, "gd_free", GD_CKV - DC)
            root(2, D)
            squares(CT, raw, ckvT, "gd_free", GD_CKV)
            root(3, CKV)
            squares(QT, raw, cq, "gd_free", GD_CQ)
            root(4, QL)
            a.wait_ge(S["kr_ready"], 1)
            a.wait_ge(S["cq_ready"], 1)
            for h in range(H):
                if h >= 2:
                    a.wait_ge(S["qr_ready"], h - 1)
                    a.wait_ge(S["gd_full"], GD_QL + CT * (h - 1))
                o = in_a()
                a.activation(qn[h % 2], o[:, 0:T], ACT.Copy).then_inc(S["ga_free"], 1)
                o = in_a()
                a.activation(rtmp[h % 2], o[0:ROPE, 0:T], ACT.Copy).then_inc(S["ga_free"], 1)
            nb, sm = cols[:, 1:2], cols[:, 2:3]
            units = [(h, q) for h in range(H) for q in range(2)]
            for u, (h, q) in enumerate(units):
                keys = (q + 1) * P
                a.wait_ge(S["max_ready"], u + 1)
                a.activation(prob2[u % 2][:, 0:keys], bank[5 + u % 2][:, 0:keys], ACT.Exp, bias=nb, scale=SCALE,
                             accum_out=sm).then_inc(S["p_exp"], 1)

            def cache_evac(b):
                for g in (0, 2, 4):
                    a.wait_ge(S["tp_full"], 6 * b + g + 1)
                    part, half = g // 2, g % 2
                    if part < CT:
                        ins = a.activation(cacheT[:, part, half * 512:(half + 1) * 512], bank[0][:, :], ACT.Copy)
                    else:
                        ins = a.activation(cacheR[:, half * 512:(half + 1) * 512], bank[0][0:ROPE, :], ACT.Copy)
                    ins.then_inc(S["tpa_free"], 1)

            cache_evac(0)
            for b in range(NB):
                a.wait_ge(S["max_ready"], len(units) + b + 1)
                a.activation(prob[0:TS, :], wide[0:TS, 0:PAST + TS], ACT.Exp, bias=nb[0:TS, :], scale=SCALE,
                             accum_out=sm[0:TS, :]).then_inc(S["p_exp"], 1)
                if b + 1 < NB:
                    cache_evac(b + 1)
            squares(DC, xT, acc_sq, "gd_free", GD_MOE - DC)
            root(5, D)
            a.wait_ge(S["mask_ready"], 2)
            a.activation(gk[:, :, 1:2], gk[:, :, 1:2], ACT.Exp).then_inc(S["gk_exp"], 1)
            a.wait_ge(S["tables_ready"], 1)
            n_items = a.value_load(ints[0:1, 0:1], min_val=E, max_val=ITEMS)
            with a.Fori(0, n_items) as it:
                for j in range(CE):
                    a.wait_ge(S["g_full"], it * CE + j + 1)
                    a.wait_ge(S["gu_done"], it * CE + 1 + max(0, j - 1))
                    a.activation(sl[j % 2], bank[j % 2][:, :], ACT.Silu).then_inc(S["silu_done"], 1)
            a.wait_ge(S["acc_done"], 1)
            for t0, tn, tt in TOK:
                s = cols[0:tn, 8 + tt:9 + tt]
                link(a.activation(xtk[0:tn, tt, :], acc[0:tn, tt, :], ACT.Square, accum_out=s))
                a.activation(s, s, ACT.Sqrt, bias=c("eps", tn), scale=1.0 / D).then_inc(S["fin_ss"], 1)

        @block.gpsimd
        def _(g):
            g.dma_start(pages[:, :], i["page_table"].rearrange("(o b) n -> o (b n)", o=1)).then_inc(S["ld_pages"], 16)
            st_C, st_n = i["state_C"][0], i["state_n"][0]
            for h in range(H):
                r, j = (h % 2) * DK, h // 2
                g.dma_start(Ce[r:r + DK, j, :, 0:DV], st_C[:, h].rearrange("b k v -> k b v")).then_inc(S["ld_state"], 16)
                g.dma_start(Ce[r:r + DK, j, :, DV], st_n[:, h].rearrange("b k -> k b")).then_inc(S["ld_state"], 16)
            g.wait_ge(S["gates_full"], 1)
            g.dma_start(wg[:, :, 0:E], rows_of(i["w_router"][0], 0, E)).then_inc(S["ld_wr"], 16)
            g.wait_ge(S["st_free"], HP)
            g.dma_start(out[2][0, 0].rearrange("h k v -> k h v"), Cp[:, :, 0:DV]).then_inc(S["stored"], 16)
            g.dma_start(out[3][0, 0].rearrange("h k -> k h"), Cp[:, :, DV]).then_inc(S["stored"], 16)
            g.dma_start(out[4][0].rearrange("a h -> h a"), tiny[:, 16:17]).then_inc(S["stored"], 16)
            g.dma_start(out[9][0].rearrange("b h -> h b"), tiny[:, 17:17 + NB]).then_inc(S["stored"], 16)
            g.wait_ge(S["st_free"], HP + 2 * NB)
            for h in range(H):
                r, j = (h % 2) * DK, h // 2
                g.dma_start(out[7][0][:, h].rearrange("b k v -> k b v"), Ce[r:r + DK, j, :, 0:DV]).then_inc(S["stored"], 16)
                g.dma_start(out[8][0][:, h].rearrange("b k -> k b"), Ce[r:r + DK, j, :, DV]).then_inc(S["stored"], 16)
            g.wait_ge(S["stored"], 16 * STORES_A)
            g.wait_ge(S["ld_pages"], 16)
            g.wait_ge(S["gd_free"], GD_FFN)

            def load_cache(b):
                with g.Fori(0, NPG) as j:
                    page = g.value_load(pages[0:1, bass.ds(j + b * NPG, 1)], min_val=0, max_val=i["cache_ckv"].shape[0] - 1)
                    g.dma_start(ctk[b % 2][:, bass.ds(j, 1), :],
                                i["cache_ckv"][bass.ds(page, 1), :, :].rearrange("g p c -> p g c")).then_inc(ck_full[b % 2], 16)
                    g.dma_start(crk[b % 2][:, bass.ds(j, 1), :],
                                i["cache_krope"][bass.ds(page, 1), :, :].rearrange("g p c -> p g c")).then_inc(ck_full[b % 2], 16)

            load_cache(0)
            load_cache(1)
            g.wait_ge(S["gd_free"], GD_QL)
            for n, (dst_c, dst_r) in enumerate(((out[5][0], out[6][0]), (out[10], out[11]))):
                for dst, a0, a1 in ((dst_c, 0, CKV), (dst_r, CKV, CKV + ROPE)):
                    if n == 0:
                        g.dma_start(dst.rearrange("(t p) c -> p t c", p=P), ctok[:, 0:2, a0:a1]).then_inc(S["kv_stored"], 16)
                    else:
                        g.dma_start(dst.rearrange("b s c -> (b s) c"), ctok[0:TS, 2, a0:a1]).then_inc(S["kv_stored"], 16)
            NU = 2 * H
            for b in range(2, NB):
                g.wait_ge(S["ol_full"], NU + b - 1)
                load_cache(b)
            g.wait_ge(S["ol_full"], NU + NB)
            g.dma_start(gfin, i["g_final"].rearrange("(a n) -> a n", a=1).to_broadcast([P, D])).then_inc(S["ld_gf"], 16)
            g.dma_start(arena[:, 15000:15000 + MCOLS], i["mconst"]).then_inc(S["ld_gf"], 16)
            g.wait_ge(S["kv_stored"], 64)

        @block.sync
        def _(sp):
            sp.dma_start(xtok[:, 0, :], i["x_prompt"][0, 0:P, :]).then_inc(S["ld_x"], 16)
            sp.dma_start(xtok[:, 1, :], i["x_prompt"][0, P:TP, :]).then_inc(S["ld_x"], 16)
            sp.dma_start(xtok[0:TS, 2, :], i["x_sample"].rearrange("b s d -> (b s) d")).then_inc(S["ld_x"], 16)
            sp.dma_start(cs[:, :], i["const"]).then_inc(S["ld_const"], 16)
            for name, rows in GAINS:
                src = i[name][0] if len(i[name].shape) > 1 else i[name]
                if len(src.shape) == 1:
                    src = src.rearrange("(r n) -> r n", n=P)
                sp.dma_start(Dh[0][G0[name]:G0[name] + rows, 0:P], src).then_inc(S["ld_gain"], 16)
            for n, (name, parts) in enumerate(chunks):
                if n >= SLOTS:
                    sp.wait_ge(*release[n - SLOTS])
                for k, w, at, rows, src in parts:
                    dst = ring[0:rows, n % SLOTS, at:at + k * w].rearrange("p (c n) -> p c n", c=k)
                    sp.dma_start(dst, src).then_inc(w_full[n % SLOTS], 16)

            kinds = ("g_full", "u_full", "d_done")

            def expert_chunk(e, k):
                w = i[("w_gate_m", "w_up_m", "w_down_m")[k % 3]][0]
                j, a = k // 3, DC if k % 3 < 2 else KD
                if k % 3 < 2:
                    src = w[bass.ds(e, 1), :, j * CW:(j + 1) * CW].rearrange("e (c p) n -> p (e c) n", p=P)
                else:
                    src = w[bass.ds(e, 1), j * CW:(j + 1) * CW, :].rearrange("e (c p) n -> p (e c) n", p=P)
                s = moe_slot(k)[0]
                sp.dma_start(ring[:, s, :].rearrange("p (c n) -> p c n", c=a), src).then_inc(w_full[s], 16)

            def item_rest(it, e):
                for k in range(SLOTS, PER_ITEM):
                    b = k - SLOTS
                    sp.wait_ge(S[kinds[b % 3]], it * CE + b // 3 + 1)
                    expert_chunk(e, k)

            def item_first(it, e):
                for k in range(SLOTS):
                    b = k + PER_ITEM - SLOTS
                    sp.wait_ge(S[kinds[b % 3]], it * CE + b // 3 + 1)
                    expert_chunk(e, k)

            for k in range(SLOTS):
                sp.wait_ge(*release[NPRE + k - SLOTS])
                expert_chunk(0, k)
            with sp.Fori(0, E - 1) as it:
                item_rest(it, it)
                item_first(it, it + 1)
            item_rest(E - 1, E - 1)
            sp.wait_ge(S["tables_ready"], 1)
            n_items = sp.value_load(ints[0:1, 0:1], min_val=E, max_val=ITEMS)
            with sp.If(n_items > E):
                with sp.Fori(E, n_items) as it:
                    e = sp.value_load(ints[0:1, bass.ds(it - (E - 1), 1)], min_val=0, max_val=E - 1)
                    item_first(it - 1, e)
                    item_rest(it, e)
            for t0, tn, tt in TOK:
                sp.wait_ge(S["fin_ready"], tt + 1)
                dst = out[0][0, t0:t0 + tn, :] if tt < 2 else out[1].rearrange("b s d -> (b s) d")
                sp.dma_start(dst, acc[0:tn, tt, :]).then_inc(S["outs"], 16)
            sp.wait_ge(S["outs"], 48)
            sp.wait_ge(S["stored"], 16 * STORES_A)


GA_FFN = HP + DC
GD_FFN = HP + 6 + 3 + DC
GD_CKV = GD_FFN + FT + DC
GD_CQ = GD_CKV + CT + 1
GD_QL = GD_CQ + QT + HP + 3
GD_MOE = GD_QL + CT * H + H + DC
STORES_A = 4 + 2 * H


def shape_constants():
    import numpy as np

    f = np.float32
    r = np.arange(P)
    t = np.arange(TS)
    parts = {
        "ident": np.eye(P), "ones": np.ones((P, P)), "rot": np.zeros((P, ROPE)), "bsel": np.zeros((P, NB)),
        "eps": np.full((P, 1), EPS), "one": np.ones((P, 1)),
        "pmask": np.where(r[None, :] <= r[:, None], 0.0, NEG),
    }
    x = np.arange((2 * NB - 1) * NS)
    parts["smask"] = np.where((x[None, :] // NS == NB - 1) & (x[None, :] % NS <= r[:, None] % NS), 0.0, NEG)
    half = ROPE // 2
    parts["rot"][half + np.arange(half), np.arange(half)] = -1.0
    parts["rot"][np.arange(half), half + np.arange(half)] = 1.0
    parts["bsel"][t, t // NS] = 1.0
    pos = np.concatenate([np.arange(TP), PAST + t % NS]).astype(f)
    inv = (f(10000.0) ** (-np.arange(half, dtype=f) / f(half))).astype(f)
    ang = (pos[:, None] * inv[None, :]).astype(f)
    for name, fn in (("cos", np.cos), ("sin", np.sin)):
        tab = fn(ang).astype(f).T
        parts[name] = np.concatenate([tab, tab, np.zeros((P - ROPE, T))])
    const = np.concatenate([parts[n] for n, _ in CONSTS], axis=1).astype(f)
    m = {
        "tri": np.where(r[:, None] <= r[None, :], 1.0, 0.0), "iota": np.tile(r, (P, 1)),
        "eidx": np.tile(np.arange(2 * E) // 2, (P, 1)), "kbase": np.tile(P * (1 + np.arange(2 * E) % 2), (P, 1)),
        "valid": np.stack([np.ones(P), np.ones(P), r < TS], axis=1),
    }
    mconst = np.concatenate([m[n] for n, _ in MCONSTS], axis=1).astype(f)
    tri = np.where(r[:, None] <= r[None, :], 0.0, NEG)
    own = np.full((P, TS), NEG)
    own[:TS] = np.where((t[:, None] // NS == t[None, :] // NS) & (t[:, None] <= t[None, :]), 0.0, NEG)
    selp = np.zeros((P, HP, P))
    for j in range(HP):
        selp[2 * j, j, :DK] = 1.0
        selp[2 * j + 1, j, DK:] = 1.0
    aconst = np.concatenate([tri, np.zeros((P, P)), tri, own, selp.reshape(P, -1)], axis=1).astype(f)
    return {"const": const, "mconst": mconst, "aconst": aconst}


_INS = """x_prompt x_sample state_C state_n state_m cache_ckv cache_krope page_table g_norm_a w_in_a b_gate_a g_head_a
    w_out_a g_kv w_dkv g_ckv w_uk w_uv g_norm_b w_dq g_q w_uq w_o_b g_ffn_d w_gate_d w_up_d w_down_d g_ffn_m w_router
    w_gate_m w_up_m w_down_m g_final""".split()
_OUTS = [(1, TP, D), (NB, NS, D), (1, 1, H, DK, DV), (1, 1, H, DK), (1, 1, H), (1, TP, CKV), (1, TP, ROPE),
         (1, NB, H, DK, DV), (1, NB, H, DK), (1, NB, H), (NB, NS, CKV), (NB, NS, ROPE)]


def kernel(**inputs):
    import numpy as np
    import concourse.bacc as bacc
    from concourse.bass_utils import run_bass_kernel_spmd

    nc = bacc.Bacc("TRN2", target_bir_lowering=False, num_devices=1)
    arrays, handles = {}, {}
    named = {**{n: inputs[n] for n in _INS}, **shape_constants()}
    for name, value in named.items():
        array = np.ascontiguousarray(value)
        arrays[f"in_{name}"] = array
        handles[name] = nc.dram_tensor(f"in_{name}", array.shape, mybir.dt.from_np(array.dtype), kind="ExternalInput").ap()
    outs = [nc.dram_tensor(f"out_{n}", shape, F32, kind="ExternalOutput").ap() for n, shape in enumerate(_OUTS)]
    build(nc, handles, outs)
    r = run_bass_kernel_spmd(nc, [arrays], core_ids=[0])
    return tuple(r.results[0][f"out_{n}"] for n in range(len(_OUTS)))
```

```python
from contextlib import ExitStack

import concourse.bass as bass
from concourse import mybir

F32 = mybir.dt.float32
I32 = mybir.dt.int32
U32 = mybir.dt.uint32
F32R = mybir.dt.float32r

P = 128
D = 1024
DC = D // P
TP = 256
NB, NS = 8, 4
TS = NB * NS
T = TP + TS
TOK = [(0, P, 0), (P, P, 1), (TP, TS, 2)]
H = 8
HP = H // 2
DK, DV = 64, 128
CAP = 15.0
NOPE, ROPE = 128, 64
CKV = 256
CT = CKV // P
QL = 384
QT = QL // P
SCALE = (NOPE + ROPE) ** -0.5
PAGE = 128
NPG = 8
PAST = NPG * PAGE
BUFS = 3
FF = 2752
FT = (FF + P - 1) // P
FLAST = FF - (FT - 1) * P
E = 8
FE = 3584
CW = 512
CE = FE // CW
KD = CW // P
SLOTS = 7
SLOTW = DC * CW
ARENA = 18368
HALFW = SLOTW // 2
HALVES = 7
STAGES = 3
ORDER = [("gate", 0), ("up", 0)] + [(kind, j + (kind != "down")) for j in range(CE - 1) for kind in ("gate", "up", "down")]
ORDER += [("down", CE - 1)]
IH = 2 * len(ORDER)
EPS = 1e-6
NEG = -1e30
EXTRA = 4
ITEMS = E + EXTRA

GAINS = [("g_norm_a", DC), ("g_head_a", H), ("g_ffn_d", DC), ("g_kv", DC), ("g_norm_b", DC), ("g_ffn_m", DC),
         ("g_ckv", CT), ("g_q", QT)]
G0, GROWS = {}, 0
for _name, _rows in GAINS:
    G0[_name] = GROWS
    GROWS += _rows

CONSTS = [("ident", P), ("ones", P), ("pmask", P), ("smask", (2 * NB - 1) * NS), ("cos", T), ("sin", T),
          ("rot", ROPE), ("bsel", NB), ("eps", 1), ("one", 1)]
MCONSTS = [("tri", P), ("iota", P), ("eidx", 2 * E), ("kbase", 2 * E), ("valid", 3)]
C0, CCOLS = {}, 0
for _name, _cols in CONSTS:
    C0[_name] = (CCOLS, _cols)
    CCOLS += _cols
M0, MCOLS = {}, 0
for _name, _cols in MCONSTS:
    M0[_name] = (MCOLS, _cols)
    MCOLS += _cols
MAT = 13800
WM = TP + P + TS
ACOLS = WM + HP * P


def build(nc, i, out):
    ALU = mybir.AluOpType
    ACT = mybir.ActivationFunctionType
    AX = mybir.AxisListType

    with ExitStack() as ctx:
        ctx.enter_context(nc.allow_non_contiguous_dma(reason="state vectors and gate biases: a few KiB in all"))

        def sb(name, shape, dt=F32):
            return ctx.enter_context(nc.sbuf_tensor(name, shape, dt))

        def sem(name):
            return ctx.enter_context(nc.semaphore(name))

        with nc.sbuf_tensor("ring", [P, SLOTS, SLOTW], F32) as ring:
            pass
        mring = sb("mring", [P, HALVES, HALFW])
        sb("gap", [P, 4 * SLOTW - HALVES * HALFW])
        wpart = sb("wpart", [P, STAGES, 2, HALFW], F32R)
        xT = sb("xT", [P, DC, T])
        xn = sb("xn", [P, DC, T])
        cs = sb("cs", [P, CCOLS])
        gT = sb("gT", [P, GROWS])
        wg = sb("wg", [P, DC, 2 * H])
        cols = sb("cols", [P, 16])
        tiny = sb("tiny", [H, 32])
        ints = sb("ints", [1, 8], I32)
        pages = sb("pages", [1, NB * NPG], I32)
        with nc.sbuf_tensor("arena", [P, ARENA], F32) as arena:
            pass
        sb("below", [P, ARENA - 2 * D - 4 * CW])
        xgp = sb("xgp", [P, 2, D], F32R)
        hhp = sb("hhp", [P, 2, 2, CW], F32R)
        bank = [ctx.enter_context(nc.psum_tensor(f"bank{n}", [P, 512], F32)) for n in range(5)]
        wide = ctx.enter_context(nc.psum_tensor("wide", [P, 3 * 512], F32))
        bank += [wide[:, 512 * n:512 * (n + 1)] for n in range(3)]

        def c(name, rows=P):
            a, n = C0[name]
            return cs[0:rows, a:a + n]

        def mc(name):
            a, n = M0[name]
            return arena[:, MAT + a:MAT + a + n]

        def gain(name, k):
            return gT[:, G0[name] + k:G0[name] + k + 1]

        def area(at, *dims, rows=P):
            n = 1
            for d in dims:
                n *= d
            v = arena[0:rows, at:at + n]
            if len(dims) == 2:
                return v.rearrange("p (a b) -> p a b", a=dims[0])
            if len(dims) == 3:
                return v.rearrange("p (a b d) -> p a b d", a=dims[0], b=dims[1])
            return v

        ident, ones = c("ident"), c("ones")
        xtok = area(0, 3, D)
        VX = area(0, 3, H, DV + 1)
        qT, kT = area(3096, HP, T), area(4248, HP, T)
        Cp = area(3096, H, DV + 1, rows=DK)
        kmb = [area(4248, H * DK, rows=TS), area(4760, H * DK, rows=TS)]
        oT = area(5400, DC, T)
        Ke = area(7704, 3, H * DK)
        Ce = area(9240, HP, NB, DV + 1)
        ac = area(13368, ACOLS)
        cmask = ac[:, 0:WM]
        selp = ac[0:H, WM:].rearrange("p (j m) -> p j m", j=HP)
        rU, rE, rA, rM, rZ = (area(14296 + T * k, T, rows=H) for k in range(5))
        Dh = [area(15736, WM), area(16152, WM)]
        Wt = area(16568, WM)
        inN, inD = area(16984, H, TS), area(17240, H, TS)
        uT = area(17496, 3, 2 * H)
        eI, eC = area(17544, HP, TS), area(17672, HP * NB)
        xflat = xn[:, :, :].rearrange("p a b -> p (a b)")
        qbd = xflat[:, 0:HP * 288].rearrange("p (j n) -> p j n", j=HP)
        qdiag = xflat[:, 0:HP * 288].rearrange("p (j b s) -> p j b s", j=HP, s=TS + NS)[:, :, 0:NB, 0:NS]
        itok = xflat[0:TS, HP * 288:HP * 288 + H * (DV + 1)].rearrange("p (h n) -> p h n", h=H)
        den = area(17832, T)
        hT = area(0, FT, T)
        sg = [area(6336, T), area(6624, T)]
        hn = area(0, DC, T)
        qlat = area(0, CT, H, TP)
        qls = area(CT * H * TP, CT, NB, H * NS)
        qrope = area(4608, H, TP, rows=ROPE)
        qrs = area(4608 + H * TP, NB, H * NS, rows=ROPE)
        ckvT, krT = area(6912, CT, T), area(7488, T, rows=ROPE)
        ctok = area(7776, 3, CKV + ROPE)
        raw = area(8736, 3, T)
        qn = [area(8736, T), area(9024, T)]
        rtmp = [area(9312, T, rows=ROPE), area(9600, T, rows=ROPE)]
        rt2 = area(9888, T, rows=ROPE)
        prob = area(8736, PAST + TS)
        osb = area(4608, CKV, rows=TS)
        prob2 = [area(8736, TP), area(8736 + TP, TP)]
        PT = area(9792, 384)
        cacheT = area(10176, CT, PAST)
        cacheR = area(12224, PAST, rows=ROPE)
        cq = area(10176, QT, T)
        ukT = area(11040, H, CKV)
        pagebuf = [area(13248, NPG * (CKV + ROPE)), area(13248 + 2560, NPG * (CKV + ROPE)), ring[:, 4, 0:NPG * (CKV + ROPE)]]
        ctk = [buf[:, 0:NPG * CKV].rearrange("p (g c) -> p g c", g=NPG) for buf in pagebuf]
        crk = [buf[:, NPG * CKV:].rearrange("p (g c) -> p g c", g=NPG) for buf in pagebuf]
        acc_sq = area(0, DC, T)

        def stdv(k):
            return den if k == 0 else area(9600 if 2 <= k <= 4 else 6912, T)

        acc = area(0, 3, D)
        xtk = area(3072, 3, D)
        xg = [xgp[:, part, :].rearrange("p (a b) -> p a b", a=DC) for part in range(2)]
        hh = [area(7168, CW), area(7680, CW)]
        ysb = area(9216, D)
        Pm, Pg = area(10240, 3, P), area(10624, 3, P)
        PTg = area(11008, T)
        gfin = area(11296, D)
        sl = [area(12320, CW), area(12832, CW)]
        rt = area(13344, 1600)
        lg, mk, gt, pos = (rt[:, 24 * k:24 * (k + 1)].rearrange("p (a b) -> p a b", a=3) for k in range(4))
        oh1, oh2, top = (rt[:, 96 + 24 * k:120 + 24 * k].rearrange("p (a b) -> p a b", a=3) for k in range(3))
        idf = rt[:, 168:192].rearrange("p (a b) -> p a b", a=3)
        gk = rt[:, 192:198].rearrange("p (a b) -> p a b", a=3)
        cnt = rt[:, 200:208]
        fl, cum, sel, s16 = (rt[:, 208 + 16 * k:224 + 16 * k] for k in range(4))
        posI = rt[:, 272:272 + 3 * 13].rearrange("p (a b) -> p a b", a=3)
        gateI = rt[:, 312:312 + 3 * 13].rearrange("p (a b) -> p a b", a=3)
        nf = rt[:, 352:360]
        p48 = rt[:, 360:408].rearrange("p (a b) -> p a b", a=3)
        idu = sb("idu", [P, 3, 8], U32)

        names = """ld_const ld_x ld_gain ld_tiny ld_wg ld_state ld_ac ld_pages ld_wr ld_gf
            gt_full gt_ready bg_ready x_full x_ready sq_ready ss_full std_ready xn_ready
            ga_full ga_free gd_full gd_free gates_full lf_ready rows_ready uT_full uT_ready e_ready
            qe_ready inter_full inter_tok inter_ready s_full D_made exp_done W_made nd_full em_done h_made kd_made
            st_full st_free hsq_ready hss_full hstd_ready y_ready stored
            ckv_raw ckv_ready kr_ready cq_raw cq_ready ss2_full std2_ready sq2_ready
            uk_ready qn_ready rr_ready qr_ready rot_full ql_ready
            sc_full max_ready p_exp p_ready pt_full pt_ready ol_full ol_ready av_full os_ready tp_full tpa_free tpd_free
            lg_full mask_ready rank_full tables_ready p_made
            hi_ready lo_ready used silu_done hh_hi xg_hi gu_done misc_full m_full xg_ready gk_exp acc_done fin_ss kv_stored misc_free y_full y_free
            dchain achain fin_sq fin_ready outs""".split()
        S = {n: sem(n) for n in names}
        ck_full = [sem(f"ck_full{k}") for k in range(BUFS)]
        cr_full = [sem(f"cr_full{k}") for k in range(BUFS)]
        w_full = [sem(f"w_full{k}") for k in range(SLOTS)]
        half_full = [sem(f"half_full{k}") for k in range(HALVES)]

        w_in, w_out = i["w_in_a"][0], i["w_out_a"][0]
        chunks = []

        def rows_of(w, c0, n):
            return w[:, c0:c0 + n].rearrange("(c p) n -> p c n", p=P)

        def chunk(name, w, c0, n):
            k = w.shape[0] // P
            chunks.append((name, [(k, n, 0, P, rows_of(w, c0, n))]))

        hq, hv = H * DK, H * DV
        chunk("k0", w_in, hq, hq)
        chunk("q0", w_in, 0, hq)
        for n in range(2):
            chunk(f"o{n}", w_in, 2 * hq + hv + n * CW, CW)
        for n in range(2):
            chunk(f"v{n}", w_in, 2 * hq + n * CW, CW)
        for n in range(2):
            chunk(f"out{n}", w_out, n * CW, CW)
        FCH = [(n * CW, min(CW, FF - n * CW)) for n in range((FF + CW - 1) // CW)]
        for n, (a, w) in enumerate(FCH):
            chunk(f"gd{n}", i["w_gate_d"][0], a, w)
            chunk(f"ud{n}", i["w_up_d"][0], a, w)
        wd = i["w_down_d"][0]
        for m in range(DC):
            chunks.append((f"dd{m}", [
                (FT - 1, P, 0, P, wd[0:(FT - 1) * P, m * P:(m + 1) * P].rearrange("(c p) n -> p c n", p=P)),
                (1, P, (FT - 1) * P, FLAST, wd[(FT - 1) * P:FF, m * P:(m + 1) * P].rearrange("(c p) n -> p c n", c=1)),
            ]))
        chunk("dkv", i["w_dkv"], 0, CKV + ROPE)
        chunk("dq", i["w_dq"][0], 0, QL)
        chunk("uk", i["w_uk"].rearrange("c h n -> c (h n)"), 0, H * NOPE)
        for n in range(2):
            chunk(f"uq{n}", i["w_uq"][0], n * HP * (NOPE + ROPE), HP * (NOPE + ROPE))
        chunk("uv", i["w_uv"].rearrange("c h n -> c (h n)"), 0, hv)
        for n in range(2):
            chunk(f"wo{n}", i["w_o_b"][0], n * CW, CW)
        NPRE = len(chunks)
        CH = {name: n for n, (name, _) in enumerate(chunks)}
        arrive, slot_sum = [], [0] * SLOTS
        for n, (_, parts) in enumerate(chunks):
            slot_sum[n % SLOTS] += 16 * len(parts)
            arrive.append(slot_sum[n % SLOTS])
        release = {}

        def wview(name, k, n):
            s = CH[name] % SLOTS
            return ring[:, s, 0:k * n].rearrange("p (c n) -> p c n", c=k)

        SHARED = 1 + CE + 2 + 6

        def place(h):
            return (h + 2) % HALVES

        def loaded(it, h):
            return (half_full[place(h % IH)], it * (16 * IH // HALVES) + 16 * (h // HALVES + 1))

        def stage(h):
            return h % STAGES

        def turn_at(j):
            return 2 * ORDER.index(("gate", j + 1)) + 1 if j < CE - 1 else 2 * ORDER.index(("down", j - 1)) + 1

        def after(kind, j):
            return STAGES + 2 * (ORDER.index((kind, j)) + 1)

        block = ctx.enter_context(nc.Block())

        @block.tensor
        def _(pe):
            n_ga, n_gd = [0], [0]

            def arrived(name):
                pe.wait_ge(w_full[CH[name] % SLOTS], arrive[CH[name]])

            def out_a():
                if n_ga[0] >= 2:
                    pe.wait_ge(S["ga_free"], n_ga[0] - 1)
                n_ga[0] += 1
                return bank[(n_ga[0] - 1) % 2]

            def out_d():
                if n_gd[0] >= 2:
                    pe.wait_ge(S["gd_free"], n_gd[0] - 1)
                n_gd[0] += 1
                return bank[2 + (n_gd[0] - 1) % 2]

            def done_a(ins, last_of=None):
                ins.then_inc(S["ga_full"], 1)
                if last_of:
                    release[CH[last_of]] = (S["ga_full"], n_ga[0])

            def done_d(ins, last_of=None):
                ins.then_inc(S["gd_full"], 1)
                if last_of:
                    release[CH[last_of]] = (S["gd_full"], n_gd[0])

            def product(o, pairs):
                for n, (w, x) in enumerate(pairs):
                    ins = pe.matmul(o, w, x, start=(n == 0), stop=(n == len(pairs) - 1))
                return ins

            def sum_squares(k, chunks_, sq, first):
                if k:
                    pe.wait_ge(S["std_ready"], k)
                for m in range(chunks_):
                    pe.wait_ge(S["sq_ready"], first + m + 1)
                    ins = pe.matmul(bank[7][:, 0:T], ones, sq[:, m, :], start=(m == 0), stop=(m == chunks_ - 1))
                ins.then_inc(S["ss_full"], 1)

            pe.wait_ge(S["ld_const"], 16)
            pe.wait_ge(S["ld_gain"], 16 * len(GAINS))
            pe.transpose(bank[4][:, 0:GROWS], Dh[0][0:GROWS, 0:P], ident[0:GROWS, 0:GROWS]).then_inc(S["gt_full"], 1)
            pe.wait_ge(S["ld_x"], 48)
            for m in range(DC):
                if m >= 2:
                    pe.wait_ge(S["x_ready"], m - 1)
                for t0, tn, tt in TOK:
                    ins = pe.transpose(bank[m % 2][:, t0:t0 + tn], xtok[0:tn, tt, m * P:(m + 1) * P],
                                       ident[0:tn, 0:tn])
                ins.then_inc(S["x_full"], 1)
            sum_squares(0, DC, xn, 0)

            pe.wait_ge(S["x_ready"], DC)
            arrived("k0")
            w = wview("k0", DC, CW)
            for m in range(HP):
                o = out_d()
                for k in range(DC):
                    if m == 0:
                        pe.wait_ge(S["xn_ready"], k + 1)
                    ins = pe.matmul(o[:, 0:T], w[:, k, m * P:(m + 1) * P], xn[:, k, :], start=(k == 0), stop=(k == DC - 1))
                done_d(ins, "k0" if m == HP - 1 else None)
            pe.wait_ge(S["ld_wg"], 16)
            pe.wait_ge(S["gt_ready"], 1)
            product(bank[4][0:H, 0:T], [(wg[:, k, 0:H], xn[:, k, :]) for k in range(DC)])
            product(bank[5][0:H, 0:T], [(wg[:, k, H:2 * H], xn[:, k, :]) for k in range(DC)]).then_inc(S["gates_full"], 1)
            arrived("q0")
            w = wview("q0", DC, CW)
            for m in range(HP):
                o = out_a()
                ins = product(o[:, 0:T], [(w[:, k, m * P:(m + 1) * P], xn[:, k, :]) for k in range(DC)])
                done_a(ins, "q0" if m == HP - 1 else None)
            for m in range(DC):
                name = f"o{m // 4}"
                arrived(name)
                w = wview(name, DC, CW)
                o = out_a()
                ins = product(o[:, 0:T], [(w[:, k, (m % 4) * P:(m % 4 + 1) * P], xn[:, k, :]) for k in range(DC)])
                done_a(ins, name if m % 4 == 3 else None)
            for n in range(2):
                name = f"v{n}"
                arrived(name)
                w = wview(name, DC, CW)
                for t0, tn, tt in TOK:
                    o = out_d()
                    ins = product(o[0:tn, :], [(xn[:, k, t0:t0 + tn], w[:, k, :]) for k in range(DC)])
                    done_d(ins, name if tt == 2 else None)

            pe.wait_ge(S["rows_ready"], 1)
            pe.wait_ge(S["ld_ac"], 16)
            for t0, tn, tt in TOK:
                pe.transpose(bank[4][0:tn, tt * 16:tt * 16 + H], rU[:, t0:t0 + tn], ident[0:H, 0:H])
                pe.transpose(bank[4][0:tn, tt * 16 + H:tt * 16 + 2 * H], rE[:, t0:t0 + tn], ident[0:H, 0:H])
            for j in range(HP):
                pe.matmul(bank[5][:, j * TS:(j + 1) * TS], selp[:, j, :], rZ[:, 0:TS], start=True, stop=True)
                ins = pe.matmul(bank[5][:, HP * TS + j * NB:HP * TS + (j + 1) * NB], selp[:, j, :],
                                rZ[:, TS:TS + NB], start=True, stop=True)
            ins.then_inc(S["uT_full"], 1)

            for t0, tn, tt in TOK:
                o = out_d()
                for j in range(HP):
                    ins = pe.transpose(o[0:tn, j * P:(j + 1) * P], kT[:, j, t0:t0 + tn], ident)
                done_d(ins)

            pe.wait_ge(S["ld_state"], 16 * 16)
            pe.wait_ge(S["qe_ready"], 1)
            pe.wait_ge(S["ga_free"], n_ga[0])
            for h in range(H):
                r, g = (h % 2) * DK, h // 2
                o = bank[(6, 0)[h % 2] + g // 3][0:TS, (g % 3) * (DV + 1):(g % 3 + 1) * (DV + 1)]
                for b in range(NB):
                    ins = pe.matmul(o, qbd[r:r + DK, g, b * TS:(b + 1) * TS], Ce[r:r + DK, g, b, :],
                                    start=(b == 0), stop=(b == NB - 1))
            ins.then_inc(S["inter_full"], 1)
            pe.wait_ge(S["inter_tok"], 1)
            for h in range(H):
                pe.transpose(bank[6][:, h * TS:(h + 1) * TS], itok[:, h, 0:DV], ident[0:TS, 0:TS])
                ins = pe.transpose(bank[7][:, h * TS:(h + 1) * TS], itok[:, h, DV:DV + 1].to_broadcast([TS, P]),
                                   ident[0:TS, 0:TS])
            ins.then_inc(S["inter_full"], 1)

            pe.wait_ge(S["gd_free"], n_gd[0])
            pe.wait_ge(S["e_ready"], 1)
            pe.wait_ge(S["inter_ready"], 1)

            def scores(h):
                if h >= 2:
                    pe.wait_ge(S["D_made"], h - 1)
                    pe.wait_ge(S["W_made"], h - 1)
                r = (h % 2) * DK
                kk, qq = kT[r:r + DK, h // 2, :], qT[r:r + DK, h // 2, :]
                s = bank[2 + h % 2]
                pe.matmul(bank[h % 2][:, 0:T], ident[0:H, h:h + 1].to_broadcast([H, P]), rM, start=True, stop=True)
                pe.matmul(s[:, 0:TP], kk[:, 0:P], qq[:, 0:TP], start=True, stop=True)
                pe.matmul(s[:, TP:TP + P], kk[:, P:TP], qq[:, P:TP], start=True, stop=True)
                pe.matmul(s[0:TS, TP + P:WM], kk[:, TP:T], qq[:, TP:T], start=True, stop=True).then_inc(S["s_full"], 1)

            def attend(h):
                if h:
                    pe.wait_ge(S["h_made"], h)
                pe.matmul(bank[4][:, 0:T], ident[0:H, h:h + 1].to_broadcast([H, P]), rA, start=True,
                          stop=True).then_inc(S["m_full"], 1)
                pe.wait_ge(S["W_made"], h + 1)
                for o, v0, v1, v2 in ((bank[5], VX[:, 0, h, 0:DV], VX[:, 1, h, 0:DV], VX[0:TS, 2, h, 0:DV]),
                                      (bank[6], ones, ones, ones[0:TS, :])):
                    pe.matmul(o[:, TP:T], v2, Wt[0:TS, TP + P:WM], start=True, stop=True)
                    pe.matmul(o[:, 0:TP], v0, Wt[:, 0:TP], start=True, stop=False)
                    ins = pe.matmul(o[:, P:TP], v1, Wt[:, TP:TP + P], start=False, stop=True)
                ins.then_inc(S["nd_full"], 1)

            scores(0)
            for h in range(H):
                if h + 1 < H:
                    scores(h + 1)
                attend(h)

            pe.wait_ge(S["h_made"], H)
            n_st = 0
            for g in range(HP):
                if n_st >= 4:
                    pe.wait_ge(S["st_free"], n_st - 3)
                o = bank[n_st % 4]
                for hh_ in range(2):
                    h = 2 * g + hh_
                    for s in range(2):
                        ins = pe.matmul(o[0:DK, hh_ * 129:hh_ * 129 + 129], Ke[:, s, h * DK:(h + 1) * DK],
                                        VX[:, s, h, :], start=(s == 0), stop=(s == 1))
                ins.then_inc(S["st_full"], 1)
                n_st += 1
            for b in range(NB):
                pe.wait_ge(S["kd_made"], b + 1)
                for g in range(2):
                    if n_st >= 4:
                        pe.wait_ge(S["st_free"], n_st - 3)
                    o = bank[n_st % 4]
                    for jj in range(2):
                        for par in range(2):
                            h = 2 * (2 * g + jj) + par
                            ins = pe.matmul(o[par * DK:(par + 1) * DK, jj * 129:jj * 129 + 129],
                                            kmb[b % 2][:, h * DK:(h + 1) * DK], VX[0:TS, 2, h, :], start=True, stop=True)
                    ins.then_inc(S["st_full"], 1)
                    n_st += 1

            for h in range(H):
                pe.wait_ge(S["hsq_ready"], h + 1)
                if h >= 2:
                    pe.wait_ge(S["y_ready"], h - 1)
                pe.matmul(bank[4 + h % 2][:, 0:T], ones, Dh[h % 2][:, 0:T], start=True, stop=True).then_inc(S["hss_full"], 1)
            pe.wait_ge(S["st_free"], n_st)
            for m in range(DC):
                name = f"out{m // 4}"
                arrived(name)
                w = wview(name, DC, CW)
                o = out_d()
                for k in range(DC):
                    if m == 0:
                        pe.wait_ge(S["y_ready"], k + 1)
                    ins = pe.matmul(o[:, 0:T], w[:, k, (m % 4) * P:(m % 4 + 1) * P], oT[:, k, :], start=(k == 0), stop=(k == DC - 1))
                done_d(ins, name if m % 4 == 3 else None)

            sum_squares(1, DC, xn, DC)
            pe.wait_ge(S["xn_ready"], 2 * DC)
            for f in range(FT):
                n, q = f // 4, f % 4
                rows = P if f < FT - 1 else FLAST
                arrived(f"gd{n}")
                arrived(f"ud{n}")
                wide_ = FCH[n][1]
                last = q == 3 or f == FT - 1
                w = wview(f"gd{n}", DC, wide_)
                o = out_a()
                ins = product(o[0:rows, 0:T], [(w[:, k, q * P:q * P + rows], xn[:, k, :]) for k in range(DC)])
                done_a(ins, f"gd{n}" if last else None)
                w = wview(f"ud{n}", DC, wide_)
                o = out_d()
                ins = product(o[0:rows, 0:T], [(w[:, k, q * P:q * P + rows], xn[:, k, :]) for k in range(DC)])
                done_d(ins, f"ud{n}" if last else None)
            up_done = n_gd[0]
            for m in range(DC):
                arrived(f"dd{m}")
                w = wview(f"dd{m}", FT, P)
                o = out_d()
                if m == 0:
                    pe.wait_ge(S["gd_free"], up_done)
                for k in range(FT):
                    rows = P if k < FT - 1 else FLAST
                    ins = pe.matmul(o[:, 0:T], w[0:rows, k, :], hT[0:rows, k, :], start=(k == 0), stop=(k == FT - 1))
                done_d(ins, f"dd{m}")

            sum_squares(2, DC, xn, 2 * DC)
            arrived("dkv")
            w = wview("dkv", DC, CKV + ROPE)
            pe.wait_ge(S["xn_ready"], 3 * DC)
            for m in range(CT + 1):
                rows = P if m < CT else ROPE
                o = out_d()
                ins = product(o[0:rows, 0:T], [(w[:, k, m * P:m * P + rows], hn[:, k, :]) for k in range(DC)])
                done_d(ins, "dkv" if m == CT else None)
            pe.wait_ge(S["xn_ready"], 4 * DC)
            arrived("dq")
            w = wview("dq", DC, QL)
            pe.wait_ge(S["gd_free"], GD_CQ)
            pe.matmul(bank[4][0:ROPE, 0:T], c("rot", ROPE), rtmp[0], start=True, stop=True).then_inc(S["rot_full"], 1)
            sum_squares(3, CT, ckvT, 3 * DC)
            pe.wait_ge(S["ckv_ready"], 1)
            for m in range(QT):
                o = out_d()
                ins = product(o[:, 0:T], [(w[:, k, m * P:(m + 1) * P], xn[:, k, :]) for k in range(DC)])
                done_d(ins, "dq" if m == QT - 1 else None)
            arrived("uk")
            w = wview("uk", CT, H * NOPE)
            for g in range(HP):
                o = out_d()
                for hh_ in range(2):
                    for k in range(CT):
                        h = 2 * g + hh_
                        ins = pe.transpose(o[:, (hh_ * CT + k) * P:(hh_ * CT + k + 1) * P],
                                           w[:, k, h * NOPE:(h + 1) * NOPE], ident)
                done_d(ins, "uk" if g == HP - 1 else None)
            sum_squares(4, QT, cq, 3 * DC + CT)
            for t0, tn, tt in TOK:
                o = out_d()
                for k in range(CT):
                    pe.transpose(o[0:tn, k * P:(k + 1) * P], ckvT[:, k, t0:t0 + tn], ident)
                ins = pe.transpose(o[0:tn, CKV:CKV + ROPE], krT[:, t0:t0 + tn], ident[0:ROPE, 0:ROPE])
                done_d(ins)
            pe.wait_ge(S["cq_ready"], 1)
            pe.wait_ge(S["kr_ready"], 1)

            def up_q(h):
                name = f"uq{h // HP}"
                arrived(name)
                w = wview(name, QT, HP * (NOPE + ROPE))
                a = (h % HP) * (NOPE + ROPE)
                o = out_a()
                done_a(product(o[:, 0:T], [(w[:, k, a:a + NOPE], cq[:, k, :]) for k in range(QT)]))
                o = out_a()
                ins = product(o[0:ROPE, 0:T], [(w[:, k, a + NOPE:a + NOPE + ROPE], cq[:, k, :]) for k in range(QT)])
                done_a(ins, name if h % HP == HP - 1 else None)

            def latent_q(h):
                pe.wait_ge(S["ga_free"], ga_q + 2 * (h + 1))
                if h:
                    pe.wait_ge(S["qr_ready"], h)
                pe.matmul(bank[4][0:ROPE, 0:T], c("rot", ROPE), rtmp[h % 2], start=True, stop=True).then_inc(S["rot_full"], 1)
                for k in range(CT):
                    o = out_d()
                    done_d(pe.matmul(o[:, 0:T], ukT[:, h, k * P:(k + 1) * P], qn[h % 2], start=True, stop=True))

            ga_q = n_ga[0]
            up_q(0)
            for h in range(H):
                if h + 1 < H:
                    up_q(h + 1)
                latent_q(h)
            pe.wait_ge(S["qr_ready"], H)
            pe.wait_ge(S["gd_free"], n_gd[0])

            units = [(h, q) for h in range(H) for q in range(2)]

            def p_scores(u):
                h, q = units[u]
                if u >= 2:
                    pe.wait_ge(S["p_exp"], u - 1)
                keys = (q + 1) * P
                o = bank[5 + u % 2][:, 0:keys]
                for k in range(CT):
                    pe.matmul(o, qlat[:, k, h, q * P:(q + 1) * P], ckvT[:, k, 0:keys], start=(k == 0), stop=False)
                pe.matmul(o, qrope[:, h, q * P:(q + 1) * P], krT[:, 0:keys], start=False, stop=True).then_inc(S["sc_full"], 1)

            def p_attend(u):
                h, q = units[u]
                pe.wait_ge(S["p_ready"], u + 1)
                for s in range(q + 1):
                    ins = pe.transpose(bank[7][:, s * P:(s + 1) * P], prob2[u % 2][:, s * P:(s + 1) * P], ident)
                ins.then_inc(S["pt_full"], 1)
                if u + 2 < len(units):
                    p_scores(u + 2)
                pe.wait_ge(S["pt_ready"], u + 1)
                if u:
                    pe.wait_ge(S["ol_ready"], u)
                for k in range(CT):
                    for s in range(q + 1):
                        ins = pe.matmul(bank[4][:, k * P:(k + 1) * P], ctok[:, s, k * P:(k + 1) * P],
                                        PT[:, s * P:(s + 1) * P], start=(s == 0), stop=(s == q))
                ins.then_inc(S["ol_full"], 1)

            p_scores(0)
            p_scores(1)
            for u in range(len(units)):
                p_attend(u)

            NU = len(units)

            def cache_transposes(b):
                pe.wait_ge(ck_full[b % BUFS], 16 * NPG * (b // BUFS + 1))
                for g in range(6):
                    n = 6 * b + g
                    if g == 2 * CT:
                        pe.wait_ge(cr_full[b % BUFS], 16 * NPG * (b // BUFS + 1))
                    if n >= 2:
                        pe.wait_ge(S["tpa_free"] if n % 2 == 0 else S["tpd_free"], n // 2)
                    part, half = g // 2, g % 2
                    for pg in range(4):
                        page = half * 4 + pg
                        src = ctk[b % BUFS][:, page, part * P:(part + 1) * P] if part < CT else crk[b % BUFS][:, page, :]
                        rows = P if part < CT else ROPE
                        ins = pe.transpose(bank[n % 2][0:rows, pg * P:(pg + 1) * P], src, ident)
                    ins.then_inc(S["tp_full"], 1)

            def s_scores(b):
                pe.wait_ge(S["tpa_free"], 3 * (b + 1))
                pe.wait_ge(S["tpd_free"], 3 * (b + 1))
                pe.wait_ge(S["p_exp"], NU + b)
                if b == 0:
                    pe.wait_ge(S["pt_ready"], NU)
                for a, n, kv, kr in ((0, 512, cacheT[:, :, 0:512], cacheR[:, 0:512]),
                                     (512, 512, cacheT[:, :, 512:PAST], cacheR[:, 512:PAST]),
                                     (PAST, TS, ckvT[:, :, TP:T], krT[:, TP:T])):
                    for k in range(CT):
                        pe.matmul(wide[0:TS, a:a + n], qls[:, k, b, :], kv[:, k, :], start=(k == 0), stop=False)
                    ins = pe.matmul(wide[0:TS, a:a + n], qrs[:, b, :], kr, start=False, stop=True)
                ins.then_inc(S["sc_full"], 1)

            def s_attend(b):
                pe.wait_ge(S["p_exp"], NU + b + 1)
                for pg in range(NPG + 1):
                    rows = P if pg < NPG else TS
                    ins = pe.transpose(bank[4][0:rows, pg * TS:(pg + 1) * TS], prob[0:TS, pg * P:pg * P + rows],
                                       ident[0:TS, 0:TS])
                ins.then_inc(S["pt_full"], 1)
                pe.wait_ge(S["pt_ready"], NU + b + 1)
                if b:
                    pe.wait_ge(S["os_ready"], b)
                for pg in range(NPG + 1):
                    kv = ctk[b % BUFS][:, pg, :] if pg < NPG else ctok[0:TS, 2, 0:CKV]
                    rows = P if pg < NPG else TS
                    ins = pe.matmul(bank[3][0:TS, 0:CKV], PT[0:rows, pg * TS:(pg + 1) * TS], kv,
                                    start=(pg == 0), stop=(pg == NPG))
                ins.then_inc(S["av_full"], 1)

            def s_turn(b):
                pe.wait_ge(S["os_ready"], b + 1)
                if b:
                    pe.wait_ge(S["ol_ready"], NU + b)
                for k in range(CT):
                    ins = pe.transpose(bank[2][:, k * TS:(k + 1) * TS], osb[:, k * P:(k + 1) * P], ident[0:TS, 0:TS])
                ins.then_inc(S["ol_full"], 1)

            pe.wait_ge(S["ol_ready"], NU)
            cache_transposes(0)
            for b in range(NB):
                s_scores(b)
                if b:
                    s_turn(b - 1)
                if b + 1 < NB:
                    cache_transposes(b + 1)
                s_attend(b)
            s_turn(NB - 1)
            pe.wait_ge(S["ol_ready"], NU + NB)
            pe.wait_ge(S["tpa_free"], 3 * NB)
            arrived("uv")
            w = wview("uv", CT, hv)
            for h in range(H):
                o = out_d()
                product(o[:, TP:T].rearrange("p (b s) -> p b s", s=NS),
                        [(w[:, k, h * DV:(h + 1) * DV], qls[:, k, :, h * NS:(h + 1) * NS]) for k in range(CT)])
                ins = product(o[:, 0:TP], [(w[:, k, h * DV:(h + 1) * DV], qlat[:, k, h, :]) for k in range(CT)])
                done_d(ins, "uv" if h == H - 1 else None)
            heads_out = n_gd[0]
            for m in range(DC):
                name = f"wo{m // 4}"
                arrived(name)
                w = wview(name, DC, CW)
                o = out_d()
                for k in range(DC):
                    if m == 0:
                        pe.wait_ge(S["gd_free"], heads_out - DC + k + 1)
                    ins = pe.matmul(o[:, 0:T], w[:, k, (m % 4) * P:(m % 4 + 1) * P], xn[:, k, :], start=(k == 0), stop=(k == DC - 1))
                done_d(ins, name if m % 4 == 3 else None)

            sum_squares(5, DC, acc_sq, 3 * DC + CT + QT)
            pe.wait_ge(S["xn_ready"], 5 * DC)
            pe.wait_ge(S["ld_wr"], 16)
            for t0, tn, tt in TOK:
                ins = product(bank[4][0:tn, tt * E:(tt + 1) * E], [(xn[:, k, t0:t0 + tn], wg[:, k, 0:E]) for k in range(DC)])
            ins.then_inc(S["lg_full"], 1)
            for src in (xn, xT):
                for t0, tn, tt in TOK:
                    for half in range(2):
                        o = out_d()
                        for q in range(4):
                            ins = pe.transpose(o[0:tn, q * P:(q + 1) * P], src[:, half * 4 + q, t0:t0 + tn], ident)
                        done_d(ins)
            pe.wait_ge(S["gd_free"], n_gd[0])
            pe.wait_ge(S["mask_ready"], 1)
            pe.wait_ge(S["ld_gf"], 32)
            tri = mc("tri")
            for t0, tn, tt in TOK:
                ins = product(bank[4][:, 32 + tt * E:32 + (tt + 1) * E],
                              [(ones, mk[:, s, :]) for s in range(tt)] + [(tri, mk[:, tt, :])])
            ins = product(bank[4][:, 64:64 + E], [(ones, mk[:, s, :]) for s in range(3)])
            ins.then_inc(S["rank_full"], 1)

            def gather(half):
                for q in range(4):
                    m = half * 4 + q
                    for t0, tn, tt in TOK:
                        ins = pe.matmul(bank[6 + half][:, q * P:(q + 1) * P], xtk[0:tn, tt, m * P:(m + 1) * P],
                                        Pm[0:tn, tt, :], start=(tt == 0), stop=(tt == 2))
                ins.then_inc(S["misc_full"], 1)

            pe.wait_ge(S["p_made"], 1)
            gather(0)
            gather(1)
            pe.wait_ge(S["tables_ready"], 1)
            n_items = pe.value_load(ints[0:1, 0:1], min_val=E, max_val=ITEMS)
            with pe.Fori(0, n_items) as it:
                def parts(h, a):
                    pe.wait_ge(S["lo_ready"], it * IH + h + 1)
                    return [wpart[:, stage(h), part, :].rearrange("p (c n) -> p c n", c=a) for part in range(2)]

                def split_product(o, x, w, start, stop):
                    pe.matmul(o, x[0], w[0], start=start, stop=False)
                    pe.matmul(o, x[1], w[0], start=False, stop=False)
                    return pe.matmul(o, x[0], w[1], start=False, stop=stop)

                def free(use):
                    if use == 11:
                        pe.wait_ge(S["xg_ready"], it + 2)
                    else:
                        pe.wait_ge(S["misc_free"], it * (SHARED - 1) + (max(1, use) if use <= 10 else use - 1))

                def rows(kind, j, o):
                    for half in range(2):
                        w = parts(2 * ORDER.index((kind, j)) + half, DC // 2)
                        for q in range(DC // 2):
                            m = half * DC // 2 + q
                            ins = split_product(o, [x[:, m, :] for x in xg], [p[:, q, :] for p in w], m == 0, m == DC - 1)
                        ins.then_inc(S["used"], 1)

                def gate(j):
                    pe.wait_ge(S["gu_done"], it * CE + 1 + max(0, j - 1))
                    rows("gate", j, bank[j % 2][:, :])

                def up(j):
                    rows("up", j, bank[2 + j % 2][:, :])

                def turn(j):
                    pe.wait_ge(S["gu_done"], it * CE + 1 + j + 1)
                    free(1 + j)
                    for q in range(KD):
                        ins = pe.transpose(bank[6 + (1 + j) % 2][:, q * P:(q + 1) * P], hh[j % 2][:, q * P:(q + 1) * P], ident)
                    ins.then_inc(S["misc_full"], 1)

                def down(j):
                    pe.wait_ge(S["misc_free"], it * (SHARED - 1) + j + 3)
                    if j == 0:
                        pe.wait_ge(S["y_free"], it + 1)
                    for half in range(2):
                        w = parts(2 * ORDER.index(("down", j)) + half, KD // 2)
                        for q in range(KD // 2):
                            m = half * KD // 2 + q
                            for n in range(2):
                                ins = split_product(bank[4 + n][:, :],
                                                    [hhp[:, j % 2, part, m * P:(m + 1) * P] for part in range(2)],
                                                    [p[:, q, n * CW:(n + 1) * CW] for p in w],
                                                    j == 0 and m == 0, j == CE - 1 and m == KD - 1)
                        ins.then_inc(S["used"], 1)

                pe.wait_ge(S["xg_ready"], it + 1)
                gate(0)
                up(0)
                free(0)
                for t0, tn, tt in TOK:
                    ins = pe.transpose(bank[6][:, t0:t0 + tn], Pg[0:tn, tt, :], ident[0:tn, 0:tn])
                ins.then_inc(S["misc_full"], 1)
                for j in range(CE - 1):
                    gate(j + 1)
                    turn(j)
                    up(j + 1)
                    down(j)
                turn(CE - 1)
                pe.wait_ge(S["p_made"], it + 2)
                free(1 + CE)
                gather(0)
                down(CE - 1)
                free(2 + CE)
                gather(1)
                pe.wait_ge(S["y_free"], it + 2)
                for u, (t0, tn, tt) in enumerate(TOK):
                    for half in range(2):
                        n = 1 + CE + 2 + 2 * u + half
                        free(n)
                        pe.matmul(bank[6 + n % 2][0:tn, :], PTg[:, t0:t0 + tn], ysb[:, half * CW:(half + 1) * CW],
                                  start=True, stop=True).then_inc(S["misc_full"], 1)

        @block.vector
        def _(v):
            chain = [0]

            def link(ins):
                chain[0] += 1
                ins.then_inc(S["dchain"], 1)
                v.wait_ge(S["dchain"], chain[0])

            n_gd = [0]

            def in_d():
                n_gd[0] += 1
                v.wait_ge(S["gd_full"], n_gd[0])
                return bank[2 + (n_gd[0] - 1) % 2]

            def free_d(ins):
                ins.then_inc(S["gd_free"], 1)

            def normalise(k, chunks_, src, gname, dst, ready, first=True, every=True):
                if first:
                    v.wait_ge(S["std_ready"], k + 1)
                    link(v.reciprocal(stdv(k), stdv(k)))
                for m in range(chunks_):
                    ins = v.scalar_tensor_tensor(out=dst[:, m, :], in0=src[:, m, :], scalar=gain(gname, m),
                                                 in1=stdv(k), op0=ALU.mult, op1=ALU.mult)
                    if every or m == chunks_ - 1:
                        ins.then_inc(S[ready], 1)

            v.wait_ge(S["gt_full"], 1)
            v.tensor_copy(gT[:, :], bank[4][:, 0:GROWS]).then_inc(S["gt_ready"], 1)
            v.wait_ge(S["ld_tiny"], 32)
            v.tensor_scalar(tiny[:, 2:4], tiny[:, 0:2], 1.0 / CAP, None, ALU.mult).then_inc(S["bg_ready"], 1)
            for m in range(DC):
                v.wait_ge(S["x_full"], m + 1)
                v.tensor_copy(xT[:, m, :], bank[m % 2][:, 0:T]).then_inc(S["x_ready"], 1)
            v.wait_ge(S["gt_ready"], 1)
            normalise(0, DC, xT, "g_norm_a", xn, "xn_ready")
            link(v.memset(VX[:, :, :, DV:DV + 1], 1.0))
            link(v.memset(uT[:, :, :], 0.0))
            link(v.memset(rZ[:, :], 0.0))
            for m in range(HP):
                o = in_d()
                free_d(v.tensor_copy(kT[:, m, :], o[:, 0:T]))

            v.wait_ge(S["lf_ready"], 1)
            m0 = tiny[:, 8:16]
            link(v.tensor_scalar(rU, rU, CAP, None, ALU.mult))
            link(v.tensor_scalar(rE, rE, -1.0, None, ALU.mult))
            link(v.tensor_tensor_scan(rA[:, 0:TP], rE[:, 0:TP], rZ[:, 0:TP], 0.0, ALU.add, ALU.add))

            def step(row, t):
                return row[:, TP:T].rearrange("p (b s) -> p b s", s=NS)[:, :, t]

            link(v.tensor_copy(step(rA, 0), step(rE, 0)))
            for t in range(1, NS):
                link(v.tensor_tensor(step(rA, t), step(rA, t - 1), step(rE, t), ALU.add))
            link(v.tensor_tensor(rU, rU, rA, ALU.subtract))
            link(v.tensor_tensor_scan(rM[:, 0:TP], rU[:, 0:TP], rU[:, 0:TP], 0.0, ALU.max, ALU.max))
            link(v.tensor_tensor(step(rM, 0), m0, step(rU, 0), ALU.max))
            for t in range(1, NS):
                link(v.tensor_tensor(step(rM, t), step(rM, t - 1), step(rU, t), ALU.max))
            link(v.tensor_scalar(rE[:, 0:TP], rU[:, 0:TP], rM[:, TP - 1:TP], None, ALU.subtract))
            for t in range(NS):
                link(v.tensor_tensor(step(rE, t), step(rU, t), step(rM, NS - 1), ALU.subtract))
            zt = rZ[:, 0:TS].rearrange("p (b s) -> p b s", s=NS)
            for t in range(NS):
                link(v.tensor_tensor(zt[:, :, t], m0, step(rM, t), ALU.subtract))
            link(v.tensor_tensor(rZ[:, TS:TS + NB], m0, step(rM, NS - 1), ALU.subtract))
            link(v.tensor_tensor(rA, rA, rM, ALU.add))
            link(v.tensor_copy(tiny[:, 16:17], rA[:, TP - 1:TP]))
            link(v.tensor_copy(tiny[:, 17:17 + NB], step(rA, NS - 1)))
            link(v.tensor_scalar(rA, rA, -1.0, None, ALU.mult))
            v.tensor_scalar(rM, rM, -1.0, None, ALU.mult).then_inc(S["rows_ready"], 1)

            for n in range(2):
                for t0, tn, tt in TOK:
                    o = in_d()
                    free_d(v.tensor_copy(VX[0:tn, tt, 4 * n:4 * n + 4, 0:DV],
                                         o[0:tn, :].rearrange("p (h n) -> p h n", h=4)))
            v.wait_ge(S["uT_full"], 1)
            v.tensor_copy(uT[:, 0:2, :], bank[4][:, 0:32].rearrange("p (a b) -> p a b", a=2)).then_inc(S["uT_ready"], 1)
            v.tensor_copy(uT[0:TS, 2, :], bank[4][0:TS, 32:48]).then_inc(S["uT_ready"], 1)
            v.wait_ge(S["e_ready"], 1)
            v.wait_ge(S["ga_free"], HP)
            link(v.memset(xflat[:, 0:HP * 288], 0.0))
            v.tensor_tensor(qdiag, qT[:, :, TP:T].rearrange("p j (b s) -> p j b s", s=NS),
                            eI[:, :, :].rearrange("p j (b s) -> p j b s", s=NS), ALU.mult).then_inc(S["qe_ready"], 1)
            for t0, tn, tt in TOK:
                o = in_d()
                free_d(v.tensor_tensor(Ke[0:tn, tt, :].rearrange("p (h k) -> p h k", h=H),
                                       o[0:tn, :].rearrange("p (h k) -> p h k", h=H),
                                       uT[0:tn, tt, H:2 * H].unsqueeze(2).to_broadcast([tn, H, DK]), ALU.mult))
            v.wait_ge(S["inter_full"], 1)
            for par in range(2):
                for g0, g1 in ((0, 3), (3, HP)):
                    ins = v.tensor_copy(itok.rearrange("p (g a) n -> p g a n", a=2)[:, g0:g1, par, :],
                                        bank[(6, 0)[par] + g0 // 3][0:TS, 0:(g1 - g0) * (DV + 1)].rearrange(
                                            "p (g n) -> p g n", n=DV + 1))
            ins.then_inc(S["inter_tok"], 1)
            v.wait_ge(S["inter_full"], 2)
            v.tensor_copy(inN.rearrange("p a b -> p (a b)"), bank[6][:, 0:H * TS])
            link(v.tensor_copy(inD.rearrange("p a b -> p (a b)"), bank[7][:, 0:H * TS]))
            v.memset(den[:, 0:1], 0.0).then_inc(S["inter_ready"], 1)

            def decay(h):
                v.wait_ge(S["s_full"], h + 1)
                if h >= 2:
                    v.wait_ge(S["W_made"], h - 1)
                d, m = Dh[h % 2], bank[h % 2]
                for a, n, m_at, tt in ((0, TP, 0, 0), (TP, P, P, 1), (TP + P, TS, TP, 2)):
                    ins = v.scalar_tensor_tensor(out=d[:, a:a + n], in0=m[:, m_at:m_at + n], scalar=uT[:, tt, h:h + 1],
                                                 in1=cmask[:, a:a + n], op0=ALU.add, op1=ALU.min)
                ins.then_inc(S["D_made"], 1)

            v.wait_ge(S["ld_ac"], 16)
            v.wait_ge(S["uT_ready"], 2)
            decay(0)
            for h in range(H):
                if h + 1 < H:
                    decay(h + 1)
                v.wait_ge(S["exp_done"], h + 1)
                if h:
                    v.wait_ge(S["nd_full"], h)
                s = bank[2 + h % 2]
                v.tensor_tensor(Wt[:, 0:TP + P], Dh[h % 2][:, 0:TP + P], s[:, 0:TP + P], ALU.mult)
                v.tensor_tensor(Wt[0:TS, TP + P:WM], Dh[h % 2][0:TS, TP + P:WM], s[0:TS, TP + P:WM],
                                ALU.mult).then_inc(S["W_made"], 1)
                v.wait_ge(S["nd_full"], h + 1)
                v.tensor_copy(den[:, 0:TP], bank[6][:, 0:TP])
                link(v.tensor_tensor(den[:, TP:T], bank[6][:, TP:T], inD[:, h, :], ALU.add))
                v.wait_ge(S["em_done"], h + 1)
                link(v.scalar_tensor_tensor(out=den, in0=den, scalar=-1.0, in1=den, op0=ALU.mult, op1=ALU.max))
                link(v.tensor_tensor(den, den, bank[4][:, 0:T], ALU.max))
                link(v.reciprocal(den, den))
                v.tensor_tensor(xn[:, h, 0:TP], bank[5][:, 0:TP], den[:, 0:TP], ALU.mult)
                link(v.tensor_tensor(inN[:, h, :], bank[5][:, TP:T], inN[:, h, :], ALU.add))
                v.tensor_tensor(xn[:, h, TP:T], inN[:, h, :], den[:, TP:T], ALU.mult).then_inc(S["h_made"], 1)

            n_st = 0
            for g in range(HP):
                n_st += 1
                v.wait_ge(S["st_full"], n_st)
                v.tensor_copy(Cp[:, 2 * g:2 * g + 2, :],
                              bank[(n_st - 1) % 4][0:DK, 0:258].rearrange("p (a b) -> p a b", a=2)).then_inc(S["st_free"], 1)

            def mask_keys(b):
                v.tensor_scalar(kmb[b % 2], Ke[0:TS, 2, :], c("bsel", TS)[:, b:b + 1], None, ALU.mult).then_inc(S["kd_made"], 1)

            v.wait_ge(S["gd_free"], n_gd[0])
            mask_keys(0)
            mask_keys(1)
            for b in range(NB):
                for g in range(2):
                    n_st += 1
                    v.wait_ge(S["st_full"], n_st)
                    o = bank[(n_st - 1) % 4]
                    for jj in range(2):
                        j = 2 * g + jj
                        ins = v.scalar_tensor_tensor(out=Ce[:, j, b, :], in0=Ce[:, j, b, :],
                                                     scalar=eC[:, j * NB + b:j * NB + b + 1],
                                                     in1=o[:, jj * 129:jj * 129 + 129], op0=ALU.mult, op1=ALU.add)
                    ins.then_inc(S["st_free"], 1)
                if b + 2 < NB:
                    mask_keys(b + 2)

            for h in range(H):
                v.wait_ge(S["hstd_ready"], h + 1)
                link(v.reciprocal(den, bank[4 + h % 2][:, 0:T]))
                link(v.scalar_tensor_tensor(out=xn[:, h, :], in0=xn[:, h, :], scalar=gain("g_head_a", h), in1=den,
                                            op0=ALU.mult, op1=ALU.mult))
                v.tensor_tensor(oT[:, h, :], oT[:, h, :], xn[:, h, :], ALU.mult).then_inc(S["y_ready"], 1)

            def residual():
                for m in range(DC):
                    o = in_d()
                    free_d(v.tensor_tensor(xT[:, m, :], xT[:, m, :], o[:, 0:T], ALU.add))

            residual()
            normalise(1, DC, xT, "g_ffn_d", xn, "xn_ready")
            v.wait_ge(S["stored"], 16 * STORES_A)
            for f in range(FT):
                rows = P if f < FT - 1 else FLAST
                o = in_d()
                v.wait_ge(S["ga_free"], GA_FFN + f + 1)
                free_d(v.tensor_tensor(hT[0:rows, f, :], sg[f % 2][0:rows, :], o[0:rows, 0:T], ALU.mult))
            residual()

            normalise(2, DC, xT, "g_kv", hn, "xn_ready")
            normalise(2, DC, xT, "g_norm_b", xn, "xn_ready", first=False)
            for m in range(CT):
                o = in_d()
                free_d(v.tensor_copy(raw[:, m, :], o[:, 0:T]))
            o = in_d()
            free_d(v.tensor_copy(rtmp[0], o[0:ROPE, 0:T]))

            def rotate(n, src):
                v.wait_ge(S["rot_full"], n)
                v.tensor_tensor(rt2, bank[4][0:ROPE, 0:T], c("sin", ROPE), ALU.mult)
                link(v.tensor_tensor(src, src, c("cos", ROPE), ALU.mult))

            rotate(1, rtmp[0])
            v.tensor_tensor(krT, rtmp[0], rt2, ALU.add).then_inc(S["kr_ready"], 1)
            normalise(3, CT, raw, "g_ckv", ckvT, "ckv_ready", every=False)
            for m in range(QT):
                o = in_d()
                if m == 0:
                    v.wait_ge(S["ckv_ready"], 1)
                free_d(v.tensor_copy(raw[:, m, :], o[:, 0:T]))
            for g in range(HP):
                o = in_d()
                free_d(v.tensor_copy(ukT[:, 2 * g:2 * g + 2, :], o[:, :].rearrange("p (a b) -> p a b", a=2)))
            normalise(4, QT, raw, "g_q", cq, "cq_ready", every=False)
            for t0, tn, tt in TOK:
                o = in_d()
                free_d(v.tensor_copy(ctok[0:tn, tt, :], o[0:tn, 0:CKV + ROPE]))
            for h in range(H):
                rt_ = rtmp[h % 2]
                rotate(2 + h, rt_)
                v.tensor_tensor(qrope[:, h, :], rt_[:, 0:TP], rt2[:, 0:TP], ALU.add)
                v.tensor_tensor(qrs[:, :, h * NS:(h + 1) * NS], rt_[:, TP:T].rearrange("p (b s) -> p b s", s=NS),
                                rt2[:, TP:T].rearrange("p (b s) -> p b s", s=NS), ALU.add).then_inc(S["qr_ready"], 1)
                for k in range(CT):
                    o = in_d()
                    v.tensor_copy(qlat[:, k, h, :], o[:, 0:TP])
                    free_d(v.tensor_copy(qls[:, k, :, h * NS:(h + 1) * NS],
                                         o[:, TP:T].rearrange("p (b s) -> p b s", s=NS)))

            def softmax_max(n, s, rows, mask_at, mask):
                mx, nb = (cols[0:rows, 4 * k + n % 2:4 * k + n % 2 + 1] for k in range(2))
                v.wait_ge(S["sc_full"], n + 1)
                m = s[:, mask_at:mask_at + mask.shape[-1]]
                link(v.tensor_tensor(m, m, mask, ALU.add))
                link(v.reduce_max(mx, s, AX.X))
                v.tensor_scalar(nb, mx, -SCALE, None, ALU.mult).then_inc(S["max_ready"], 1)

            def reciprocal_sum(n, rows):
                sm = cols[0:rows, 8 + n % 2:9 + n % 2]
                v.wait_ge(S["p_exp"], n + 1)
                link(v.reciprocal(sm, sm))
                return sm

            units = [(h, q) for h in range(H) for q in range(2)]

            def prompt_max(u):
                q = units[u][1]
                softmax_max(u, bank[5 + u % 2][:, 0:(q + 1) * P], P, q * P, c("pmask"))

            prompt_max(0)
            prompt_max(1)
            for u, (h, q) in enumerate(units):
                keys = (q + 1) * P
                p = prob2[u % 2][:, 0:keys]
                v.tensor_scalar(p, p, reciprocal_sum(u, P), None, ALU.mult).then_inc(S["p_ready"], 1)
                v.wait_ge(S["pt_full"], u + 1)
                v.tensor_copy(PT[:, 0:keys], bank[7][:, 0:keys]).then_inc(S["pt_ready"], 1)
                if u + 2 < len(units):
                    prompt_max(u + 2)
                v.wait_ge(S["ol_full"], u + 1)
                v.tensor_copy(qlat[:, :, h, q * P:(q + 1) * P],
                              bank[4][:, 0:CT * P].rearrange("p (a b) -> p a b", a=CT)).then_inc(S["ol_ready"], 1)
            NU = len(units)

            def cache_evac(b):
                for g in (1, 3, 5):
                    n = 6 * b + g
                    v.wait_ge(S["tp_full"], n + 1)
                    part, half = g // 2, g % 2
                    if part < CT:
                        ins = v.tensor_copy(cacheT[:, part, half * 512:(half + 1) * 512], bank[1][:, :])
                    else:
                        ins = v.tensor_copy(cacheR[:, half * 512:(half + 1) * 512], bank[1][0:ROPE, :])
                    ins.then_inc(S["tpd_free"], 1)

            def turned(b):
                v.wait_ge(S["ol_full"], NU + b + 1)
                v.tensor_copy(qls[:, :, b, :], bank[2][:, 0:CT * TS].rearrange(
                    "p (a n) -> p a n", a=CT)).then_inc(S["ol_ready"], 1)

            cache_evac(0)
            for b in range(NB):
                u = NU + b
                softmax_max(u, wide[0:TS, 0:PAST + TS], TS, PAST,
                            c("smask", TS)[:, (NB - 1 - b) * NS:(NB - 1 - b) * NS + TS])
                if b:
                    turned(b - 1)
                if b + 1 < NB:
                    cache_evac(b + 1)
                rs = reciprocal_sum(u, TS)
                v.wait_ge(S["pt_full"], u + 1)
                v.tensor_copy(PT[:, 0:NPG * TS], bank[4][:, 0:NPG * TS])
                v.tensor_copy(PT[0:TS, NPG * TS:(NPG + 1) * TS],
                              bank[4][0:TS, NPG * TS:(NPG + 1) * TS]).then_inc(S["pt_ready"], 1)
                v.wait_ge(S["av_full"], b + 1)
                v.tensor_scalar(osb, bank[3][0:TS, 0:CKV], rs, None, ALU.mult).then_inc(S["os_ready"], 1)
            turned(NB - 1)
            for h in range(H):
                o = in_d()
                free_d(v.tensor_copy(xn[:, h, :], o[:, 0:T]))
            residual()
            normalise(5, DC, xT, "g_ffn_m", xn, "xn_ready")

            for dst in (xtk, acc):
                for t0, tn, tt in TOK:
                    for half in range(2):
                        o = in_d()
                        free_d(v.tensor_copy(dst[0:tn, tt, half * CW:(half + 1) * CW], o[0:tn, :]))
            v.wait_ge(S["lg_full"], 1)
            v.wait_ge(S["ld_gf"], 32)
            link(v.memset(rt[:, 0:408], 0.0))
            link(v.tensor_copy(lg[:, 0:2, :], bank[4][:, 0:2 * E].rearrange("p (a b) -> p a b", a=2)))
            link(v.tensor_copy(lg[0:TS, 2, :], bank[4][0:TS, 2 * E:3 * E]))
            for tt in range(3):
                link(v.max(top[:, tt, :], lg[:, tt, :]))
                link(v.max_index(idu[:, tt, :], top[:, tt, :], lg[:, tt, :]))
            link(v.tensor_copy(idf, idu[:, :, :]))
            iota8 = mc("iota")[:, 0:E].unsqueeze(1).to_broadcast([P, 3, E])
            link(v.tensor_tensor(oh1, iota8, idf[:, :, 0:1].to_broadcast([P, 3, E]), ALU.is_equal))
            link(v.tensor_tensor(oh2, iota8, idf[:, :, 1:2].to_broadcast([P, 3, E]), ALU.is_equal))
            link(v.tensor_tensor(mk, oh1, oh2, ALU.add))
            v.tensor_tensor(mk, mk, mc("valid").unsqueeze(2).to_broadcast([P, 3, E]), ALU.mult).then_inc(S["mask_ready"], 1)
            v.tensor_tensor(gk[:, :, 1:2], top[:, :, 1:2], top[:, :, 0:1], ALU.subtract).then_inc(S["mask_ready"], 1)
            v.wait_ge(S["gk_exp"], 1)
            link(v.tensor_scalar(gk[:, :, 0:1], gk[:, :, 1:2], 1.0, None, ALU.add))
            link(v.reciprocal(gk[:, :, 0:1], gk[:, :, 0:1]))
            link(v.tensor_tensor(gk[:, :, 1:2], gk[:, :, 1:2], gk[:, :, 0:1], ALU.mult))
            link(v.tensor_tensor(oh1, oh1, gk[:, :, 0:1].to_broadcast([P, 3, E]), ALU.mult))
            link(v.tensor_tensor(oh2, oh2, gk[:, :, 1:2].to_broadcast([P, 3, E]), ALU.mult))
            link(v.tensor_tensor(gt, oh1, oh2, ALU.add))
            v.wait_ge(S["rank_full"], 1)
            link(v.tensor_copy(pos, bank[4][:, 32:56].rearrange("p (a b) -> p a b", a=3)))
            link(v.tensor_copy(cnt, bank[4][:, 64:72]))
            link(v.tensor_tensor(pos, pos, mk, ALU.mult))
            link(v.tensor_scalar(pos, pos, -1.0, None, ALU.add))
            link(v.tensor_copy(posI[:, :, 0:E], pos))
            link(v.tensor_copy(gateI[:, :, 0:E], gt))

            def one_hots(item):
                for tt in range(3):
                    v.tensor_scalar(Pm[:, tt, :], mc("iota"), posI[:, tt, item], None, ALU.is_equal)
                    ins = v.tensor_scalar(Pg[:, tt, :], mc("iota"), posI[:, tt, item], gateI[:, tt, item],
                                          ALU.is_equal, ALU.mult)
                return ins

            one_hots(slice(0, 1)).then_inc(S["p_made"], 1)
            two = lambda a: a.unsqueeze(2).to_broadcast([P, E, 2])
            link(v.tensor_tensor(fl.rearrange("p (e k) -> p e k", k=2), two(cnt),
                                 mc("kbase").rearrange("p (e k) -> p e k", k=2), ALU.is_gt))
            link(v.tensor_tensor_scan(cum, fl, mc("kbase"), 0.0, ALU.add, ALU.min))
            link(v.memset(nf, 0.0))
            link(v.tensor_scalar(nf[:, 0:1], cum[:, 2 * E - 1:2 * E], float(E), None, ALU.add))
            link(v.tensor_tensor(cum, cum, fl, ALU.subtract))
            for j in range(EXTRA):
                link(v.scalar_tensor_tensor(out=sel, in0=cum, scalar=float(j), in1=fl, op0=ALU.is_equal, op1=ALU.mult))
                link(v.tensor_tensor(s16, sel, mc("eidx"), ALU.mult))
                link(v.reduce_sum(nf[:, 1 + j:2 + j], s16, AX.X))
                link(v.tensor_tensor(s16, sel, mc("kbase"), ALU.mult))
                link(v.reduce_sum(nf[:, 6:7], s16, AX.X))
                for src, dst in ((pos, posI), (gt, gateI)):
                    link(v.tensor_tensor(p48.rearrange("p a (e k) -> p a e k", k=2),
                                         src.unsqueeze(3).to_broadcast([P, 3, E, 2]),
                                         sel.rearrange("p (e k) -> p e k", k=2).unsqueeze(1).to_broadcast([P, 3, E, 2]), ALU.mult))
                    link(v.reduce_sum(dst[:, :, E + j:E + j + 1], p48, AX.X))
                link(v.tensor_scalar(posI[:, :, E + j], posI[:, :, E + j], nf[:, 6:7], None, ALU.subtract))
            v.tensor_copy(ints[0:1, 0:2 + EXTRA], nf[0:1, 0:2 + EXTRA]).then_inc(S["tables_ready"], 1)

            v.wait_ge(S["tables_ready"], 1)
            n_items = v.value_load(ints[0:1, 0:1], min_val=E, max_val=ITEMS)

            def low(dst, src, high):
                return v.tensor_tensor(dst, src, high.bitcast(F32), ALU.subtract)

            def take_tokens(half, count):
                v.wait_ge(S["xg_hi"], count)
                cut = slice(half * CW, (half + 1) * CW)
                low(xgp[:, 1, cut], bank[6 + half][:, :], xgp[:, 0, cut]).then_inc(S[("misc_free", "xg_ready")[half]], 1)

            def split(it, h):
                v.wait_ge(S["hi_ready"], it * IH + h + 1)
                low(wpart[:, stage(h), 1, :], mring[:, place(h % IH), :], wpart[:, stage(h), 0, :]).then_inc(S["lo_ready"], 1)

            take_tokens(0, 1)
            take_tokens(1, 2)
            v.memset(cols[0:1, 12:13], 0.0).then_inc(S["gu_done"], 1)
            v.memset(cols[0:1, 15:16], 0.0).then_inc(S["used"], STAGES)
            v.memset(cols[0:1, 13:14], 0.0).then_inc(S["y_free"], 1)
            for h in range(STAGES):
                split(0, h)
            with v.Fori(0, n_items) as it:
                base = it * SHARED + 2
                for h in range(STAGES, IH + STAGES):
                    split(it, h)
                    for j in range(CE):
                        first = 2 * ORDER.index(("up", j))
                        if h == first + 3:
                            v.wait_ge(S["silu_done"], it * CE + j + 1)
                            v.wait_ge(S["used"], it * IH + after("up", j))
                            v.tensor_tensor(hh[j % 2], sl[j % 2], bank[2 + j % 2][:, :], ALU.mult).then_inc(S["gu_done"], 1)
                        if h == turn_at(j) + 2:
                            v.wait_ge(S["hh_hi"], it * CE + j + 1)
                            low(hhp[:, j % 2, 1, :], bank[6 + (1 + j) % 2][:, :], hhp[:, j % 2, 0, :]).then_inc(S["misc_free"], 1)
                    if h == 6:
                        v.wait_ge(S["misc_full"], base + 1)
                        v.tensor_copy(PTg, bank[6][:, 0:T]).then_inc(S["misc_free"], 1)
                        one_hots(bass.ds(it + 1, 1)).then_inc(S["p_made"], 1)
                    if h == IH - 1:
                        take_tokens(0, it * 2 + 3)
                    if h == IH:
                        v.wait_ge(S["used"], it * IH + after("down", CE - 1))
                        v.tensor_copy(ysb[:, 0:CW], bank[4][:, :])
                        v.tensor_copy(ysb[:, CW:D], bank[5][:, :]).then_inc(S["y_free"], 1)
                    if h == IH + 1:
                        take_tokens(1, it * 2 + 4)
                for u, (t0, tn, tt) in enumerate(TOK):
                    for half in range(2):
                        n = 1 + CE + 2 + 2 * u + half
                        v.wait_ge(S["misc_full"], base + n + 1)
                        a = acc[0:tn, tt, half * CW:(half + 1) * CW]
                        v.tensor_tensor(a, a, bank[6 + n % 2][0:tn, :], ALU.add).then_inc(S["misc_free"], 1)

            v.memset(cols[0:1, 14:15], 0.0).then_inc(S["acc_done"], 1)
            for t0, tn, tt in TOK:
                v.wait_ge(S["fin_ss"], tt + 1)
                s = cols[0:tn, 8 + tt:9 + tt]
                link(v.reciprocal(s, s))
                v.scalar_tensor_tensor(out=acc[0:tn, tt, :], in0=acc[0:tn, tt, :], scalar=s, in1=gfin[0:tn, :],
                                       op0=ALU.mult, op1=ALU.mult).then_inc(S["fin_ready"], 1)

        @block.scalar
        def _(a):
            b_gate = i["b_gate_a"][0].rearrange("(g h) -> h g", g=2)
            a.dma_start(tiny[:, 0:2], b_gate).then_inc(S["ld_tiny"], 16)
            a.dma_start(tiny[:, 8:16], i["state_m"][0].rearrange("b h -> h b")).then_inc(S["ld_tiny"], 16)
            a.dma_start(wg[:, :, :], rows_of(w_in, 2 * hq + 2 * hv, 2 * H)).then_inc(S["ld_wg"], 16)
            a.dma_start(ac[:, :], i["aconst"]).then_inc(S["ld_ac"], 16)
            n_ga, n_link = [0], [0]

            def link(ins):
                n_link[0] += 1
                ins.then_inc(S["achain"], 1)
                a.wait_ge(S["achain"], n_link[0])

            def in_a():
                n_ga[0] += 1
                a.wait_ge(S["ga_full"], n_ga[0])
                return bank[(n_ga[0] - 1) % 2]

            def squares(chunks_, src, dst, sem_, first):
                for m in range(chunks_):
                    a.wait_ge(S[sem_], first + m + 1)
                    a.activation(dst[:, m, :], src[:, m, :], ACT.Square).then_inc(S["sq_ready"], 1)

            def root(k, width):
                a.wait_ge(S["ss_full"], k + 1)
                a.activation(stdv(k), bank[7][:, 0:T], ACT.Sqrt, bias=c("eps"), scale=1.0 / width).then_inc(S["std_ready"], 1)

            a.wait_ge(S["ld_const"], 16)
            squares(DC, xT, xn, "x_ready", 0)
            root(0, D)
            a.wait_ge(S["gates_full"], 1)
            a.wait_ge(S["bg_ready"], 1)
            a.activation(rU, bank[4][0:H, 0:T], ACT.Tanh, bias=tiny[:, 2:3], scale=1.0 / CAP)
            link(a.activation(rE, bank[5][0:H, 0:T], ACT.Tanh, bias=tiny[:, 3:4], scale=1.0 / CAP))
            link(a.activation(rE, rE, ACT.Exp, scale=-CAP))
            a.activation(rE, rE, ACT.Ln, bias=c("one", H), scale=1.0).then_inc(S["lf_ready"], 1)
            for m in range(HP):
                o = in_a()
                a.activation(qT[:, m, :], o[:, 0:T], ACT.Copy, scale=DK ** -0.5).then_inc(S["ga_free"], 1)
            for m in range(DC):
                o = in_a()
                a.activation(oT[:, m, :], o[:, 0:T], ACT.Sigmoid).then_inc(S["ga_free"], 1)
            a.wait_ge(S["uT_full"], 1)
            a.activation(eI.rearrange("p a b -> p (a b)"), bank[5][:, 0:HP * TS], ACT.Exp)
            a.activation(eC, bank[5][:, HP * TS:HP * TS + HP * NB], ACT.Exp)
            a.wait_ge(S["uT_ready"], 2)
            a.activation(uT[:, :, H:2 * H], uT[:, :, H:2 * H], ACT.Exp).then_inc(S["e_ready"], 1)
            for h in range(H):
                a.wait_ge(S["D_made"], h + 1)
                a.activation(Dh[h % 2], Dh[h % 2], ACT.Exp).then_inc(S["exp_done"], 1)
                a.wait_ge(S["m_full"], h + 1)
                a.activation(bank[4][:, 0:T], bank[4][:, 0:T], ACT.Exp).then_inc(S["em_done"], 1)
            a.wait_ge(S["h_made"], H)

            def head_square(h):
                if h >= 2:
                    a.wait_ge(S["hss_full"], h - 1)
                a.activation(Dh[h % 2][:, 0:T], xn[:, h, :], ACT.Square).then_inc(S["hsq_ready"], 1)

            head_square(0)
            for h in range(H):
                if h + 1 < H:
                    head_square(h + 1)
                a.wait_ge(S["hss_full"], h + 1)
                b4 = bank[4 + h % 2][:, 0:T]
                a.activation(b4, b4, ACT.Sqrt, bias=c("eps"), scale=1.0 / DV).then_inc(S["hstd_ready"], 1)
            squares(DC, xT, xn, "gd_free", GD_FFN - DC)
            root(1, D)
            for f in range(FT):
                rows = P if f < FT - 1 else FLAST
                o = in_a()
                if f >= 2:
                    a.wait_ge(S["gd_free"], GD_FFN + f - 1)
                a.activation(sg[f % 2][0:rows, :], o[0:rows, 0:T], ACT.Silu).then_inc(S["ga_free"], 1)
            squares(DC, xT, xn, "gd_free", GD_CKV - DC)
            root(2, D)
            squares(CT, raw, ckvT, "gd_free", GD_CKV)
            root(3, CKV)
            squares(QT, raw, cq, "gd_free", GD_CQ)
            root(4, QL)
            a.wait_ge(S["kr_ready"], 1)
            a.wait_ge(S["cq_ready"], 1)
            for h in range(H):
                if h >= 2:
                    a.wait_ge(S["qr_ready"], h - 1)
                    a.wait_ge(S["gd_full"], GD_QL + CT * (h - 1))
                o = in_a()
                a.activation(qn[h % 2], o[:, 0:T], ACT.Copy).then_inc(S["ga_free"], 1)
                o = in_a()
                a.activation(rtmp[h % 2], o[0:ROPE, 0:T], ACT.Copy).then_inc(S["ga_free"], 1)

            def col(k, n, rows=P):
                return cols[0:rows, 4 * k + n % 2:4 * k + n % 2 + 1]

            units = [(h, q) for h in range(H) for q in range(2)]
            for u, (h, q) in enumerate(units):
                keys = (q + 1) * P
                a.wait_ge(S["max_ready"], u + 1)
                a.activation(prob2[u % 2][:, 0:keys], bank[5 + u % 2][:, 0:keys], ACT.Exp, bias=col(1, u), scale=SCALE,
                             accum_out=col(2, u)).then_inc(S["p_exp"], 1)

            def cache_evac(b):
                for g in (0, 2, 4):
                    a.wait_ge(S["tp_full"], 6 * b + g + 1)
                    part, half = g // 2, g % 2
                    if part < CT:
                        ins = a.activation(cacheT[:, part, half * 512:(half + 1) * 512], bank[0][:, :], ACT.Copy)
                    else:
                        ins = a.activation(cacheR[:, half * 512:(half + 1) * 512], bank[0][0:ROPE, :], ACT.Copy)
                    ins.then_inc(S["tpa_free"], 1)

            cache_evac(0)
            for b in range(NB):
                a.wait_ge(S["max_ready"], len(units) + b + 1)
                a.activation(prob[0:TS, :], wide[0:TS, 0:PAST + TS], ACT.Exp, bias=col(1, b, TS), scale=SCALE,
                             accum_out=col(2, b, TS)).then_inc(S["p_exp"], 1)
                if b + 1 < NB:
                    cache_evac(b + 1)
            squares(DC, xT, acc_sq, "gd_free", GD_MOE - DC)
            root(5, D)
            a.wait_ge(S["mask_ready"], 2)
            a.activation(gk[:, :, 1:2], gk[:, :, 1:2], ACT.Exp).then_inc(S["gk_exp"], 1)
            a.wait_ge(S["tables_ready"], 1)
            n_items = a.value_load(ints[0:1, 0:1], min_val=E, max_val=ITEMS)

            def take_tokens(half, full, count):
                a.wait_ge(S["misc_full"], full)
                a.activation(xgp[:, 0, half * CW:(half + 1) * CW], bank[6 + half][:, :], ACT.Copy).then_inc(S["xg_hi"], 1)

            def split(it, h):
                a.wait_ge(*loaded(it, h))
                a.wait_ge(S["used"], it * IH + h + 1)
                a.activation(wpart[:, stage(h), 0, :], mring[:, place(h % IH), :], ACT.Copy).then_inc(S["hi_ready"], 1)

            a.wait_ge(S["kv_stored"], 64)
            take_tokens(0, 1, 1)
            take_tokens(1, 2, 2)
            for n in (NPRE - 4, NPRE - 3, NPRE - 2):
                a.wait_ge(*release[n])
            for h in range(STAGES):
                a.wait_ge(*loaded(0, h))
                a.activation(wpart[:, stage(h), 0, :], mring[:, place(h), :], ACT.Copy).then_inc(S["hi_ready"], 1)
            with a.Fori(0, n_items) as it:
                for h in range(STAGES, IH + STAGES):
                    split(it, h)
                    for j in range(CE):
                        first = 2 * ORDER.index(("gate", j))
                        if h == first + 3:
                            a.wait_ge(S["used"], it * IH + after("gate", j))
                            a.wait_ge(S["gu_done"], it * CE + 1 + max(0, j - 1))
                            a.activation(sl[j % 2], bank[j % 2][:, :], ACT.Silu).then_inc(S["silu_done"], 1)
                        if h == turn_at(j) + 2:
                            a.wait_ge(S["misc_full"], it * SHARED + 2 + 1 + j + 1)
                            a.activation(hhp[:, j % 2, 0, :], bank[6 + (1 + j) % 2][:, :], ACT.Copy).then_inc(S["hh_hi"], 1)
                    if h == IH - 1:
                        take_tokens(0, it * SHARED + 2 + 1 + CE + 1, it * 2 + 3)
                    if h == IH + 1:
                        take_tokens(1, it * SHARED + 2 + 1 + CE + 2, it * 2 + 4)
            a.wait_ge(S["acc_done"], 1)
            for t0, tn, tt in TOK:
                s = cols[0:tn, 8 + tt:9 + tt]
                link(a.activation(xtk[0:tn, tt, :], acc[0:tn, tt, :], ACT.Square, accum_out=s))
                a.activation(s, s, ACT.Sqrt, bias=c("eps", tn), scale=1.0 / D).then_inc(S["fin_ss"], 1)

        @block.gpsimd
        def _(g):
            g.dma_start(pages[:, :], i["page_table"].rearrange("(o b) n -> o (b n)", o=1)).then_inc(S["ld_pages"], 16)
            st_C, st_n = i["state_C"][0], i["state_n"][0]
            for h in range(H):
                r, j = (h % 2) * DK, h // 2
                g.dma_start(Ce[r:r + DK, j, :, 0:DV], st_C[:, h].rearrange("b k v -> k b v")).then_inc(S["ld_state"], 16)
                g.dma_start(Ce[r:r + DK, j, :, DV], st_n[:, h].rearrange("b k -> k b")).then_inc(S["ld_state"], 16)
            g.wait_ge(S["gates_full"], 1)
            g.dma_start(wg[:, :, 0:E], rows_of(i["w_router"][0], 0, E)).then_inc(S["ld_wr"], 16)
            g.wait_ge(S["st_free"], HP)
            g.dma_start(out[2][0, 0].rearrange("h k v -> k h v"), Cp[:, :, 0:DV]).then_inc(S["stored"], 16)
            g.dma_start(out[3][0, 0].rearrange("h k -> k h"), Cp[:, :, DV]).then_inc(S["stored"], 16)
            g.dma_start(out[4][0].rearrange("a h -> h a"), tiny[:, 16:17]).then_inc(S["stored"], 16)
            g.dma_start(out[9][0].rearrange("b h -> h b"), tiny[:, 17:17 + NB]).then_inc(S["stored"], 16)
            g.wait_ge(S["st_free"], HP + 2 * NB)
            for h in range(H):
                r, j = (h % 2) * DK, h // 2
                g.dma_start(out[7][0][:, h].rearrange("b k v -> k b v"), Ce[r:r + DK, j, :, 0:DV]).then_inc(S["stored"], 16)
                g.dma_start(out[8][0][:, h].rearrange("b k -> k b"), Ce[r:r + DK, j, :, DV]).then_inc(S["stored"], 16)

            def load_rotary(b):
                with g.Fori(0, NPG) as j:
                    page = g.value_load(pages[0:1, bass.ds(j + b * NPG, 1)], min_val=0, max_val=i["cache_krope"].shape[0] - 1)
                    g.dma_start(crk[b % BUFS][:, bass.ds(j, 1), :],
                                i["cache_krope"][bass.ds(page, 1), :, :].rearrange("g p c -> p g c")).then_inc(cr_full[b % BUFS], 16)

            g.wait_ge(S["stored"], 16 * STORES_A)
            g.wait_ge(S["gd_free"], GD_FFN)
            g.wait_ge(S["ld_pages"], 16)
            load_rotary(0)
            load_rotary(1)
            g.wait_ge(S["gd_free"], GD_QL)
            for n, (dst_c, dst_r) in enumerate(((out[5][0], out[6][0]), (out[10], out[11]))):
                for dst, a0, a1 in ((dst_c, 0, CKV), (dst_r, CKV, CKV + ROPE)):
                    if n == 0:
                        g.dma_start(dst.rearrange("(t p) c -> p t c", p=P), ctok[:, 0:2, a0:a1]).then_inc(S["kv_stored"], 16)
                    else:
                        g.dma_start(dst.rearrange("b s c -> (b s) c"), ctok[0:TS, 2, a0:a1]).then_inc(S["kv_stored"], 16)
            for b in range(2, NB):
                if b == 2:
                    g.wait_ge(*release[CH["uq1"]])
                else:
                    g.wait_ge(S["av_full"], b - BUFS + 1)
                load_rotary(b)
            NU = 2 * H
            g.wait_ge(S["ol_full"], NU + NB)
            g.dma_start(gfin, i["g_final"].rearrange("(a n) -> a n", a=1).to_broadcast([P, D])).then_inc(S["ld_gf"], 16)
            g.dma_start(arena[:, MAT:MAT + MCOLS], i["mconst"]).then_inc(S["ld_gf"], 16)
            g.wait_ge(S["kv_stored"], 64)

        @block.sync
        def _(sp):
            sp.dma_start(xtok[:, 0, :], i["x_prompt"][0, 0:P, :]).then_inc(S["ld_x"], 16)
            sp.dma_start(xtok[:, 1, :], i["x_prompt"][0, P:TP, :]).then_inc(S["ld_x"], 16)
            sp.dma_start(xtok[0:TS, 2, :], i["x_sample"].rearrange("b s d -> (b s) d")).then_inc(S["ld_x"], 16)
            sp.dma_start(cs[:, :], i["const"]).then_inc(S["ld_const"], 16)
            for name, rows in GAINS:
                src = i[name][0] if len(i[name].shape) > 1 else i[name]
                if len(src.shape) == 1:
                    src = src.rearrange("(r n) -> r n", n=P)
                sp.dma_start(Dh[0][G0[name]:G0[name] + rows, 0:P], src).then_inc(S["ld_gain"], 16)

            def load_cache(b):
                with sp.Fori(0, NPG) as j:
                    page = sp.value_load(pages[0:1, bass.ds(j + b * NPG, 1)], min_val=0, max_val=i["cache_ckv"].shape[0] - 1)
                    sp.dma_start(ctk[b % BUFS][:, bass.ds(j, 1), :],
                                 i["cache_ckv"][bass.ds(page, 1), :, :].rearrange("g p c -> p g c")).then_inc(ck_full[b % BUFS], 16)

            for n, (name, parts) in enumerate(chunks):
                if name == "dd4":
                    sp.wait_ge(S["stored"], 16 * STORES_A)
                    sp.wait_ge(S["ld_pages"], 16)
                    load_cache(0)
                    load_cache(1)
                if n >= SLOTS:
                    sp.wait_ge(*release[n - SLOTS])
                for k, w, at, rows, src in parts:
                    dst = ring[0:rows, n % SLOTS, at:at + k * w].rearrange("p (c n) -> p c n", c=k)
                    sp.dma_start(dst, src).then_inc(w_full[n % SLOTS], 16)

            def expert_half(e, h):
                kind, j = ORDER[h // 2]
                w, a, half = i[f"w_{kind}_m"][0], HALFW // CW if kind != "down" else KD // 2, h % 2
                if kind != "down":
                    src = w[bass.ds(e, 1), half * D // 2:(half + 1) * D // 2, j * CW:(j + 1) * CW]
                else:
                    src = w[bass.ds(e, 1), j * CW + half * CW // 2:j * CW + (half + 1) * CW // 2, :]
                sp.dma_start(mring[:, place(h), :].rearrange("p (c n) -> p c n", c=a),
                             src.rearrange("e (c p) n -> p (e c) n", p=P)).then_inc(half_full[place(h)], 16)

            def item_rest(it, e):
                h0 = 2 * ORDER.index(("down", 0))
                for h in range(HALVES, IH):
                    if h != h0:
                        sp.wait_ge(S["lo_ready"], it * IH + h - HALVES + 1)
                        expert_half(e, h)
                    if h == h0 + 1:
                        expert_half(e, h0)

            def item_first(it, e, halves=range(HALVES)):
                for h in halves:
                    sp.wait_ge(S["lo_ready"], it * IH + IH + h - HALVES + 1)
                    expert_half(e, h)

            under = [NPRE - 7, NPRE - 7, NPRE - 6, NPRE - 6, NPRE - 5, NPRE - 1, NPRE - 1]
            for h in range(HALVES):
                if h == 5:
                    for b in range(2, NB):
                        if b == 2:
                            sp.wait_ge(*release[CH["uq1"]])
                        else:
                            sp.wait_ge(S["av_full"], b - BUFS + 1)
                        load_cache(b)
                sp.wait_ge(*release[under[h]])
                expert_half(0, h)
            with sp.Fori(0, E - 1) as it:
                item_rest(it, it)
                item_first(it, it + 1)
            item_rest(E - 1, E - 1)
            def expert(number):
                return sp.value_load(ints[0:1, number], min_val=0, max_val=E - 1)

            sp.wait_ge(S["tables_ready"], 1)
            n_items = sp.value_load(ints[0:1, 0:1], min_val=E, max_val=ITEMS)
            item_first(E - 1, expert(slice(1, 2)), range(STAGES))
            with sp.If(n_items > E):
                with sp.Fori(E, n_items) as it:
                    e, following = expert(bass.ds(it - (E - 1), 1)), expert(bass.ds(it - (E - 2), 1))
                    item_first(it - 1, e, range(STAGES, HALVES))
                    item_rest(it, e)
                    item_first(it, following, range(STAGES))
            for t0, tn, tt in TOK:
                sp.wait_ge(S["fin_ready"], tt + 1)
                dst = out[0][0, t0:t0 + tn, :] if tt < 2 else out[1].rearrange("b s d -> (b s) d")
                sp.dma_start(dst, acc[0:tn, tt, :]).then_inc(S["outs"], 16)
            sp.wait_ge(S["outs"], 48)
            sp.wait_ge(S["stored"], 16 * STORES_A)


GA_FFN = HP + DC
GD_FFN = HP + 6 + 3 + DC
GD_CKV = GD_FFN + FT + DC
GD_CQ = GD_CKV + CT + 1
GD_QL = GD_CQ + QT + HP + 3
GD_MOE = GD_QL + CT * H + H + DC
STORES_A = 4 + 2 * H


def shape_constants():
    import numpy as np

    f = np.float32
    r = np.arange(P)
    t = np.arange(TS)
    parts = {
        "ident": np.eye(P), "ones": np.ones((P, P)), "rot": np.zeros((P, ROPE)), "bsel": np.zeros((P, NB)),
        "eps": np.full((P, 1), EPS), "one": np.ones((P, 1)),
        "pmask": np.where(r[None, :] <= r[:, None], 0.0, NEG),
    }
    x = np.arange((2 * NB - 1) * NS)
    parts["smask"] = np.where((x[None, :] // NS == NB - 1) & (x[None, :] % NS <= r[:, None] % NS), 0.0, NEG)
    half = ROPE // 2
    parts["rot"][half + np.arange(half), np.arange(half)] = -1.0
    parts["rot"][np.arange(half), half + np.arange(half)] = 1.0
    parts["bsel"][t, t // NS] = 1.0
    pos = np.concatenate([np.arange(TP), PAST + t % NS]).astype(f)
    inv = (f(10000.0) ** (-np.arange(half, dtype=f) / f(half))).astype(f)
    ang = (pos[:, None] * inv[None, :]).astype(f)
    for name, fn in (("cos", np.cos), ("sin", np.sin)):
        tab = fn(ang).astype(f).T
        parts[name] = np.concatenate([tab, tab, np.zeros((P - ROPE, T))])
    const = np.concatenate([parts[n] for n, _ in CONSTS], axis=1).astype(f)
    m = {
        "tri": np.where(r[:, None] <= r[None, :], 1.0, 0.0), "iota": np.tile(r, (P, 1)),
        "eidx": np.tile(np.arange(2 * E) // 2, (P, 1)), "kbase": np.tile(P * (1 + np.arange(2 * E) % 2), (P, 1)),
        "valid": np.stack([np.ones(P), np.ones(P), r < TS], axis=1),
    }
    mconst = np.concatenate([m[n] for n, _ in MCONSTS], axis=1).astype(f)
    tri = np.where(r[:, None] <= r[None, :], 0.0, NEG)
    own = np.full((P, TS), NEG)
    own[:TS] = np.where((t[:, None] // NS == t[None, :] // NS) & (t[:, None] <= t[None, :]), 0.0, NEG)
    selp = np.zeros((P, HP, P))
    for j in range(HP):
        selp[2 * j, j, :DK] = 1.0
        selp[2 * j + 1, j, DK:] = 1.0
    aconst = np.concatenate([tri, np.zeros((P, P)), tri, own, selp.reshape(P, -1)], axis=1).astype(f)
    return {"const": const, "mconst": mconst, "aconst": aconst}


_INS = """x_prompt x_sample state_C state_n state_m cache_ckv cache_krope page_table g_norm_a w_in_a b_gate_a g_head_a
    w_out_a g_kv w_dkv g_ckv w_uk w_uv g_norm_b w_dq g_q w_uq w_o_b g_ffn_d w_gate_d w_up_d w_down_d g_ffn_m w_router
    w_gate_m w_up_m w_down_m g_final""".split()
_OUTS = [(1, TP, D), (NB, NS, D), (1, 1, H, DK, DV), (1, 1, H, DK), (1, 1, H), (1, TP, CKV), (1, TP, ROPE),
         (1, NB, H, DK, DV), (1, NB, H, DK), (1, NB, H), (NB, NS, CKV), (NB, NS, ROPE)]


def kernel(**inputs):
    import numpy as np
    import concourse.bacc as bacc
    from concourse.bass_utils import run_bass_kernel_spmd

    nc = bacc.Bacc("TRN2", target_bir_lowering=False, num_devices=1)
    arrays, handles = {}, {}
    named = {**{n: inputs[n] for n in _INS}, **shape_constants()}
    for name, value in named.items():
        array = np.ascontiguousarray(value)
        arrays[f"in_{name}"] = array
        handles[name] = nc.dram_tensor(f"in_{name}", array.shape, mybir.dt.from_np(array.dtype), kind="ExternalInput").ap()
    outs = [nc.dram_tensor(f"out_{n}", shape, F32, kind="ExternalOutput").ap() for n, shape in enumerate(_OUTS)]
    build(nc, handles, outs)
    r = run_bass_kernel_spmd(nc, [arrays], core_ids=[0])
    return tuple(r.results[0][f"out_{n}"] for n in range(len(_OUTS)))
```

```python
from contextlib import ExitStack

import concourse.bass as bass
from concourse import mybir

F32 = mybir.dt.float32
I32 = mybir.dt.int32
U32 = mybir.dt.uint32
F32R = mybir.dt.float32r

P = 128
D = 1024
DC = D // P
TP = 256
NB, NS = 8, 4
TS = NB * NS
T = TP + TS
TOK = [(0, P, 0), (P, P, 1), (TP, TS, 2)]
H = 8
HP = H // 2
DK, DV = 64, 128
CAP = 15.0
NOPE, ROPE = 128, 64
CKV = 256
CT = CKV // P
QL = 384
QT = QL // P
SCALE = (NOPE + ROPE) ** -0.5
PAGE = 128
NPG = 8
PAST = NPG * PAGE
BUFS = 3
FF = 2752
FT = (FF + P - 1) // P
FLAST = FF - (FT - 1) * P
E = 8
FE = 3584
CW = 512
CE = FE // CW
KD = CW // P
SLOTS = 7
SLOTW = DC * CW
ARENA = 18368
HALFW = SLOTW // 2
HALVES = 7
STAGES = 3
ORDER = [("gate", 0), ("up", 0)] + [(kind, j + (kind != "down")) for j in range(CE - 1) for kind in ("gate", "up", "down")]
ORDER += [("down", CE - 1)]
IH = 2 * len(ORDER)
EPS = 1e-6
NEG = -1e30
EXTRA = 4
ITEMS = E + EXTRA

GAINS = [("g_norm_a", DC), ("g_head_a", H), ("g_ffn_d", DC), ("g_kv", DC), ("g_norm_b", DC), ("g_ffn_m", DC),
         ("g_ckv", CT), ("g_q", QT)]
G0, GROWS = {}, 0
for _name, _rows in GAINS:
    G0[_name] = GROWS
    GROWS += _rows

CONSTS = [("ident", P), ("ones", P), ("pmask", P), ("smask", (2 * NB - 1) * NS), ("cos", T), ("sin", T),
          ("rot", ROPE), ("bsel", NB), ("eps", 1), ("one", 1)]
MCONSTS = [("tri", P), ("iota", P), ("eidx", 2 * E), ("kbase", 2 * E), ("valid", 3)]
C0, CCOLS = {}, 0
for _name, _cols in CONSTS:
    C0[_name] = (CCOLS, _cols)
    CCOLS += _cols
M0, MCOLS = {}, 0
for _name, _cols in MCONSTS:
    M0[_name] = (MCOLS, _cols)
    MCOLS += _cols
MAT = 8736
WM = TP + P + TS
ACOLS = WM + HP * P


def build(nc, i, out):
    ALU = mybir.AluOpType
    ACT = mybir.ActivationFunctionType
    AX = mybir.AxisListType

    with ExitStack() as ctx:
        ctx.enter_context(nc.allow_non_contiguous_dma(reason="state vectors and gate biases: a few KiB in all"))

        def sb(name, shape, dt=F32):
            return ctx.enter_context(nc.sbuf_tensor(name, shape, dt))

        def sem(name):
            return ctx.enter_context(nc.semaphore(name))

        with nc.sbuf_tensor("ring", [P, SLOTS, SLOTW], F32) as ring:
            pass
        mring = sb("mring", [P, HALVES, HALFW])
        sb("gap", [P, 4 * SLOTW - HALVES * HALFW])
        wpart = sb("wpart", [P, STAGES, 2, HALFW], F32R)
        xT = sb("xT", [P, DC, T])
        xn = sb("xn", [P, DC, T])
        cs = sb("cs", [P, CCOLS])
        gT = sb("gT", [P, GROWS])
        wg = sb("wg", [P, DC, 2 * H])
        cols = sb("cols", [P, 16])
        tiny = sb("tiny", [H, 32])
        ints = sb("ints", [1, 8], I32)
        pages = sb("pages", [1, NB * NPG], I32)
        with nc.sbuf_tensor("arena", [P, ARENA], F32) as arena:
            pass
        with nc.sbuf_tensor("ffparts", [P, 2 * (FT + DC) * T], F32R) as ffparts:
            pass
        sb("below", [P, ARENA - 4 * D - 4 * CW - 2 * T])
        yp = sb("yp", [P, 2, D], F32R)
        ptp = sb("ptp", [P, 2, T], F32R)
        xgp = sb("xgp", [P, 2, D], F32R)
        hhp = sb("hhp", [P, 2, 2, CW], F32R)
        bank = [ctx.enter_context(nc.psum_tensor(f"bank{n}", [P, 512], F32)) for n in range(5)]
        wide = ctx.enter_context(nc.psum_tensor("wide", [P, 3 * 512], F32))
        bank += [wide[:, 512 * n:512 * (n + 1)] for n in range(3)]

        def c(name, rows=P):
            a, n = C0[name]
            return cs[0:rows, a:a + n]

        def mc(name):
            a, n = M0[name]
            return arena[:, MAT + a:MAT + a + n]

        def gain(name, k):
            return gT[:, G0[name] + k:G0[name] + k + 1]

        def area(at, *dims, rows=P):
            n = 1
            for d in dims:
                n *= d
            v = arena[0:rows, at:at + n]
            if len(dims) == 2:
                return v.rearrange("p (a b) -> p a b", a=dims[0])
            if len(dims) == 3:
                return v.rearrange("p (a b d) -> p a b d", a=dims[0], b=dims[1])
            return v

        ident, ones = c("ident"), c("ones")
        xtok = area(0, 3, D)
        VX = area(0, 3, H, DV + 1)
        qT, kT = area(3096, HP, T), area(4248, HP, T)
        Cp = area(3096, H, DV + 1, rows=DK)
        kmb = [area(4248, H * DK, rows=TS), area(4760, H * DK, rows=TS)]
        oT = area(5400, DC, T)
        Ke = area(7704, 3, H * DK)
        Ce = area(9240, HP, NB, DV + 1)
        ac = area(13368, ACOLS)
        cmask = ac[:, 0:WM]
        selp = ac[0:H, WM:].rearrange("p (j m) -> p j m", j=HP)
        rU, rE, rA, rM, rZ = (area(14296 + T * k, T, rows=H) for k in range(5))
        Dh = [area(15736, WM), area(16152, WM)]
        Wt = area(16568, WM)
        inN, inD = area(16984, H, TS), area(17240, H, TS)
        uT = area(17496, 3, 2 * H)
        eI, eC = area(17544, HP, TS), area(17672, HP * NB)
        xflat = xn[:, :, :].rearrange("p a b -> p (a b)")
        qbd = xflat[:, 0:HP * 288].rearrange("p (j n) -> p j n", j=HP)
        qdiag = xflat[:, 0:HP * 288].rearrange("p (j b s) -> p j b s", j=HP, s=TS + NS)[:, :, 0:NB, 0:NS]
        itok = xflat[0:TS, HP * 288:HP * 288 + H * (DV + 1)].rearrange("p (h n) -> p h n", h=H)
        den = area(17832, T)
        hp = ffparts[:, 0:2 * FT * T].rearrange("p (s f t) -> p s f t", s=2, f=FT)
        xp = ffparts[:, 2 * FT * T:].rearrange("p (s f t) -> p s f t", s=2, f=DC)
        sg = [area(17280, T), area(17568, T), area(17856, T)]
        hn = area(0, DC, T)
        qlat = area(0, CT, H, TP)
        qls = area(CT * H * TP, CT, NB, H * NS)
        qrope = area(4608, H, TP, rows=ROPE)
        qrs = area(4608 + H * TP, NB, H * NS, rows=ROPE)
        ckvT, krT = area(6912, CT, T), area(7488, T, rows=ROPE)
        ctok = area(7776, 3, CKV + ROPE)
        raw = area(8736, 3, T)
        qn = [area(8736, T), area(9024, T)]
        rtmp = [area(9312, T, rows=ROPE), area(9600, T, rows=ROPE)]
        rt2 = area(9888, T, rows=ROPE)
        prob = area(8736, PAST + TS)
        osb = area(4608, CKV, rows=TS)
        prob2 = [area(8736, TP), area(8736 + TP, TP)]
        PT = area(9792, 384)
        cacheT = area(10176, CT, PAST)
        cacheR = area(12224, PAST, rows=ROPE)
        cq = area(10176, QT, T)
        ukT = area(11040, H, CKV)
        pagebuf = [area(13248, NPG * (CKV + ROPE)), area(13248 + 2560, NPG * (CKV + ROPE)), ring[:, 4, 0:NPG * (CKV + ROPE)]]
        ctk = [buf[:, 0:NPG * CKV].rearrange("p (g c) -> p g c", g=NPG) for buf in pagebuf]
        crk = [buf[:, NPG * CKV:].rearrange("p (g c) -> p g c", g=NPG) for buf in pagebuf]
        acc_sq = area(0, DC, T)

        def stdv(k):
            return den if k == 0 else area(9600 if 2 <= k <= 4 else 6912, T)

        acc = area(0, 3, D)
        xtk = area(3072, 3, D)
        xg = [xgp[:, part, :].rearrange("p (a b) -> p a b", a=DC) for part in range(2)]
        hh = [area(7168, CW), area(7680, CW)]
        Pm, Pg = area(10240, 3, P), area(10624, 3, P)
        gfin = area(9216, D)
        sl = [area(6144, CW), area(6656, CW)]
        rt = area(8192, 408)
        lg, mk, gt, pos = (rt[:, 24 * k:24 * (k + 1)].rearrange("p (a b) -> p a b", a=3) for k in range(4))
        oh1, oh2, top = (rt[:, 96 + 24 * k:120 + 24 * k].rearrange("p (a b) -> p a b", a=3) for k in range(3))
        idf = rt[:, 168:192].rearrange("p (a b) -> p a b", a=3)
        gk = rt[:, 192:198].rearrange("p (a b) -> p a b", a=3)
        cnt = rt[:, 200:208]
        fl, cum, sel, s16 = (rt[:, 208 + 16 * k:224 + 16 * k] for k in range(4))
        posI = rt[:, 272:272 + 3 * 13].rearrange("p (a b) -> p a b", a=3)
        gateI = rt[:, 312:312 + 3 * 13].rearrange("p (a b) -> p a b", a=3)
        nf = rt[:, 352:360]
        p48 = rt[:, 360:408].rearrange("p (a b) -> p a b", a=3)
        idu = sb("idu", [P, 3, 8], U32)

        names = """ld_const ld_x ld_gain ld_tiny ld_wg ld_state ld_ac ld_pages ld_wr ld_gf
            gt_full gt_ready bg_ready x_full x_ready sq_ready ss_full std_ready xn_ready
            ga_full ga_free gd_full gd_free gates_full lf_ready rows_ready uT_full uT_ready e_ready
            qe_ready inter_full inter_tok inter_ready s_full D_made exp_done W_made nd_full nd_read em_done h_made kd_made
            st_full st_free hsq_ready hss_full hstd_ready y_ready stored
            ckv_raw ckv_ready kr_ready cq_raw cq_ready ss2_full std2_ready sq2_ready
            uk_ready qn_ready rr_ready qr_ready rot_full ql_ready
            sc_full max_ready p_exp p_ready pt_full pt_ready ol_full ol_ready av_full os_ready tp_full tpa_free tpd_free
            lg_full mask_ready rank_full tables_ready p_made
            f_hi f_lo f_used xp_hi xp_lo hp_hi hp_lo hi_ready lo_ready used silu_done hh_hi xg_hi pg_hi y_hi gu_done misc_full m_full xg_ready gk_exp acc_done fin_ss kv_stored misc_free y_full y_free
            dchain achain fin_sq fin_ready outs""".split()
        S = {n: sem(n) for n in names}
        ck_full = [sem(f"ck_full{k}") for k in range(BUFS)]
        cr_full = [sem(f"cr_full{k}") for k in range(BUFS)]
        w_full = [sem(f"w_full{k}") for k in range(SLOTS)]
        half_full = [sem(f"half_full{k}") for k in range(HALVES)]

        w_in, w_out = i["w_in_a"][0], i["w_out_a"][0]
        chunks = []

        def rows_of(w, c0, n):
            return w[:, c0:c0 + n].rearrange("(c p) n -> p c n", p=P)

        def chunk(name, w, c0, n):
            k = w.shape[0] // P
            chunks.append((name, [(k, n, 0, P, rows_of(w, c0, n))]))

        hq, hv = H * DK, H * DV
        chunk("k0", w_in, hq, hq)
        chunk("q0", w_in, 0, hq)
        for n in range(2):
            chunk(f"o{n}", w_in, 2 * hq + hv + n * CW, CW)
        for n in range(2):
            chunk(f"v{n}", w_in, 2 * hq + n * CW, CW)
        for n in range(2):
            chunk(f"out{n}", w_out, n * CW, CW)
        FCH = [(n * CW, min(CW, FF - n * CW)) for n in range((FF + CW - 1) // CW)]
        for n, (a, w) in enumerate(FCH):
            chunk(f"gd{n}", i["w_gate_d"][0], a, w)
            chunk(f"ud{n}", i["w_up_d"][0], a, w)
        wd = i["w_down_d"][0]
        for m in range(DC):
            chunks.append((f"dd{m}", [
                (FT - 1, P, 0, P, wd[0:(FT - 1) * P, m * P:(m + 1) * P].rearrange("(c p) n -> p c n", p=P)),
                (1, P, (FT - 1) * P, FLAST, wd[(FT - 1) * P:FF, m * P:(m + 1) * P].rearrange("(c p) n -> p c n", c=1)),
            ]))
        chunk("dkv", i["w_dkv"], 0, CKV + ROPE)
        chunk("dq", i["w_dq"][0], 0, QL)
        chunk("uk", i["w_uk"].rearrange("c h n -> c (h n)"), 0, H * NOPE)
        for n in range(2):
            chunk(f"uq{n}", i["w_uq"][0], n * HP * (NOPE + ROPE), HP * (NOPE + ROPE))
        chunk("uv", i["w_uv"].rearrange("c h n -> c (h n)"), 0, hv)
        for n in range(2):
            chunk(f"wo{n}", i["w_o_b"][0], n * CW, CW)
        NPRE = len(chunks)
        CH = {name: n for n, (name, _) in enumerate(chunks)}
        slot_of = list(range(SLOTS)) + [n % 4 for n in range(CH["uq0"] + 1 - SLOTS)] + [4, 5, 6, 0]
        arrive, slot_sum, behind = [], [0] * SLOTS, []
        for n, (_, parts) in enumerate(chunks):
            slot_sum[slot_of[n]] += 16 * len(parts)
            arrive.append(slot_sum[slot_of[n]])
            behind.append(([None] + [b for b in range(n) if slot_of[b] == slot_of[n]])[-1])
        release = {}
        FHALF = []
        for n, (_, w) in enumerate(FCH):
            for a in range(0, w, 2 * P):
                if w - a < P:
                    break
                FHALF += [(f"gd{n}", a, min(2 * P, w - a)), (f"ud{n}", a, min(2 * P, w - a))]
                if w - a < 2 * P:
                    break
        FGU = len(FHALF)
        for m in range(DC):
            FHALF += [(f"dd{m}", 0, FT // 2), (f"dd{m}", FT // 2, FT // 2)]
        for h, (name, _, _) in enumerate(FHALF):
            release[CH[name]] = (S["f_lo"], h + 1)

        def fview(tensor, h):
            name, a, w = FHALF[h]
            k = DC if h < FGU else w
            w = w if h < FGU else P
            return tensor[:, 0:k * w].rearrange("p (c n) -> p c n", c=k)

        def f_consumed(h):
            if h < FGU:
                last = min(2 * (h // 2) + 2, FT)
                return (S["ga_full"], GA_FFN + last) if h % 2 == 0 else (S["gd_full"], GD_FFN + last)
            m = (h - FGU) // 2
            return (S["f_used"], m + 1) if (h - FGU) % 2 == 0 else (S["gd_full"], GD_FFN + FT + m + 1)

        def wview(name, k, n):
            s = slot_of[CH[name]]
            return ring[:, s, 0:k * n].rearrange("p (c n) -> p c n", c=k)

        SHARED = 6 + 1 + CE + 2

        def place(h):
            return (h + 2) % HALVES

        def loaded(it, h):
            return (half_full[place(h % IH)], it * (16 * IH // HALVES) + 16 * (h // HALVES + 1))

        def stage(h):
            return h % STAGES

        def turn_at(j):
            return 2 * ORDER.index(("gate", j + 1)) + 1 if j < CE - 1 else 2 * ORDER.index(("down", j - 1)) + 1

        def after(kind, j):
            return STAGES + 2 * (ORDER.index((kind, j)) + 1)

        block = ctx.enter_context(nc.Block())

        @block.tensor
        def _(pe):
            n_ga, n_gd = [0], [0]

            def arrived(name):
                pe.wait_ge(w_full[slot_of[CH[name]]], arrive[CH[name]])

            def out_a():
                if n_ga[0] >= 2:
                    pe.wait_ge(S["ga_free"], n_ga[0] - 1)
                n_ga[0] += 1
                return bank[(n_ga[0] - 1) % 2]

            def out_d():
                if n_gd[0] >= 2:
                    pe.wait_ge(S["gd_free"], n_gd[0] - 1)
                n_gd[0] += 1
                return bank[2 + (n_gd[0] - 1) % 2]

            def done_a(ins, last_of=None):
                ins.then_inc(S["ga_full"], 1)
                if last_of:
                    release[CH[last_of]] = (S["ga_full"], n_ga[0])

            def done_d(ins, last_of=None):
                ins.then_inc(S["gd_full"], 1)
                if last_of:
                    release[CH[last_of]] = (S["gd_full"], n_gd[0])

            def product(o, pairs):
                for n, (w, x) in enumerate(pairs):
                    ins = pe.matmul(o, w, x, start=(n == 0), stop=(n == len(pairs) - 1))
                return ins

            def split_product(o, a, b, start, stop):
                pe.matmul(o, a[0], b[0], start=start, stop=False)
                pe.matmul(o, a[1], b[0], start=False, stop=False)
                return pe.matmul(o, a[0], b[1], start=False, stop=stop)

            def sum_squares(k, chunks_, sq, first):
                if k:
                    pe.wait_ge(S["std_ready"], k)
                for m in range(chunks_):
                    pe.wait_ge(S["sq_ready"], first + m + 1)
                    ins = pe.matmul(bank[7][:, 0:T], ones, sq[:, m, :], start=(m == 0), stop=(m == chunks_ - 1))
                ins.then_inc(S["ss_full"], 1)

            pe.wait_ge(S["ld_const"], 16)
            pe.wait_ge(S["ld_gain"], 16 * len(GAINS))
            pe.transpose(bank[4][:, 0:GROWS], Dh[0][0:GROWS, 0:P], ident[0:GROWS, 0:GROWS]).then_inc(S["gt_full"], 1)
            pe.wait_ge(S["ld_x"], 48)
            for m in range(DC):
                if m >= 2:
                    pe.wait_ge(S["x_ready"], m - 1)
                for t0, tn, tt in TOK:
                    ins = pe.transpose(bank[m % 2][:, t0:t0 + tn], xtok[0:tn, tt, m * P:(m + 1) * P],
                                       ident[0:tn, 0:tn])
                ins.then_inc(S["x_full"], 1)
            sum_squares(0, DC, xn, 0)

            pe.wait_ge(S["x_ready"], DC)
            arrived("k0")
            w = wview("k0", DC, CW)
            for m in range(HP):
                o = out_d()
                for k in range(DC):
                    if m == 0:
                        pe.wait_ge(S["xn_ready"], k + 1)
                    ins = pe.matmul(o[:, 0:T], w[:, k, m * P:(m + 1) * P], xn[:, k, :], start=(k == 0), stop=(k == DC - 1))
                done_d(ins, "k0" if m == HP - 1 else None)
            pe.wait_ge(S["ld_wg"], 16)
            pe.wait_ge(S["gt_ready"], 1)
            product(bank[4][0:H, 0:T], [(wg[:, k, 0:H], xn[:, k, :]) for k in range(DC)])
            product(bank[5][0:H, 0:T], [(wg[:, k, H:2 * H], xn[:, k, :]) for k in range(DC)]).then_inc(S["gates_full"], 1)
            arrived("q0")
            w = wview("q0", DC, CW)
            for m in range(HP):
                o = out_a()
                ins = product(o[:, 0:T], [(w[:, k, m * P:(m + 1) * P], xn[:, k, :]) for k in range(DC)])
                done_a(ins, "q0" if m == HP - 1 else None)
            for m in range(DC):
                name = f"o{m // 4}"
                arrived(name)
                w = wview(name, DC, CW)
                o = out_a()
                ins = product(o[:, 0:T], [(w[:, k, (m % 4) * P:(m % 4 + 1) * P], xn[:, k, :]) for k in range(DC)])
                done_a(ins, name if m % 4 == 3 else None)
            for n in range(2):
                name = f"v{n}"
                arrived(name)
                w = wview(name, DC, CW)
                for t0, tn, tt in TOK:
                    o = out_d()
                    ins = product(o[0:tn, :], [(xn[:, k, t0:t0 + tn], w[:, k, :]) for k in range(DC)])
                    done_d(ins, name if tt == 2 else None)

            pe.wait_ge(S["rows_ready"], 1)
            pe.wait_ge(S["ld_ac"], 16)
            for t0, tn, tt in TOK:
                pe.transpose(bank[4][0:tn, tt * 16:tt * 16 + H], rU[:, t0:t0 + tn], ident[0:H, 0:H])
                pe.transpose(bank[4][0:tn, tt * 16 + H:tt * 16 + 2 * H], rE[:, t0:t0 + tn], ident[0:H, 0:H])
            for j in range(HP):
                pe.matmul(bank[5][:, j * TS:(j + 1) * TS], selp[:, j, :], rZ[:, 0:TS], start=True, stop=True)
                ins = pe.matmul(bank[5][:, HP * TS + j * NB:HP * TS + (j + 1) * NB], selp[:, j, :],
                                rZ[:, TS:TS + NB], start=True, stop=True)
            ins.then_inc(S["uT_full"], 1)

            for t0, tn, tt in TOK:
                o = out_d()
                for j in range(HP):
                    ins = pe.transpose(o[0:tn, j * P:(j + 1) * P], kT[:, j, t0:t0 + tn], ident)
                done_d(ins)

            pe.wait_ge(S["ld_state"], 16 * 16)
            pe.wait_ge(S["qe_ready"], 1)
            pe.wait_ge(S["ga_free"], n_ga[0])
            for h in range(H):
                r, g = (h % 2) * DK, h // 2
                o = bank[(6, 0)[h % 2] + g // 3][0:TS, (g % 3) * (DV + 1):(g % 3 + 1) * (DV + 1)]
                for b in range(NB):
                    ins = pe.matmul(o, qbd[r:r + DK, g, b * TS:(b + 1) * TS], Ce[r:r + DK, g, b, :],
                                    start=(b == 0), stop=(b == NB - 1))
            ins.then_inc(S["inter_full"], 1)
            pe.wait_ge(S["inter_tok"], 1)
            for h in range(H):
                pe.transpose(bank[6][:, h * TS:(h + 1) * TS], itok[:, h, 0:DV], ident[0:TS, 0:TS])
                ins = pe.transpose(bank[7][:, h * TS:(h + 1) * TS], itok[:, h, DV:DV + 1].to_broadcast([TS, P]),
                                   ident[0:TS, 0:TS])
            ins.then_inc(S["inter_full"], 1)

            pe.wait_ge(S["gd_free"], n_gd[0])
            pe.wait_ge(S["e_ready"], 1)
            pe.wait_ge(S["inter_ready"], 1)

            def scores(h):
                if h >= 2:
                    pe.wait_ge(S["D_made"], h - 1)
                    pe.wait_ge(S["W_made"], h - 1)
                r = (h % 2) * DK
                kk, qq = kT[r:r + DK, h // 2, :], qT[r:r + DK, h // 2, :]
                s = bank[2 + h % 2]
                pe.matmul(bank[h % 2][:, 0:T], ident[0:H, h:h + 1].to_broadcast([H, P]), rM, start=True, stop=True)
                pe.matmul(s[:, 0:TP], kk[:, 0:P], qq[:, 0:TP], start=True, stop=True)
                pe.matmul(s[:, TP:TP + P], kk[:, P:TP], qq[:, P:TP], start=True, stop=True)
                pe.matmul(s[0:TS, TP + P:WM], kk[:, TP:T], qq[:, TP:T], start=True, stop=True).then_inc(S["s_full"], 1)

            def attend(h):
                if h:
                    pe.wait_ge(S["nd_read"], h)
                pe.matmul(bank[4][:, 0:T], ident[0:H, h:h + 1].to_broadcast([H, P]), rA, start=True,
                          stop=True).then_inc(S["m_full"], 1)
                pe.wait_ge(S["W_made"], h + 1)
                for o, v0, v1, v2 in ((bank[5], VX[:, 0, h, 0:DV], VX[:, 1, h, 0:DV], VX[0:TS, 2, h, 0:DV]),
                                      (bank[6], ones, ones, ones[0:TS, :])):
                    pe.matmul(o[:, TP:T], v2, Wt[0:TS, TP + P:WM], start=True, stop=True)
                    pe.matmul(o[:, 0:TP], v0, Wt[:, 0:TP], start=True, stop=False)
                    ins = pe.matmul(o[:, P:TP], v1, Wt[:, TP:TP + P], start=False, stop=True)
                ins.then_inc(S["nd_full"], 1)

            scores(0)
            for h in range(H):
                if h + 1 < H:
                    scores(h + 1)
                attend(h)

            pe.wait_ge(S["h_made"], H)
            n_st = 0
            for g in range(HP):
                if n_st >= 4:
                    pe.wait_ge(S["st_free"], n_st - 3)
                o = bank[n_st % 4]
                for hh_ in range(2):
                    h = 2 * g + hh_
                    for s in range(2):
                        ins = pe.matmul(o[0:DK, hh_ * 129:hh_ * 129 + 129], Ke[:, s, h * DK:(h + 1) * DK],
                                        VX[:, s, h, :], start=(s == 0), stop=(s == 1))
                ins.then_inc(S["st_full"], 1)
                n_st += 1
            for b in range(NB):
                pe.wait_ge(S["kd_made"], b + 1)
                for g in range(2):
                    if n_st >= 4:
                        pe.wait_ge(S["st_free"], n_st - 3)
                    o = bank[n_st % 4]
                    for jj in range(2):
                        for par in range(2):
                            h = 2 * (2 * g + jj) + par
                            ins = pe.matmul(o[par * DK:(par + 1) * DK, jj * 129:jj * 129 + 129],
                                            kmb[b % 2][:, h * DK:(h + 1) * DK], VX[0:TS, 2, h, :], start=True, stop=True)
                    ins.then_inc(S["st_full"], 1)
                    n_st += 1

            for h in range(H):
                pe.wait_ge(S["hsq_ready"], h + 1)
                if h >= 2:
                    pe.wait_ge(S["y_ready"], h - 1)
                pe.matmul(bank[4 + h % 2][:, 0:T], ones, Dh[h % 2][:, 0:T], start=True, stop=True).then_inc(S["hss_full"], 1)
            pe.wait_ge(S["st_free"], n_st)
            for m in range(DC):
                name = f"out{m // 4}"
                arrived(name)
                w = wview(name, DC, CW)
                o = out_d()
                for k in range(DC):
                    if m == 0:
                        pe.wait_ge(S["y_ready"], k + 1)
                    ins = pe.matmul(o[:, 0:T], w[:, k, (m % 4) * P:(m % 4 + 1) * P], oT[:, k, :], start=(k == 0), stop=(k == DC - 1))
                done_d(ins, name if m % 4 == 3 else None)

            sum_squares(1, DC, xn, DC)
            for h in range(FGU):
                pe.wait_ge(S["f_lo"], h + 1)
                w = [fview(wpart[:, h % STAGES, part, :], h) for part in range(2)]
                for q in range((FHALF[h][2] + P - 1) // P):
                    f = 2 * (h // 2) + q
                    rows = P if f < FT - 1 else FLAST
                    o = out_a() if h % 2 == 0 else out_d()
                    for k in range(DC):
                        if f == 0 and h == 0:
                            pe.wait_ge(S["xp_lo"], k + 1)
                        ins = split_product(o[0:rows, 0:T], [p[:, k, q * P:q * P + rows] for p in w],
                                            [xp[:, part, k, :] for part in range(2)], k == 0, k == DC - 1)
                    (done_a if h % 2 == 0 else done_d)(ins)
            for h in range(FGU, len(FHALF)):
                pe.wait_ge(S["f_lo"], h + 1)
                w = [fview(wpart[:, h % STAGES, part, :], h) for part in range(2)]
                first = (h - FGU) % 2 == 0
                if first:
                    o = out_d()
                for q in range(FT // 2):
                    f = FHALF[h][1] + q
                    rows = P if f < FT - 1 else FLAST
                    if h < FGU + 2:
                        pe.wait_ge(S["hp_lo"], f + 1)
                    ins = split_product(o[:, 0:T], [p[0:rows, q, :] for p in w],
                                        [hp[0:rows, part, f, :] for part in range(2)], f == 0, f == FT - 1)
                if first:
                    ins.then_inc(S["f_used"], 1)
                else:
                    done_d(ins)

            sum_squares(2, DC, xn, 2 * DC)
            arrived("dkv")
            w = wview("dkv", DC, CKV + ROPE)
            pe.wait_ge(S["xn_ready"], 3 * DC)
            for m in range(CT + 1):
                rows = P if m < CT else ROPE
                o = out_d()
                ins = product(o[0:rows, 0:T], [(w[:, k, m * P:m * P + rows], hn[:, k, :]) for k in range(DC)])
                done_d(ins, "dkv" if m == CT else None)
            pe.wait_ge(S["xn_ready"], 4 * DC)
            arrived("dq")
            w = wview("dq", DC, QL)
            pe.wait_ge(S["gd_free"], GD_CQ)
            pe.matmul(bank[4][0:ROPE, 0:T], c("rot", ROPE), rtmp[0], start=True, stop=True).then_inc(S["rot_full"], 1)
            sum_squares(3, CT, ckvT, 3 * DC)
            pe.wait_ge(S["ckv_ready"], 1)
            for m in range(QT):
                o = out_d()
                ins = product(o[:, 0:T], [(w[:, k, m * P:(m + 1) * P], xn[:, k, :]) for k in range(DC)])
                done_d(ins, "dq" if m == QT - 1 else None)
            arrived("uk")
            w = wview("uk", CT, H * NOPE)
            for g in range(HP):
                o = out_d()
                for hh_ in range(2):
                    for k in range(CT):
                        h = 2 * g + hh_
                        ins = pe.transpose(o[:, (hh_ * CT + k) * P:(hh_ * CT + k + 1) * P],
                                           w[:, k, h * NOPE:(h + 1) * NOPE], ident)
                done_d(ins, "uk" if g == HP - 1 else None)
            sum_squares(4, QT, cq, 3 * DC + CT)
            for t0, tn, tt in TOK:
                o = out_d()
                for k in range(CT):
                    pe.transpose(o[0:tn, k * P:(k + 1) * P], ckvT[:, k, t0:t0 + tn], ident)
                ins = pe.transpose(o[0:tn, CKV:CKV + ROPE], krT[:, t0:t0 + tn], ident[0:ROPE, 0:ROPE])
                done_d(ins)
            pe.wait_ge(S["cq_ready"], 1)
            pe.wait_ge(S["kr_ready"], 1)

            def up_q(h):
                name = f"uq{h // HP}"
                arrived(name)
                w = wview(name, QT, HP * (NOPE + ROPE))
                a = (h % HP) * (NOPE + ROPE)
                o = out_a()
                done_a(product(o[:, 0:T], [(w[:, k, a:a + NOPE], cq[:, k, :]) for k in range(QT)]))
                o = out_a()
                ins = product(o[0:ROPE, 0:T], [(w[:, k, a + NOPE:a + NOPE + ROPE], cq[:, k, :]) for k in range(QT)])
                done_a(ins, name if h % HP == HP - 1 else None)

            def latent_q(h):
                pe.wait_ge(S["ga_free"], ga_q + 2 * (h + 1))
                if h:
                    pe.wait_ge(S["qr_ready"], h)
                pe.matmul(bank[4][0:ROPE, 0:T], c("rot", ROPE), rtmp[h % 2], start=True, stop=True).then_inc(S["rot_full"], 1)
                for k in range(CT):
                    o = out_d()
                    done_d(pe.matmul(o[:, 0:T], ukT[:, h, k * P:(k + 1) * P], qn[h % 2], start=True, stop=True))

            ga_q = n_ga[0]
            up_q(0)
            for h in range(H):
                if h + 1 < H:
                    up_q(h + 1)
                latent_q(h)
            pe.wait_ge(S["qr_ready"], H)
            pe.wait_ge(S["gd_free"], n_gd[0])

            units = [(h, q) for h in range(H) for q in range(2)]

            def p_scores(u):
                h, q = units[u]
                if u >= 2:
                    pe.wait_ge(S["p_exp"], u - 1)
                keys = (q + 1) * P
                o = bank[5 + u % 2][:, 0:keys]
                for k in range(CT):
                    pe.matmul(o, qlat[:, k, h, q * P:(q + 1) * P], ckvT[:, k, 0:keys], start=(k == 0), stop=False)
                pe.matmul(o, qrope[:, h, q * P:(q + 1) * P], krT[:, 0:keys], start=False, stop=True).then_inc(S["sc_full"], 1)

            def p_attend(u):
                h, q = units[u]
                pe.wait_ge(S["p_ready"], u + 1)
                for s in range(q + 1):
                    ins = pe.transpose(bank[7][:, s * P:(s + 1) * P], prob2[u % 2][:, s * P:(s + 1) * P], ident)
                ins.then_inc(S["pt_full"], 1)
                if u + 2 < len(units):
                    p_scores(u + 2)
                pe.wait_ge(S["pt_ready"], u + 1)
                if u:
                    pe.wait_ge(S["ol_ready"], u)
                for k in range(CT):
                    for s in range(q + 1):
                        ins = pe.matmul(bank[4][:, k * P:(k + 1) * P], ctok[:, s, k * P:(k + 1) * P],
                                        PT[:, s * P:(s + 1) * P], start=(s == 0), stop=(s == q))
                ins.then_inc(S["ol_full"], 1)

            p_scores(0)
            p_scores(1)
            for u in range(len(units)):
                p_attend(u)

            NU = len(units)

            def cache_transposes(b):
                pe.wait_ge(ck_full[b % BUFS], 16 * NPG * (b // BUFS + 1))
                for g in range(6):
                    n = 6 * b + g
                    if g == 2 * CT:
                        pe.wait_ge(cr_full[b % BUFS], 16 * NPG * (b // BUFS + 1))
                    if n >= 2:
                        pe.wait_ge(S["tpa_free"] if n % 2 == 0 else S["tpd_free"], n // 2)
                    part, half = g // 2, g % 2
                    for pg in range(4):
                        page = half * 4 + pg
                        src = ctk[b % BUFS][:, page, part * P:(part + 1) * P] if part < CT else crk[b % BUFS][:, page, :]
                        rows = P if part < CT else ROPE
                        ins = pe.transpose(bank[n % 2][0:rows, pg * P:(pg + 1) * P], src, ident)
                    ins.then_inc(S["tp_full"], 1)

            def s_scores(b):
                pe.wait_ge(S["tpa_free"], 3 * (b + 1))
                pe.wait_ge(S["tpd_free"], 3 * (b + 1))
                pe.wait_ge(S["p_exp"], NU + b)
                if b == 0:
                    pe.wait_ge(S["pt_ready"], NU)
                for a, n, kv, kr in ((0, 512, cacheT[:, :, 0:512], cacheR[:, 0:512]),
                                     (512, 512, cacheT[:, :, 512:PAST], cacheR[:, 512:PAST]),
                                     (PAST, TS, ckvT[:, :, TP:T], krT[:, TP:T])):
                    for k in range(CT):
                        pe.matmul(wide[0:TS, a:a + n], qls[:, k, b, :], kv[:, k, :], start=(k == 0), stop=False)
                    ins = pe.matmul(wide[0:TS, a:a + n], qrs[:, b, :], kr, start=False, stop=True)
                ins.then_inc(S["sc_full"], 1)

            def s_attend(b):
                pe.wait_ge(S["p_exp"], NU + b + 1)
                for pg in range(NPG + 1):
                    rows = P if pg < NPG else TS
                    ins = pe.transpose(bank[4][0:rows, pg * TS:(pg + 1) * TS], prob[0:TS, pg * P:pg * P + rows],
                                       ident[0:TS, 0:TS])
                ins.then_inc(S["pt_full"], 1)
                pe.wait_ge(S["pt_ready"], NU + b + 1)
                if b:
                    pe.wait_ge(S["os_ready"], b)
                for pg in range(NPG + 1):
                    kv = ctk[b % BUFS][:, pg, :] if pg < NPG else ctok[0:TS, 2, 0:CKV]
                    rows = P if pg < NPG else TS
                    ins = pe.matmul(bank[3][0:TS, 0:CKV], PT[0:rows, pg * TS:(pg + 1) * TS], kv,
                                    start=(pg == 0), stop=(pg == NPG))
                ins.then_inc(S["av_full"], 1)

            def s_turn(b):
                pe.wait_ge(S["os_ready"], b + 1)
                if b:
                    pe.wait_ge(S["ol_ready"], NU + b)
                for k in range(CT):
                    ins = pe.transpose(bank[2][:, k * TS:(k + 1) * TS], osb[:, k * P:(k + 1) * P], ident[0:TS, 0:TS])
                ins.then_inc(S["ol_full"], 1)

            pe.wait_ge(S["ol_ready"], NU)
            cache_transposes(0)
            for b in range(NB):
                s_scores(b)
                if b:
                    s_turn(b - 1)
                if b + 1 < NB:
                    cache_transposes(b + 1)
                s_attend(b)
            s_turn(NB - 1)
            pe.wait_ge(S["ol_ready"], NU + NB)
            pe.wait_ge(S["tpa_free"], 3 * NB)
            arrived("uv")
            w = wview("uv", CT, hv)
            for h in range(H):
                o = out_d()
                product(o[:, TP:T].rearrange("p (b s) -> p b s", s=NS),
                        [(w[:, k, h * DV:(h + 1) * DV], qls[:, k, :, h * NS:(h + 1) * NS]) for k in range(CT)])
                ins = product(o[:, 0:TP], [(w[:, k, h * DV:(h + 1) * DV], qlat[:, k, h, :]) for k in range(CT)])
                done_d(ins, "uv" if h == H - 1 else None)
            heads_out = n_gd[0]
            for m in range(DC):
                name = f"wo{m // 4}"
                arrived(name)
                w = wview(name, DC, CW)
                o = out_d()
                for k in range(DC):
                    if m == 0:
                        pe.wait_ge(S["gd_free"], heads_out - DC + k + 1)
                    ins = pe.matmul(o[:, 0:T], w[:, k, (m % 4) * P:(m % 4 + 1) * P], xn[:, k, :], start=(k == 0), stop=(k == DC - 1))
                done_d(ins, name if m % 4 == 3 else None)

            sum_squares(5, DC, acc_sq, 3 * DC + CT + QT)
            pe.wait_ge(S["xn_ready"], 5 * DC)
            pe.wait_ge(S["ld_wr"], 16)
            for t0, tn, tt in TOK:
                ins = product(bank[4][0:tn, tt * E:(tt + 1) * E], [(xn[:, k, t0:t0 + tn], wg[:, k, 0:E]) for k in range(DC)])
            ins.then_inc(S["lg_full"], 1)
            for src in (xn, xT):
                for t0, tn, tt in TOK:
                    for half in range(2):
                        o = out_d()
                        for q in range(4):
                            ins = pe.transpose(o[0:tn, q * P:(q + 1) * P], src[:, half * 4 + q, t0:t0 + tn], ident)
                        done_d(ins)
            pe.wait_ge(S["gd_free"], n_gd[0])
            pe.wait_ge(S["mask_ready"], 1)
            pe.wait_ge(S["ld_gf"], 32)
            tri = mc("tri")
            for t0, tn, tt in TOK:
                ins = product(bank[4][:, 32 + tt * E:32 + (tt + 1) * E],
                              [(ones, mk[:, s, :]) for s in range(tt)] + [(tri, mk[:, tt, :])])
            ins = product(bank[4][:, 64:64 + E], [(ones, mk[:, s, :]) for s in range(3)])
            ins.then_inc(S["rank_full"], 1)

            def gather(half):
                for q in range(4):
                    m = half * 4 + q
                    for t0, tn, tt in TOK:
                        ins = pe.matmul(bank[6 + half][:, q * P:(q + 1) * P], xtk[0:tn, tt, m * P:(m + 1) * P],
                                        Pm[0:tn, tt, :], start=(tt == 0), stop=(tt == 2))
                ins.then_inc(S["misc_full"], 1)

            pe.wait_ge(S["p_made"], 1)
            gather(0)
            gather(1)
            pe.wait_ge(S["tables_ready"], 1)
            n_items = pe.value_load(ints[0:1, 0:1], min_val=E, max_val=ITEMS)
            def free(it, use):
                if use == 1:
                    pe.wait_ge(S["xg_ready"], it + 1)
                else:
                    pe.wait_ge(S["misc_free"], it * (SHARED - 1) + max(1, use))

            def combine(it, tile):
                t0, tn, tt = TOK[tile]
                for half in range(2):
                    n = 2 * tile + half
                    free(it, n)
                    split_product(bank[6 + n % 2][0:tn, :], [ptp[:, part, t0:t0 + tn] for part in range(2)],
                                  [yp[:, part, half * CW:(half + 1) * CW] for part in range(2)],
                                  True, True).then_inc(S["misc_full"], 1)

            with pe.Fori(0, n_items) as it:
                def parts(h, a):
                    pe.wait_ge(S["lo_ready"], it * IH + h + 1)
                    return [wpart[:, stage(h), part, :].rearrange("p (c n) -> p c n", c=a) for part in range(2)]

                def rows(kind, j, o, between=None):
                    for half in range(2):
                        if half and between:
                            between()
                        w = parts(2 * ORDER.index((kind, j)) + half, DC // 2)
                        for q in range(DC // 2):
                            m = half * DC // 2 + q
                            ins = split_product(o, [x[:, m, :] for x in xg], [p[:, q, :] for p in w], m == 0, m == DC - 1)
                        ins.then_inc(S["used"], 1)

                def gate(j, between=None):
                    pe.wait_ge(S["gu_done"], it * CE + 1 + max(0, j - 1))
                    rows("gate", j, bank[j % 2][:, :], between)

                def up(j, between=None):
                    rows("up", j, bank[2 + j % 2][:, :], between)

                def turn(j):
                    pe.wait_ge(S["gu_done"], it * CE + 1 + j + 1)
                    free(it, 7 + j)
                    for q in range(KD):
                        ins = pe.transpose(bank[6 + (1 + j) % 2][:, q * P:(q + 1) * P], hh[j % 2][:, q * P:(q + 1) * P], ident)
                    ins.then_inc(S["misc_full"], 1)

                def down(j):
                    pe.wait_ge(S["misc_free"], it * (SHARED - 1) + j + 9)
                    for half in range(2):
                        w = parts(2 * ORDER.index(("down", j)) + half, KD // 2)
                        for q in range(KD // 2):
                            m = half * KD // 2 + q
                            for n in range(2):
                                ins = split_product(bank[4 + n][:, :],
                                                    [hhp[:, j % 2, part, m * P:(m + 1) * P] for part in range(2)],
                                                    [p[:, q, n * CW:(n + 1) * CW] for p in w],
                                                    j == 0 and m == 0, j == CE - 1 and m == KD - 1)
                        ins.then_inc(S["used"], 1)

                def gates():
                    free(it, 6)
                    for t0, tn, tt in TOK:
                        ins = pe.transpose(bank[6][:, t0:t0 + tn], Pg[0:tn, tt, :], ident[0:tn, 0:tn])
                    ins.then_inc(S["misc_full"], 1)

                pe.wait_ge(S["misc_free"], it * (SHARED - 1) + 1)
                gate(0, lambda: pe.wait_ge(S["xg_ready"], it + 1))
                pe.wait_ge(S["y_free"], it + 1)
                combine(it, 0)
                up(0, lambda: combine(it, 1))
                combine(it, 2)
                for j in range(CE - 1):
                    gate(j + 1, gates if j == 0 else None)
                    turn(j)
                    up(j + 1)
                    down(j)
                turn(CE - 1)
                pe.wait_ge(S["p_made"], it + 2)
                free(it, 14)
                gather(0)
                down(CE - 1)
                free(it, 15)
                gather(1)
            pe.wait_ge(S["y_free"], n_items + 1)
            for tile in range(3):
                combine(n_items, tile)

        @block.vector
        def _(v):
            chain = [0]

            def link(ins):
                chain[0] += 1
                ins.then_inc(S["dchain"], 1)
                v.wait_ge(S["dchain"], chain[0])

            def low(dst, src, high):
                return v.tensor_tensor(dst, src, high.bitcast(F32), ALU.subtract)

            n_gd = [0]

            def in_d():
                n_gd[0] += 1
                v.wait_ge(S["gd_full"], n_gd[0])
                return bank[2 + (n_gd[0] - 1) % 2]

            def free_d(ins):
                ins.then_inc(S["gd_free"], 1)

            def normalise(k, chunks_, src, gname, dst, ready, first=True, every=True, m0=0):
                if first:
                    v.wait_ge(S["std_ready"], k + 1)
                    link(v.reciprocal(stdv(k), stdv(k)))
                for m in range(m0, m0 + chunks_):
                    ins = v.scalar_tensor_tensor(out=dst[:, m, :], in0=src[:, m, :], scalar=gain(gname, m),
                                                 in1=stdv(k), op0=ALU.mult, op1=ALU.mult)
                    if every or m == m0 + chunks_ - 1:
                        ins.then_inc(S[ready], 1)

            v.wait_ge(S["gt_full"], 1)
            v.tensor_copy(gT[:, :], bank[4][:, 0:GROWS]).then_inc(S["gt_ready"], 1)
            v.wait_ge(S["ld_tiny"], 32)
            v.tensor_scalar(tiny[:, 2:4], tiny[:, 0:2], 1.0 / CAP, None, ALU.mult).then_inc(S["bg_ready"], 1)
            for m in range(DC):
                v.wait_ge(S["x_full"], m + 1)
                v.tensor_copy(xT[:, m, :], bank[m % 2][:, 0:T]).then_inc(S["x_ready"], 1)
            v.wait_ge(S["gt_ready"], 1)
            normalise(0, DC, xT, "g_norm_a", xn, "xn_ready")
            link(v.memset(VX[:, :, :, DV:DV + 1], 1.0))
            link(v.memset(uT[:, :, :], 0.0))
            link(v.memset(rZ[:, :], 0.0))
            for m in range(HP):
                o = in_d()
                free_d(v.tensor_copy(kT[:, m, :], o[:, 0:T]))

            v.wait_ge(S["lf_ready"], 1)
            m0 = tiny[:, 8:16]
            link(v.tensor_scalar(rU, rU, CAP, None, ALU.mult))
            link(v.tensor_scalar(rE, rE, -1.0, None, ALU.mult))
            link(v.tensor_tensor_scan(rA[:, 0:TP], rE[:, 0:TP], rZ[:, 0:TP], 0.0, ALU.add, ALU.add))

            def step(row, t):
                return row[:, TP:T].rearrange("p (b s) -> p b s", s=NS)[:, :, t]

            link(v.tensor_copy(step(rA, 0), step(rE, 0)))
            for t in range(1, NS):
                link(v.tensor_tensor(step(rA, t), step(rA, t - 1), step(rE, t), ALU.add))
            link(v.tensor_tensor(rU, rU, rA, ALU.subtract))
            link(v.tensor_tensor_scan(rM[:, 0:TP], rU[:, 0:TP], rU[:, 0:TP], 0.0, ALU.max, ALU.max))
            link(v.tensor_tensor(step(rM, 0), m0, step(rU, 0), ALU.max))
            for t in range(1, NS):
                link(v.tensor_tensor(step(rM, t), step(rM, t - 1), step(rU, t), ALU.max))
            link(v.tensor_scalar(rE[:, 0:TP], rU[:, 0:TP], rM[:, TP - 1:TP], None, ALU.subtract))
            for t in range(NS):
                link(v.tensor_tensor(step(rE, t), step(rU, t), step(rM, NS - 1), ALU.subtract))
            zt = rZ[:, 0:TS].rearrange("p (b s) -> p b s", s=NS)
            for t in range(NS):
                link(v.tensor_tensor(zt[:, :, t], m0, step(rM, t), ALU.subtract))
            link(v.tensor_tensor(rZ[:, TS:TS + NB], m0, step(rM, NS - 1), ALU.subtract))
            link(v.tensor_tensor(rA, rA, rM, ALU.add))
            link(v.tensor_copy(tiny[:, 16:17], rA[:, TP - 1:TP]))
            link(v.tensor_copy(tiny[:, 17:17 + NB], step(rA, NS - 1)))
            link(v.tensor_scalar(rA, rA, -1.0, None, ALU.mult))
            v.tensor_scalar(rM, rM, -1.0, None, ALU.mult).then_inc(S["rows_ready"], 1)

            for n in range(2):
                for t0, tn, tt in TOK:
                    o = in_d()
                    free_d(v.tensor_copy(VX[0:tn, tt, 4 * n:4 * n + 4, 0:DV],
                                         o[0:tn, :].rearrange("p (h n) -> p h n", h=4)))
            v.wait_ge(S["uT_full"], 1)
            v.tensor_copy(uT[:, 0:2, :], bank[4][:, 0:32].rearrange("p (a b) -> p a b", a=2)).then_inc(S["uT_ready"], 1)
            v.tensor_copy(uT[0:TS, 2, :], bank[4][0:TS, 32:48]).then_inc(S["uT_ready"], 1)
            v.wait_ge(S["e_ready"], 1)
            v.wait_ge(S["ga_free"], HP)
            link(v.memset(xflat[:, 0:HP * 288], 0.0))
            v.tensor_tensor(qdiag, qT[:, :, TP:T].rearrange("p j (b s) -> p j b s", s=NS),
                            eI[:, :, :].rearrange("p j (b s) -> p j b s", s=NS), ALU.mult).then_inc(S["qe_ready"], 1)
            for t0, tn, tt in TOK:
                o = in_d()
                free_d(v.tensor_tensor(Ke[0:tn, tt, :].rearrange("p (h k) -> p h k", h=H),
                                       o[0:tn, :].rearrange("p (h k) -> p h k", h=H),
                                       uT[0:tn, tt, H:2 * H].unsqueeze(2).to_broadcast([tn, H, DK]), ALU.mult))
            v.wait_ge(S["inter_full"], 1)
            for par in range(2):
                for g0, g1 in ((0, 3), (3, HP)):
                    ins = v.tensor_copy(itok.rearrange("p (g a) n -> p g a n", a=2)[:, g0:g1, par, :],
                                        bank[(6, 0)[par] + g0 // 3][0:TS, 0:(g1 - g0) * (DV + 1)].rearrange(
                                            "p (g n) -> p g n", n=DV + 1))
            ins.then_inc(S["inter_tok"], 1)
            v.wait_ge(S["inter_full"], 2)
            v.tensor_copy(inN.rearrange("p a b -> p (a b)"), bank[6][:, 0:H * TS])
            link(v.tensor_copy(inD.rearrange("p a b -> p (a b)"), bank[7][:, 0:H * TS]))
            v.memset(den[:, 0:1], 0.0).then_inc(S["inter_ready"], 1)

            def decay(h):
                v.wait_ge(S["s_full"], h + 1)
                if h >= 2:
                    v.wait_ge(S["W_made"], h - 1)
                d, m = Dh[h % 2], bank[h % 2]
                for a, n, m_at, tt in ((0, TP, 0, 0), (TP, P, P, 1), (TP + P, TS, TP, 2)):
                    ins = v.scalar_tensor_tensor(out=d[:, a:a + n], in0=m[:, m_at:m_at + n], scalar=uT[:, tt, h:h + 1],
                                                 in1=cmask[:, a:a + n], op0=ALU.add, op1=ALU.min)
                ins.then_inc(S["D_made"], 1)

            v.wait_ge(S["ld_ac"], 16)
            v.wait_ge(S["uT_ready"], 2)
            decay(0)
            decay(1)

            def weights(h):
                v.wait_ge(S["exp_done"], h + 1)
                s = bank[2 + h % 2]
                v.tensor_tensor(Wt[:, 0:TP + P], Dh[h % 2][:, 0:TP + P], s[:, 0:TP + P], ALU.mult)
                v.tensor_tensor(Wt[0:TS, TP + P:WM], Dh[h % 2][0:TS, TP + P:WM], s[0:TS, TP + P:WM],
                                ALU.mult).then_inc(S["W_made"], 1)

            weights(0)
            for h in range(H):
                v.wait_ge(S["nd_full"], h + 1)
                if h + 1 < H:
                    weights(h + 1)
                if h:
                    v.wait_ge(S["h_made"], h)
                v.tensor_copy(den[:, 0:TP], bank[6][:, 0:TP])
                v.tensor_tensor(den[:, TP:T], bank[6][:, TP:T], inD[:, h, :], ALU.add)
                v.tensor_copy(xn[:, h, 0:TP], bank[5][:, 0:TP])
                link(v.tensor_tensor(xn[:, h, TP:T], bank[5][:, TP:T], inN[:, h, :], ALU.add))
                v.wait_ge(S["em_done"], h + 1)
                link(v.scalar_tensor_tensor(out=den, in0=den, scalar=-1.0, in1=den, op0=ALU.mult, op1=ALU.max))
                v.tensor_tensor(den, den, bank[4][:, 0:T], ALU.max).then_inc(S["nd_read"], 1)
                if h + 2 < H:
                    decay(h + 2)
                v.wait_ge(S["nd_read"], h + 1)
                link(v.reciprocal(den, den))
                v.tensor_tensor(xn[:, h, :], xn[:, h, :], den, ALU.mult).then_inc(S["h_made"], 1)

            n_st = 0
            for g in range(HP):
                n_st += 1
                v.wait_ge(S["st_full"], n_st)
                v.tensor_copy(Cp[:, 2 * g:2 * g + 2, :],
                              bank[(n_st - 1) % 4][0:DK, 0:258].rearrange("p (a b) -> p a b", a=2)).then_inc(S["st_free"], 1)

            def mask_keys(b):
                v.tensor_scalar(kmb[b % 2], Ke[0:TS, 2, :], c("bsel", TS)[:, b:b + 1], None, ALU.mult).then_inc(S["kd_made"], 1)

            v.wait_ge(S["gd_free"], n_gd[0])
            mask_keys(0)
            mask_keys(1)
            for b in range(NB):
                for g in range(2):
                    n_st += 1
                    v.wait_ge(S["st_full"], n_st)
                    o = bank[(n_st - 1) % 4]
                    for jj in range(2):
                        j = 2 * g + jj
                        ins = v.scalar_tensor_tensor(out=Ce[:, j, b, :], in0=Ce[:, j, b, :],
                                                     scalar=eC[:, j * NB + b:j * NB + b + 1],
                                                     in1=o[:, jj * 129:jj * 129 + 129], op0=ALU.mult, op1=ALU.add)
                    ins.then_inc(S["st_free"], 1)
                if b + 2 < NB:
                    mask_keys(b + 2)

            for h in range(H):
                v.wait_ge(S["hstd_ready"], h + 1)
                link(v.reciprocal(den, bank[4 + h % 2][:, 0:T]))
                link(v.scalar_tensor_tensor(out=xn[:, h, :], in0=xn[:, h, :], scalar=gain("g_head_a", h), in1=den,
                                            op0=ALU.mult, op1=ALU.mult))
                v.tensor_tensor(oT[:, h, :], oT[:, h, :], xn[:, h, :], ALU.mult).then_inc(S["y_ready"], 1)

            def add_residual(m):
                o = in_d()
                free_d(v.tensor_tensor(xT[:, m, :], xT[:, m, :], o[:, 0:T], ALU.add))

            def f_split(h):
                name, a0, w = FHALF[h]
                v.wait_ge(S["f_hi"], h + 1)
                dst, high = (fview(wpart[:, h % STAGES, part, :], h) for part in (1, 0))
                if h < FGU:
                    ins = low(dst, wview(name, DC, FCH[int(name[2:])][1])[:, :, a0:a0 + w], high)
                else:
                    src = wview(name, FT, P)[:, a0:a0 + w, :]
                    if a0:
                        low(dst[:, 0:w - 1, :], src[:, 0:w - 1, :], high[:, 0:w - 1, :])
                        ins = low(dst[0:FLAST, w - 1, :], src[0:FLAST, w - 1, :], high[0:FLAST, w - 1, :])
                    else:
                        ins = low(dst, src, high)
                ins.then_inc(S["f_lo"], 1)

            for m in range(DC):
                add_residual(m)
                if m in (0, 1, 5):
                    f_split(min(m, 2))
            for m in range(DC):
                normalise(1, 1, xT, "g_ffn_d", xn, "xn_ready", first=(m == 0), m0=m)
                if m:
                    v.wait_ge(S["xp_hi"], m)
                    low(xp[:, 1, m - 1, :], xn[:, m - 1, :], xp[:, 0, m - 1, :]).then_inc(S["xp_lo"], 1)
            v.wait_ge(S["xp_hi"], DC)
            low(xp[:, 1, DC - 1, :], xn[:, DC - 1, :], xp[:, 0, DC - 1, :]).then_inc(S["xp_lo"], 1)
            v.wait_ge(S["stored"], 16 * STORES_A)

            for h in range(len(FHALF)):
                if h >= STAGES:
                    f_split(h)
                if h % 2 and 3 <= h < FGU + 2:
                    tiles = [(f, P if f < FT - 1 else FLAST) for f in (h - 3, h - 2)]
                    for f, rows in tiles:
                        o = in_d()
                        v.wait_ge(S["ga_free"], GA_FFN + f + 1)
                        free_d(v.tensor_tensor(sg[f % 3][0:rows, :], sg[f % 3][0:rows, :], o[0:rows, 0:T], ALU.mult))
                    for f, rows in tiles:
                        v.wait_ge(S["hp_hi"], f + 1)
                        low(hp[0:rows, 1, f, :], sg[f % 3][0:rows, :], hp[0:rows, 0, f, :]).then_inc(S["hp_lo"], 1)
                if h % 2 and h >= FGU + 3:
                    add_residual((h - FGU - 3) // 2)
            add_residual(DC - 1)

            normalise(2, DC, xT, "g_kv", hn, "xn_ready")
            normalise(2, DC, xT, "g_norm_b", xn, "xn_ready", first=False)
            for m in range(CT):
                o = in_d()
                free_d(v.tensor_copy(raw[:, m, :], o[:, 0:T]))
            o = in_d()
            free_d(v.tensor_copy(rtmp[0], o[0:ROPE, 0:T]))

            def rotate(n, src):
                v.wait_ge(S["rot_full"], n)
                v.tensor_tensor(rt2, bank[4][0:ROPE, 0:T], c("sin", ROPE), ALU.mult)
                link(v.tensor_tensor(src, src, c("cos", ROPE), ALU.mult))

            rotate(1, rtmp[0])
            v.tensor_tensor(krT, rtmp[0], rt2, ALU.add).then_inc(S["kr_ready"], 1)
            normalise(3, CT, raw, "g_ckv", ckvT, "ckv_ready", every=False)
            for m in range(QT):
                o = in_d()
                if m == 0:
                    v.wait_ge(S["ckv_ready"], 1)
                free_d(v.tensor_copy(raw[:, m, :], o[:, 0:T]))
            for g in range(HP):
                o = in_d()
                free_d(v.tensor_copy(ukT[:, 2 * g:2 * g + 2, :], o[:, :].rearrange("p (a b) -> p a b", a=2)))
            normalise(4, QT, raw, "g_q", cq, "cq_ready", every=False)
            for t0, tn, tt in TOK:
                o = in_d()
                free_d(v.tensor_copy(ctok[0:tn, tt, :], o[0:tn, 0:CKV + ROPE]))
            for h in range(H):
                rt_ = rtmp[h % 2]
                rotate(2 + h, rt_)
                v.tensor_tensor(qrope[:, h, :], rt_[:, 0:TP], rt2[:, 0:TP], ALU.add)
                v.tensor_tensor(qrs[:, :, h * NS:(h + 1) * NS], rt_[:, TP:T].rearrange("p (b s) -> p b s", s=NS),
                                rt2[:, TP:T].rearrange("p (b s) -> p b s", s=NS), ALU.add).then_inc(S["qr_ready"], 1)
                for k in range(CT):
                    o = in_d()
                    v.tensor_copy(qlat[:, k, h, :], o[:, 0:TP])
                    free_d(v.tensor_copy(qls[:, k, :, h * NS:(h + 1) * NS],
                                         o[:, TP:T].rearrange("p (b s) -> p b s", s=NS)))

            def softmax_max(n, s, rows, mask_at, mask):
                mx, nb = (cols[0:rows, 4 * k + n % 2:4 * k + n % 2 + 1] for k in range(2))
                v.wait_ge(S["sc_full"], n + 1)
                m = s[:, mask_at:mask_at + mask.shape[-1]]
                link(v.tensor_tensor(m, m, mask, ALU.add))
                link(v.reduce_max(mx, s, AX.X))
                v.tensor_scalar(nb, mx, -SCALE, None, ALU.mult).then_inc(S["max_ready"], 1)

            def reciprocal_sum(n, rows):
                sm = cols[0:rows, 8 + n % 2:9 + n % 2]
                v.wait_ge(S["p_exp"], n + 1)
                link(v.reciprocal(sm, sm))
                return sm

            units = [(h, q) for h in range(H) for q in range(2)]

            def prompt_max(u):
                q = units[u][1]
                softmax_max(u, bank[5 + u % 2][:, 0:(q + 1) * P], P, q * P, c("pmask"))

            prompt_max(0)
            prompt_max(1)
            for u, (h, q) in enumerate(units):
                keys = (q + 1) * P
                p = prob2[u % 2][:, 0:keys]
                v.tensor_scalar(p, p, reciprocal_sum(u, P), None, ALU.mult).then_inc(S["p_ready"], 1)
                v.wait_ge(S["pt_full"], u + 1)
                v.tensor_copy(PT[:, 0:keys], bank[7][:, 0:keys]).then_inc(S["pt_ready"], 1)
                if u + 2 < len(units):
                    prompt_max(u + 2)
                v.wait_ge(S["ol_full"], u + 1)
                v.tensor_copy(qlat[:, :, h, q * P:(q + 1) * P],
                              bank[4][:, 0:CT * P].rearrange("p (a b) -> p a b", a=CT)).then_inc(S["ol_ready"], 1)
            NU = len(units)

            def cache_evac(b):
                for g in (1, 3, 5):
                    n = 6 * b + g
                    v.wait_ge(S["tp_full"], n + 1)
                    part, half = g // 2, g % 2
                    if part < CT:
                        ins = v.tensor_copy(cacheT[:, part, half * 512:(half + 1) * 512], bank[1][:, :])
                    else:
                        ins = v.tensor_copy(cacheR[:, half * 512:(half + 1) * 512], bank[1][0:ROPE, :])
                    ins.then_inc(S["tpd_free"], 1)

            def turned(b):
                v.wait_ge(S["ol_full"], NU + b + 1)
                v.tensor_copy(qls[:, :, b, :], bank[2][:, 0:CT * TS].rearrange(
                    "p (a n) -> p a n", a=CT)).then_inc(S["ol_ready"], 1)

            cache_evac(0)
            for b in range(NB):
                u = NU + b
                softmax_max(u, wide[0:TS, 0:PAST + TS], TS, PAST,
                            c("smask", TS)[:, (NB - 1 - b) * NS:(NB - 1 - b) * NS + TS])
                if b:
                    turned(b - 1)
                if b + 1 < NB:
                    cache_evac(b + 1)
                rs = reciprocal_sum(u, TS)
                v.wait_ge(S["pt_full"], u + 1)
                v.tensor_copy(PT[:, 0:NPG * TS], bank[4][:, 0:NPG * TS])
                v.tensor_copy(PT[0:TS, NPG * TS:(NPG + 1) * TS],
                              bank[4][0:TS, NPG * TS:(NPG + 1) * TS]).then_inc(S["pt_ready"], 1)
                v.wait_ge(S["av_full"], b + 1)
                v.tensor_scalar(osb, bank[3][0:TS, 0:CKV], rs, None, ALU.mult).then_inc(S["os_ready"], 1)
            turned(NB - 1)
            for h in range(H):
                o = in_d()
                free_d(v.tensor_copy(xn[:, h, :], o[:, 0:T]))

            def split(it, h):
                v.wait_ge(S["hi_ready"], it * IH + h + 1)
                low(wpart[:, stage(h), 1, :], mring[:, place(h % IH), :], wpart[:, stage(h), 0, :]).then_inc(S["lo_ready"], 1)

            for m in range(DC):
                add_residual(m)
                if 4 <= m < 4 + STAGES:
                    split(0, m - 4)
            normalise(5, DC, xT, "g_ffn_m", xn, "xn_ready")

            for dst in (xtk, acc):
                for t0, tn, tt in TOK:
                    for half in range(2):
                        o = in_d()
                        free_d(v.tensor_copy(dst[0:tn, tt, half * CW:(half + 1) * CW], o[0:tn, :]))
            v.wait_ge(S["lg_full"], 1)
            v.wait_ge(S["ld_gf"], 32)
            link(v.memset(rt[:, 0:408], 0.0))
            link(v.tensor_copy(lg[:, 0:2, :], bank[4][:, 0:2 * E].rearrange("p (a b) -> p a b", a=2)))
            link(v.tensor_copy(lg[0:TS, 2, :], bank[4][0:TS, 2 * E:3 * E]))
            for tt in range(3):
                link(v.max(top[:, tt, :], lg[:, tt, :]))
                link(v.max_index(idu[:, tt, :], top[:, tt, :], lg[:, tt, :]))
            link(v.tensor_copy(idf, idu[:, :, :]))
            iota8 = mc("iota")[:, 0:E].unsqueeze(1).to_broadcast([P, 3, E])
            link(v.tensor_tensor(oh1, iota8, idf[:, :, 0:1].to_broadcast([P, 3, E]), ALU.is_equal))
            link(v.tensor_tensor(oh2, iota8, idf[:, :, 1:2].to_broadcast([P, 3, E]), ALU.is_equal))
            link(v.tensor_tensor(mk, oh1, oh2, ALU.add))
            v.tensor_tensor(mk, mk, mc("valid").unsqueeze(2).to_broadcast([P, 3, E]), ALU.mult).then_inc(S["mask_ready"], 1)
            v.tensor_tensor(gk[:, :, 1:2], top[:, :, 1:2], top[:, :, 0:1], ALU.subtract).then_inc(S["mask_ready"], 1)
            v.wait_ge(S["gk_exp"], 1)
            link(v.tensor_scalar(gk[:, :, 0:1], gk[:, :, 1:2], 1.0, None, ALU.add))
            link(v.reciprocal(gk[:, :, 0:1], gk[:, :, 0:1]))
            link(v.tensor_tensor(gk[:, :, 1:2], gk[:, :, 1:2], gk[:, :, 0:1], ALU.mult))
            link(v.tensor_tensor(oh1, oh1, gk[:, :, 0:1].to_broadcast([P, 3, E]), ALU.mult))
            link(v.tensor_tensor(oh2, oh2, gk[:, :, 1:2].to_broadcast([P, 3, E]), ALU.mult))
            link(v.tensor_tensor(gt, oh1, oh2, ALU.add))
            v.wait_ge(S["rank_full"], 1)
            link(v.tensor_copy(pos, bank[4][:, 32:56].rearrange("p (a b) -> p a b", a=3)))
            link(v.tensor_copy(cnt, bank[4][:, 64:72]))
            link(v.tensor_tensor(pos, pos, mk, ALU.mult))
            link(v.tensor_scalar(pos, pos, -1.0, None, ALU.add))
            link(v.tensor_copy(posI[:, :, 0:E], pos))
            link(v.tensor_copy(gateI[:, :, 0:E], gt))

            def one_hots(item):
                for tt in range(3):
                    v.tensor_scalar(Pm[:, tt, :], mc("iota"), posI[:, tt, item], None, ALU.is_equal)
                    ins = v.tensor_scalar(Pg[:, tt, :], mc("iota"), posI[:, tt, item], gateI[:, tt, item],
                                          ALU.is_equal, ALU.mult)
                return ins

            one_hots(slice(0, 1)).then_inc(S["p_made"], 1)
            two = lambda a: a.unsqueeze(2).to_broadcast([P, E, 2])
            link(v.tensor_tensor(fl.rearrange("p (e k) -> p e k", k=2), two(cnt),
                                 mc("kbase").rearrange("p (e k) -> p e k", k=2), ALU.is_gt))
            link(v.tensor_tensor_scan(cum, fl, mc("kbase"), 0.0, ALU.add, ALU.min))
            link(v.memset(nf, 0.0))
            link(v.tensor_scalar(nf[:, 0:1], cum[:, 2 * E - 1:2 * E], float(E), None, ALU.add))
            link(v.tensor_tensor(cum, cum, fl, ALU.subtract))
            for j in range(EXTRA):
                link(v.scalar_tensor_tensor(out=sel, in0=cum, scalar=float(j), in1=fl, op0=ALU.is_equal, op1=ALU.mult))
                link(v.tensor_tensor(s16, sel, mc("eidx"), ALU.mult))
                link(v.reduce_sum(nf[:, 1 + j:2 + j], s16, AX.X))
                link(v.tensor_tensor(s16, sel, mc("kbase"), ALU.mult))
                link(v.reduce_sum(nf[:, 6:7], s16, AX.X))
                for src, dst in ((pos, posI), (gt, gateI)):
                    link(v.tensor_tensor(p48.rearrange("p a (e k) -> p a e k", k=2),
                                         src.unsqueeze(3).to_broadcast([P, 3, E, 2]),
                                         sel.rearrange("p (e k) -> p e k", k=2).unsqueeze(1).to_broadcast([P, 3, E, 2]), ALU.mult))
                    link(v.reduce_sum(dst[:, :, E + j:E + j + 1], p48, AX.X))
                link(v.tensor_scalar(posI[:, :, E + j], posI[:, :, E + j], nf[:, 6:7], None, ALU.subtract))
            v.tensor_copy(ints[0:1, 0:2 + EXTRA], nf[0:1, 0:2 + EXTRA]).then_inc(S["tables_ready"], 1)

            v.wait_ge(S["tables_ready"], 1)
            n_items = v.value_load(ints[0:1, 0:1], min_val=E, max_val=ITEMS)

            def take_tokens(half, count):
                v.wait_ge(S["xg_hi"], count)
                cut = slice(half * CW, (half + 1) * CW)
                low(xgp[:, 1, cut], bank[6 + half][:, :], xgp[:, 0, cut]).then_inc(S[("misc_free", "xg_ready")[half]], 1)

            take_tokens(0, 1)
            take_tokens(1, 2)
            v.memset(cols[0:1, 12:13], 0.0).then_inc(S["gu_done"], 1)
            v.memset(cols[0:1, 15:16], 0.0).then_inc(S["used"], STAGES)
            v.memset(cols[0:1, 13:14], 0.0).then_inc(S["y_free"], 1)

            def accumulate(it, tile):
                t0, tn, tt = TOK[tile]
                for half in range(2):
                    n = 2 * tile + half
                    v.wait_ge(S["misc_full"], it * SHARED + 2 + n + 1)
                    sums = acc[0:tn, tt, half * CW:(half + 1) * CW]
                    v.tensor_tensor(sums, sums, bank[6 + n % 2][0:tn, :], ALU.add).then_inc(S["misc_free"], 1)

            with v.Fori(0, n_items) as it:
                for h in range(STAGES, IH + STAGES):
                    split(it, h)
                    for j in range(CE):
                        first = 2 * ORDER.index(("up", j))
                        if h == first + 3:
                            v.wait_ge(S["silu_done"], it * CE + j + 1)
                            v.wait_ge(S["used"], it * IH + after("up", j))
                            v.tensor_tensor(hh[j % 2], sl[j % 2], bank[2 + j % 2][:, :], ALU.mult).then_inc(S["gu_done"], 1)
                        if h == min(turn_at(j) + 3, IH - 1):
                            v.wait_ge(S["hh_hi"], it * CE + j + 1)
                            low(hhp[:, j % 2, 1, :], bank[6 + (1 + j) % 2][:, :], hhp[:, j % 2, 0, :]).then_inc(S["misc_free"], 1)
                    if h < STAGES + 3:
                        accumulate(it, h - STAGES)
                    if h == 6:
                        v.wait_ge(S["pg_hi"], it + 1)
                        low(ptp[:, 1, :], bank[6][:, 0:T], ptp[:, 0, :]).then_inc(S["misc_free"], 1)
                        one_hots(bass.ds(it + 1, 1)).then_inc(S["p_made"], 1)
                    if h == IH:
                        take_tokens(0, it * 2 + 3)
                    if h == IH + 1:
                        v.wait_ge(S["y_hi"], it + 1)
                        low(yp[:, 1, 0:CW], bank[4][:, :], yp[:, 0, 0:CW])
                        low(yp[:, 1, CW:D], bank[5][:, :], yp[:, 0, CW:D]).then_inc(S["y_free"], 1)
                        take_tokens(1, it * 2 + 4)
            for tile in range(3):
                accumulate(n_items, tile)

            v.memset(cols[0:1, 14:15], 0.0).then_inc(S["acc_done"], 1)
            for t0, tn, tt in TOK:
                v.wait_ge(S["fin_ss"], tt + 1)
                s = cols[0:tn, 8 + tt:9 + tt]
                link(v.reciprocal(s, s))
                v.scalar_tensor_tensor(out=acc[0:tn, tt, :], in0=acc[0:tn, tt, :], scalar=s, in1=gfin[0:tn, :],
                                       op0=ALU.mult, op1=ALU.mult).then_inc(S["fin_ready"], 1)

        @block.scalar
        def _(a):
            b_gate = i["b_gate_a"][0].rearrange("(g h) -> h g", g=2)
            a.dma_start(tiny[:, 0:2], b_gate).then_inc(S["ld_tiny"], 16)
            a.dma_start(tiny[:, 8:16], i["state_m"][0].rearrange("b h -> h b")).then_inc(S["ld_tiny"], 16)
            a.dma_start(wg[:, :, :], rows_of(w_in, 2 * hq + 2 * hv, 2 * H)).then_inc(S["ld_wg"], 16)
            a.dma_start(ac[:, :], i["aconst"]).then_inc(S["ld_ac"], 16)
            n_ga, n_link = [0], [0]

            def link(ins):
                n_link[0] += 1
                ins.then_inc(S["achain"], 1)
                a.wait_ge(S["achain"], n_link[0])

            def in_a():
                n_ga[0] += 1
                a.wait_ge(S["ga_full"], n_ga[0])
                return bank[(n_ga[0] - 1) % 2]

            def high(dst, src):
                return a.activation(dst, src, ACT.Copy)

            def squares(chunks_, src, dst, sem_, first, m0=0):
                for m in range(m0, m0 + chunks_):
                    a.wait_ge(S[sem_], first + m + 1)
                    a.activation(dst[:, m, :], src[:, m, :], ACT.Square).then_inc(S["sq_ready"], 1)

            def root(k, width):
                a.wait_ge(S["ss_full"], k + 1)
                a.activation(stdv(k), bank[7][:, 0:T], ACT.Sqrt, bias=c("eps"), scale=1.0 / width).then_inc(S["std_ready"], 1)

            a.wait_ge(S["ld_const"], 16)
            squares(DC, xT, xn, "x_ready", 0)
            root(0, D)
            a.wait_ge(S["gates_full"], 1)
            a.wait_ge(S["bg_ready"], 1)
            a.activation(rU, bank[4][0:H, 0:T], ACT.Tanh, bias=tiny[:, 2:3], scale=1.0 / CAP)
            link(a.activation(rE, bank[5][0:H, 0:T], ACT.Tanh, bias=tiny[:, 3:4], scale=1.0 / CAP))
            link(a.activation(rE, rE, ACT.Exp, scale=-CAP))
            a.activation(rE, rE, ACT.Ln, bias=c("one", H), scale=1.0).then_inc(S["lf_ready"], 1)
            for m in range(HP):
                o = in_a()
                a.activation(qT[:, m, :], o[:, 0:T], ACT.Copy, scale=DK ** -0.5).then_inc(S["ga_free"], 1)
            for m in range(DC):
                o = in_a()
                a.activation(oT[:, m, :], o[:, 0:T], ACT.Sigmoid).then_inc(S["ga_free"], 1)
            a.wait_ge(S["uT_full"], 1)
            a.activation(eI.rearrange("p a b -> p (a b)"), bank[5][:, 0:HP * TS], ACT.Exp)
            a.activation(eC, bank[5][:, HP * TS:HP * TS + HP * NB], ACT.Exp)
            a.wait_ge(S["uT_ready"], 2)
            a.activation(uT[:, :, H:2 * H], uT[:, :, H:2 * H], ACT.Exp).then_inc(S["e_ready"], 1)
            for h in range(H):
                a.wait_ge(S["D_made"], h + 1)
                a.activation(Dh[h % 2], Dh[h % 2], ACT.Exp).then_inc(S["exp_done"], 1)
                a.wait_ge(S["m_full"], h + 1)
                a.activation(bank[4][:, 0:T], bank[4][:, 0:T], ACT.Exp).then_inc(S["em_done"], 1)
            a.wait_ge(S["h_made"], H)

            def head_square(h):
                if h >= 2:
                    a.wait_ge(S["hss_full"], h - 1)
                a.activation(Dh[h % 2][:, 0:T], xn[:, h, :], ACT.Square).then_inc(S["hsq_ready"], 1)

            head_square(0)
            for h in range(H):
                if h + 1 < H:
                    head_square(h + 1)
                a.wait_ge(S["hss_full"], h + 1)
                b4 = bank[4 + h % 2][:, 0:T]
                a.activation(b4, b4, ACT.Sqrt, bias=c("eps"), scale=1.0 / DV).then_inc(S["hstd_ready"], 1)
            def f_split(h):
                name, a0, w = FHALF[h]
                a.wait_ge(w_full[slot_of[CH[name]]], arrive[CH[name]])
                if h < STAGES:
                    a.wait_ge(*release[CH[("v0", "v1", "out0")[h]]])
                else:
                    a.wait_ge(*f_consumed(h - STAGES))
                dst = fview(wpart[:, h % STAGES, 0, :], h)
                if h < FGU:
                    ins = high(dst, wview(name, DC, FCH[int(name[2:])][1])[:, :, a0:a0 + w])
                else:
                    src = wview(name, FT, P)[:, a0:a0 + w, :]
                    if a0:
                        high(dst[:, 0:w - 1, :], src[:, 0:w - 1, :])
                        ins = high(dst[0:FLAST, w - 1, :], src[0:FLAST, w - 1, :])
                    else:
                        ins = high(dst, src)
                ins.then_inc(S["f_hi"], 1)

            f_split(0)
            f_split(1)
            squares(5, xT, xn, "gd_free", GD_FFN - DC)
            f_split(2)
            squares(DC - 5, xT, xn, "gd_free", GD_FFN - DC, 5)
            root(1, D)
            for m in range(DC):
                a.wait_ge(S["xn_ready"], DC + m + 1)
                if m == 0:
                    a.wait_ge(S["stored"], 16 * STORES_A)
                high(xp[:, 0, m, :], xn[:, m, :]).then_inc(S["xp_hi"], 1)
            for h in range(len(FHALF)):
                if h >= STAGES:
                    f_split(h)
                if h % 2 == 0 and 2 <= h < FGU + 1:
                    for f in (h - 2, h - 1):
                        rows = P if f < FT - 1 else FLAST
                        o = in_a()
                        if f >= 3:
                            a.wait_ge(S["hp_lo"], f - 2)
                        a.activation(sg[f % 3][0:rows, :], o[0:rows, 0:T], ACT.Silu).then_inc(S["ga_free"], 1)
                if h % 2 and 3 <= h < FGU + 2:
                    for f in (h - 3, h - 2):
                        rows = P if f < FT - 1 else FLAST
                        a.wait_ge(S["gd_free"], GD_FFN + f + 1)
                        high(hp[0:rows, 0, f, :], sg[f % 3][0:rows, :]).then_inc(S["hp_hi"], 1)
                if h % 2 == 0 and h >= FGU + 4:
                    squares(1, xT, xn, "gd_free", GD_CKV - DC, (h - FGU - 4) // 2)
            squares(2, xT, xn, "gd_free", GD_CKV - DC, DC - 2)
            root(2, D)
            squares(CT, raw, ckvT, "gd_free", GD_CKV)
            root(3, CKV)
            squares(QT, raw, cq, "gd_free", GD_CQ)
            root(4, QL)
            a.wait_ge(S["kr_ready"], 1)
            a.wait_ge(S["cq_ready"], 1)
            for h in range(H):
                if h >= 2:
                    a.wait_ge(S["qr_ready"], h - 1)
                    a.wait_ge(S["gd_full"], GD_QL + CT * (h - 1))
                o = in_a()
                a.activation(qn[h % 2], o[:, 0:T], ACT.Copy).then_inc(S["ga_free"], 1)
                o = in_a()
                a.activation(rtmp[h % 2], o[0:ROPE, 0:T], ACT.Copy).then_inc(S["ga_free"], 1)

            def col(k, n, rows=P):
                return cols[0:rows, 4 * k + n % 2:4 * k + n % 2 + 1]

            units = [(h, q) for h in range(H) for q in range(2)]
            for u, (h, q) in enumerate(units):
                keys = (q + 1) * P
                a.wait_ge(S["max_ready"], u + 1)
                a.activation(prob2[u % 2][:, 0:keys], bank[5 + u % 2][:, 0:keys], ACT.Exp, bias=col(1, u), scale=SCALE,
                             accum_out=col(2, u)).then_inc(S["p_exp"], 1)

            def cache_evac(b):
                for g in (0, 2, 4):
                    a.wait_ge(S["tp_full"], 6 * b + g + 1)
                    part, half = g // 2, g % 2
                    if part < CT:
                        ins = a.activation(cacheT[:, part, half * 512:(half + 1) * 512], bank[0][:, :], ACT.Copy)
                    else:
                        ins = a.activation(cacheR[:, half * 512:(half + 1) * 512], bank[0][0:ROPE, :], ACT.Copy)
                    ins.then_inc(S["tpa_free"], 1)

            cache_evac(0)
            for b in range(NB):
                a.wait_ge(S["max_ready"], len(units) + b + 1)
                a.activation(prob[0:TS, :], wide[0:TS, 0:PAST + TS], ACT.Exp, bias=col(1, b, TS), scale=SCALE,
                             accum_out=col(2, b, TS)).then_inc(S["p_exp"], 1)
                if b + 1 < NB:
                    cache_evac(b + 1)
            squares(4, xT, acc_sq, "gd_free", GD_MOE - DC)
            for name in ("uq1", "uv", "wo0"):
                a.wait_ge(*release[CH[name]])
            for h in range(STAGES):
                a.wait_ge(*loaded(0, h))
                high(wpart[:, stage(h), 0, :], mring[:, place(h), :]).then_inc(S["hi_ready"], 1)
            for part in range(2):
                a.activation(yp[:, part, :], ones[:, 0:1].to_broadcast([P, D]), ACT.Copy, scale=0.0)
                a.activation(ptp[:, part, :], ones[:, 0:1].to_broadcast([P, T]), ACT.Copy, scale=0.0)
            squares(4, xT, acc_sq, "gd_free", GD_MOE - DC, 4)
            root(5, D)
            a.wait_ge(S["mask_ready"], 2)
            a.activation(gk[:, :, 1:2], gk[:, :, 1:2], ACT.Exp).then_inc(S["gk_exp"], 1)

            def take_tokens(half, full, count):
                a.wait_ge(S["misc_full"], full)
                a.activation(xgp[:, 0, half * CW:(half + 1) * CW], bank[6 + half][:, :], ACT.Copy).then_inc(S["xg_hi"], 1)

            def split(it, h):
                a.wait_ge(*loaded(it, h))
                a.wait_ge(S["used"], it * IH + h + 1)
                a.activation(wpart[:, stage(h), 0, :], mring[:, place(h % IH), :], ACT.Copy).then_inc(S["hi_ready"], 1)

            a.wait_ge(S["kv_stored"], 64)
            take_tokens(0, 1, 1)
            take_tokens(1, 2, 2)
            a.wait_ge(S["tables_ready"], 1)
            n_items = a.value_load(ints[0:1, 0:1], min_val=E, max_val=ITEMS)
            with a.Fori(0, n_items) as it:
                for h in range(STAGES, IH + STAGES):
                    split(it, h)
                    for j in range(CE):
                        first = 2 * ORDER.index(("gate", j))
                        if h == first + 3:
                            a.wait_ge(S["used"], it * IH + after("gate", j))
                            a.wait_ge(S["gu_done"], it * CE + 1 + max(0, j - 1))
                            a.activation(sl[j % 2], bank[j % 2][:, :], ACT.Silu).then_inc(S["silu_done"], 1)
                        if h == min(turn_at(j) + 3, IH - 1):
                            a.wait_ge(S["misc_full"], it * SHARED + 2 + 7 + j + 1)
                            a.activation(hhp[:, j % 2, 0, :], bank[6 + (1 + j) % 2][:, :], ACT.Copy).then_inc(S["hh_hi"], 1)
                    if h == 6:
                        a.wait_ge(S["misc_full"], it * SHARED + 2 + 7)
                        high(ptp[:, 0, :], bank[6][:, 0:T]).then_inc(S["pg_hi"], 1)
                    if h == IH:
                        take_tokens(0, it * SHARED + 2 + SHARED - 1, it * 2 + 3)
                    if h == IH + 1:
                        a.wait_ge(S["used"], it * IH + after("down", CE - 1))
                        high(yp[:, 0, 0:CW], bank[4][:, :])
                        high(yp[:, 0, CW:D], bank[5][:, :]).then_inc(S["y_hi"], 1)
                        take_tokens(1, it * SHARED + 2 + SHARED, it * 2 + 4)
            a.wait_ge(S["acc_done"], 1)
            for t0, tn, tt in TOK:
                s = cols[0:tn, 8 + tt:9 + tt]
                link(a.activation(xtk[0:tn, tt, :], acc[0:tn, tt, :], ACT.Square, accum_out=s))
                a.activation(s, s, ACT.Sqrt, bias=c("eps", tn), scale=1.0 / D).then_inc(S["fin_ss"], 1)

        @block.gpsimd
        def _(g):
            g.dma_start(pages[:, :], i["page_table"].rearrange("(o b) n -> o (b n)", o=1)).then_inc(S["ld_pages"], 16)
            st_C, st_n = i["state_C"][0], i["state_n"][0]
            for h in range(H):
                r, j = (h % 2) * DK, h // 2
                g.dma_start(Ce[r:r + DK, j, :, 0:DV], st_C[:, h].rearrange("b k v -> k b v")).then_inc(S["ld_state"], 16)
                g.dma_start(Ce[r:r + DK, j, :, DV], st_n[:, h].rearrange("b k -> k b")).then_inc(S["ld_state"], 16)
            g.wait_ge(S["gates_full"], 1)
            g.dma_start(wg[:, :, 0:E], rows_of(i["w_router"][0], 0, E)).then_inc(S["ld_wr"], 16)
            g.wait_ge(S["st_free"], HP)
            g.dma_start(out[2][0, 0].rearrange("h k v -> k h v"), Cp[:, :, 0:DV]).then_inc(S["stored"], 16)
            g.dma_start(out[3][0, 0].rearrange("h k -> k h"), Cp[:, :, DV]).then_inc(S["stored"], 16)
            g.dma_start(out[4][0].rearrange("a h -> h a"), tiny[:, 16:17]).then_inc(S["stored"], 16)
            g.dma_start(out[9][0].rearrange("b h -> h b"), tiny[:, 17:17 + NB]).then_inc(S["stored"], 16)
            g.wait_ge(S["st_free"], HP + 2 * NB)
            for h in range(H):
                r, j = (h % 2) * DK, h // 2
                g.dma_start(out[7][0][:, h].rearrange("b k v -> k b v"), Ce[r:r + DK, j, :, 0:DV]).then_inc(S["stored"], 16)
                g.dma_start(out[8][0][:, h].rearrange("b k -> k b"), Ce[r:r + DK, j, :, DV]).then_inc(S["stored"], 16)

            def load_rotary(b):
                with g.Fori(0, NPG) as j:
                    page = g.value_load(pages[0:1, bass.ds(j + b * NPG, 1)], min_val=0, max_val=i["cache_krope"].shape[0] - 1)
                    g.dma_start(crk[b % BUFS][:, bass.ds(j, 1), :],
                                i["cache_krope"][bass.ds(page, 1), :, :].rearrange("g p c -> p g c")).then_inc(cr_full[b % BUFS], 16)

            g.wait_ge(S["stored"], 16 * STORES_A)
            g.wait_ge(S["gd_full"], GD_FFN + FT)
            g.wait_ge(S["hp_lo"], FT)
            g.wait_ge(S["ld_pages"], 16)
            load_rotary(0)
            load_rotary(1)
            g.wait_ge(S["gd_free"], GD_QL)
            for n, (dst_c, dst_r) in enumerate(((out[5][0], out[6][0]), (out[10], out[11]))):
                for dst, a0, a1 in ((dst_c, 0, CKV), (dst_r, CKV, CKV + ROPE)):
                    if n == 0:
                        g.dma_start(dst.rearrange("(t p) c -> p t c", p=P), ctok[:, 0:2, a0:a1]).then_inc(S["kv_stored"], 16)
                    else:
                        g.dma_start(dst.rearrange("b s c -> (b s) c"), ctok[0:TS, 2, a0:a1]).then_inc(S["kv_stored"], 16)
            for b in range(2, NB):
                if b == 2:
                    g.wait_ge(*release[CH["uq1"]])
                else:
                    g.wait_ge(S["av_full"], b - BUFS + 1)
                load_rotary(b)
            NU = 2 * H
            g.wait_ge(S["ol_full"], NU + NB)
            g.dma_start(gfin, i["g_final"].rearrange("(a n) -> a n", a=1).to_broadcast([P, D])).then_inc(S["ld_gf"], 16)
            g.dma_start(arena[:, MAT:MAT + MCOLS], i["mconst"]).then_inc(S["ld_gf"], 16)
            g.wait_ge(S["kv_stored"], 64)

        @block.sync
        def _(sp):
            sp.dma_start(xtok[:, 0, :], i["x_prompt"][0, 0:P, :]).then_inc(S["ld_x"], 16)
            sp.dma_start(xtok[:, 1, :], i["x_prompt"][0, P:TP, :]).then_inc(S["ld_x"], 16)
            sp.dma_start(xtok[0:TS, 2, :], i["x_sample"].rearrange("b s d -> (b s) d")).then_inc(S["ld_x"], 16)
            sp.dma_start(cs[:, :], i["const"]).then_inc(S["ld_const"], 16)
            for name, rows in GAINS:
                src = i[name][0] if len(i[name].shape) > 1 else i[name]
                if len(src.shape) == 1:
                    src = src.rearrange("(r n) -> r n", n=P)
                sp.dma_start(Dh[0][G0[name]:G0[name] + rows, 0:P], src).then_inc(S["ld_gain"], 16)

            def load_cache(b):
                with sp.Fori(0, NPG) as j:
                    page = sp.value_load(pages[0:1, bass.ds(j + b * NPG, 1)], min_val=0, max_val=i["cache_ckv"].shape[0] - 1)
                    sp.dma_start(ctk[b % BUFS][:, bass.ds(j, 1), :],
                                 i["cache_ckv"][bass.ds(page, 1), :, :].rearrange("g p c -> p g c")).then_inc(ck_full[b % BUFS], 16)

            for n, (name, parts) in enumerate(chunks):
                if name == "dd4":
                    sp.wait_ge(S["gd_full"], GD_FFN + FT)
                    sp.wait_ge(S["hp_lo"], FT)
                    sp.wait_ge(S["stored"], 16 * STORES_A)
                    sp.wait_ge(S["ld_pages"], 16)
                    load_cache(0)
                    load_cache(1)
                if slot_of[n] >= 4 and n >= SLOTS:
                    sp.wait_ge(S["gd_full"], GD_CKV)
                elif n >= SLOTS:
                    sp.wait_ge(*release[behind[n]])
                for k, w, at, rows, src in parts:
                    dst = ring[0:rows, slot_of[n], at:at + k * w].rearrange("p (c n) -> p c n", c=k)
                    sp.dma_start(dst, src).then_inc(w_full[slot_of[n]], 16)

            def expert_half(e, h):
                kind, j = ORDER[h // 2]
                w, a, half = i[f"w_{kind}_m"][0], HALFW // CW if kind != "down" else KD // 2, h % 2
                if kind != "down":
                    src = w[bass.ds(e, 1), half * D // 2:(half + 1) * D // 2, j * CW:(j + 1) * CW]
                else:
                    src = w[bass.ds(e, 1), j * CW + half * CW // 2:j * CW + (half + 1) * CW // 2, :]
                sp.dma_start(mring[:, place(h), :].rearrange("p (c n) -> p c n", c=a),
                             src.rearrange("e (c p) n -> p (e c) n", p=P)).then_inc(half_full[place(h)], 16)

            def item_rest(it, e):
                h0 = 2 * ORDER.index(("down", 0))
                for h in range(HALVES, IH):
                    if h != h0:
                        sp.wait_ge(S["lo_ready"], it * IH + h - HALVES + 1)
                        expert_half(e, h)
                    if h == h0 + 1:
                        expert_half(e, h0)

            def item_first(it, e, halves=range(HALVES)):
                for h in halves:
                    sp.wait_ge(S["lo_ready"], it * IH + IH + h - HALVES + 1)
                    expert_half(e, h)

            under = [CH[name] for name in ("dkv", "dkv", "dq", "dq", "uk", "wo1", "wo1")]
            for h in range(HALVES):
                if h == 5:
                    for b in range(2, NB):
                        if b == 2:
                            sp.wait_ge(*release[CH["uq1"]])
                        else:
                            sp.wait_ge(S["av_full"], b - BUFS + 1)
                        load_cache(b)
                sp.wait_ge(*release[under[h]])
                expert_half(0, h)
            with sp.Fori(0, E - 1) as it:
                item_rest(it, it)
                item_first(it, it + 1)
            item_rest(E - 1, E - 1)
            def expert(number):
                return sp.value_load(ints[0:1, number], min_val=0, max_val=E - 1)

            sp.wait_ge(S["tables_ready"], 1)
            n_items = sp.value_load(ints[0:1, 0:1], min_val=E, max_val=ITEMS)
            item_first(E - 1, expert(slice(1, 2)), range(STAGES))
            with sp.If(n_items > E):
                with sp.Fori(E, n_items) as it:
                    e, following = expert(bass.ds(it - (E - 1), 1)), expert(bass.ds(it - (E - 2), 1))
                    item_first(it - 1, e, range(STAGES, HALVES))
                    item_rest(it, e)
                    item_first(it, following, range(STAGES))
            for t0, tn, tt in TOK:
                sp.wait_ge(S["fin_ready"], tt + 1)
                dst = out[0][0, t0:t0 + tn, :] if tt < 2 else out[1].rearrange("b s d -> (b s) d")
                sp.dma_start(dst, acc[0:tn, tt, :]).then_inc(S["outs"], 16)
            sp.wait_ge(S["outs"], 48)
            sp.wait_ge(S["stored"], 16 * STORES_A)


GA_FFN = HP + DC
GD_FFN = HP + 6 + 3 + DC
GD_CKV = GD_FFN + FT + DC
GD_CQ = GD_CKV + CT + 1
GD_QL = GD_CQ + QT + HP + 3
GD_MOE = GD_QL + CT * H + H + DC
STORES_A = 4 + 2 * H


def shape_constants():
    import numpy as np

    f = np.float32
    r = np.arange(P)
    t = np.arange(TS)
    parts = {
        "ident": np.eye(P), "ones": np.ones((P, P)), "rot": np.zeros((P, ROPE)), "bsel": np.zeros((P, NB)),
        "eps": np.full((P, 1), EPS), "one": np.ones((P, 1)),
        "pmask": np.where(r[None, :] <= r[:, None], 0.0, NEG),
    }
    x = np.arange((2 * NB - 1) * NS)
    parts["smask"] = np.where((x[None, :] // NS == NB - 1) & (x[None, :] % NS <= r[:, None] % NS), 0.0, NEG)
    half = ROPE // 2
    parts["rot"][half + np.arange(half), np.arange(half)] = -1.0
    parts["rot"][np.arange(half), half + np.arange(half)] = 1.0
    parts["bsel"][t, t // NS] = 1.0
    pos = np.concatenate([np.arange(TP), PAST + t % NS]).astype(f)
    inv = (f(10000.0) ** (-np.arange(half, dtype=f) / f(half))).astype(f)
    ang = (pos[:, None] * inv[None, :]).astype(f)
    for name, fn in (("cos", np.cos), ("sin", np.sin)):
        tab = fn(ang).astype(f).T
        parts[name] = np.concatenate([tab, tab, np.zeros((P - ROPE, T))])
    const = np.concatenate([parts[n] for n, _ in CONSTS], axis=1).astype(f)
    m = {
        "tri": np.where(r[:, None] <= r[None, :], 1.0, 0.0), "iota": np.tile(r, (P, 1)),
        "eidx": np.tile(np.arange(2 * E) // 2, (P, 1)), "kbase": np.tile(P * (1 + np.arange(2 * E) % 2), (P, 1)),
        "valid": np.stack([np.ones(P), np.ones(P), r < TS], axis=1),
    }
    mconst = np.concatenate([m[n] for n, _ in MCONSTS], axis=1).astype(f)
    tri = np.where(r[:, None] <= r[None, :], 0.0, NEG)
    own = np.full((P, TS), NEG)
    own[:TS] = np.where((t[:, None] // NS == t[None, :] // NS) & (t[:, None] <= t[None, :]), 0.0, NEG)
    selp = np.zeros((P, HP, P))
    for j in range(HP):
        selp[2 * j, j, :DK] = 1.0
        selp[2 * j + 1, j, DK:] = 1.0
    aconst = np.concatenate([tri, np.zeros((P, P)), tri, own, selp.reshape(P, -1)], axis=1).astype(f)
    return {"const": const, "mconst": mconst, "aconst": aconst}


_INS = """x_prompt x_sample state_C state_n state_m cache_ckv cache_krope page_table g_norm_a w_in_a b_gate_a g_head_a
    w_out_a g_kv w_dkv g_ckv w_uk w_uv g_norm_b w_dq g_q w_uq w_o_b g_ffn_d w_gate_d w_up_d w_down_d g_ffn_m w_router
    w_gate_m w_up_m w_down_m g_final""".split()
_OUTS = [(1, TP, D), (NB, NS, D), (1, 1, H, DK, DV), (1, 1, H, DK), (1, 1, H), (1, TP, CKV), (1, TP, ROPE),
         (1, NB, H, DK, DV), (1, NB, H, DK), (1, NB, H), (NB, NS, CKV), (NB, NS, ROPE)]


def kernel(**inputs):
    import numpy as np
    import concourse.bacc as bacc
    from concourse.bass_utils import run_bass_kernel_spmd

    nc = bacc.Bacc("TRN2", target_bir_lowering=False, num_devices=1)
    arrays, handles = {}, {}
    named = {**{n: inputs[n] for n in _INS}, **shape_constants()}
    for name, value in named.items():
        array = np.ascontiguousarray(value)
        arrays[f"in_{name}"] = array
        handles[name] = nc.dram_tensor(f"in_{name}", array.shape, mybir.dt.from_np(array.dtype), kind="ExternalInput").ap()
    outs = [nc.dram_tensor(f"out_{n}", shape, F32, kind="ExternalOutput").ap() for n, shape in enumerate(_OUTS)]
    build(nc, handles, outs)
    r = run_bass_kernel_spmd(nc, [arrays], core_ids=[0])
    return tuple(r.results[0][f"out_{n}"] for n in range(len(_OUTS)))
```
